# Optimizing a Trainium2 kernel written in Bass

```python
import jax, jax.numpy as jnp
from jax import lax
import numpy as np

D_MODEL = 2048
BATCH = 1
SEQ = 256
DEPTH = 1
DEC_BATCH = 8
DEC_SEQ = 4
PAST_LEN = 2048
PAGE_SIZE = 128

SSM_EXPAND = 2
D_INNER = SSM_EXPAND * D_MODEL
HEAD_DIM = 64
SSM_HEADS = D_INNER // HEAD_DIM
N_GROUPS = 8
HEADS_PER_GROUP = SSM_HEADS // N_GROUPS
D_STATE = 128
CONV_WIDTH = 4
CONV_DIM = D_INNER + 2 * N_GROUPS * D_STATE
CHUNK = 128
S5_WIDTH = D_MODEL
S5_GROUP = 16
S5_GROUPS = S5_WIDTH // S5_GROUP
S5_STATE = 64
D_FF = ((8 * D_MODEL // 3 + 255) // 256) * 256
EPS = 1e-6
OFF_XBC = D_INNER
OFF_DT = OFF_XBC + CONV_DIM
OFF_U = OFF_DT + SSM_HEADS
OFF_GA = OFF_U + S5_WIDTH
OFF_GB = OFF_GA + D_MODEL
IN_DIM = OFF_GB + D_MODEL

kernel_name = 'hybrid_ssd_s5_gated_decoder_step'

def rms_norm(x, g):
    xf = x.astype(jnp.float32)
    y = xf * lax.rsqrt(jnp.mean(xf * xf, axis=-1, keepdims=True) + EPS)
    return (y * g.astype(jnp.float32)).astype(x.dtype)

def causal_conv(xbc, buf, w, b):
    L = xbc.shape[1]
    xfull = jnp.concatenate([buf.astype(xbc.dtype), xbc], axis=1)
    out = b
    for k in range(CONV_WIDTH):
        out = out + xfull[:, k:k + L] * w[k]
    return out, xfull[:, L:]

def ssd_chunked(x, dt, a, bm, cm, h0):
    bsz, L = x.shape[:2]
    q = min(CHUNK, L)
    nc = -(-L // q)
    pad = nc * q - L
    if pad:
        def padt(t):
            return jnp.pad(t, [(0, 0), (0, pad)] + [(0, 0)] * (t.ndim - 2))
        x, dt, bm, cm = padt(x), padt(dt), padt(bm), padt(cm)
    x = x.reshape(bsz, nc, q, N_GROUPS, HEADS_PER_GROUP, HEAD_DIM)
    dt = dt.reshape(bsz, nc, q, N_GROUPS, HEADS_PER_GROUP)
    bm = bm.reshape(bsz, nc, q, N_GROUPS, D_STATE)
    cm = cm.reshape(bsz, nc, q, N_GROUPS, D_STATE)
    acs = jnp.cumsum(dt * a.reshape(N_GROUPS, HEADS_PER_GROUP), axis=2)
    causal = jnp.tril(jnp.ones((q, q), bool))[:, :, None, None]
    seg = jnp.exp(jnp.where(causal, acs[:, :, :, None] - acs[:, :, None, :], -jnp.inf))
    xdt = x * dt[..., None]
    cb = jnp.einsum('bcqgn,bcsgn->bcqsg', cm, bm)
    y_diag = jnp.einsum('bcqsgj,bcsgjp->bcqgjp', cb[..., None] * seg, xdt)
    decay = jnp.exp(acs[:, :, -1:] - acs)
    states = jnp.einsum('bcsgn,bcsgjp->bcgjpn', bm, xdt * decay[..., None])
    chunk_decay = jnp.exp(acs[:, :, -1])

    def step(h, inp):
        s_c, d_c = inp
        return d_c[..., None, None] * h + s_c, h

    h_init = h0.reshape(bsz, N_GROUPS, HEADS_PER_GROUP, HEAD_DIM, D_STATE)
    h_final, h_prev = lax.scan(step, h_init, (jnp.moveaxis(states, 1, 0), jnp.moveaxis(chunk_decay, 1, 0)))
    h_prev = jnp.moveaxis(h_prev, 0, 1)
    y_off = jnp.einsum('bcqgn,bcgjpn->bcqgjp', cm, h_prev) * jnp.exp(acs)[..., None]
    y = (y_diag + y_off).reshape(bsz, nc * q, SSM_HEADS, HEAD_DIM)[:, :L]
    return y, h_final.reshape(bsz, SSM_HEADS, HEAD_DIM, D_STATE)

def s5_combine(e1, e2):
    ar1, ai1, br1, bi1 = e1
    ar2, ai2, br2, bi2 = e2
    ar = ar1 * ar2 - ai1 * ai2
    ai = ar1 * ai2 + ai1 * ar2
    br = ar2 * br1 - ai2 * bi1 + br2
    bi = ar2 * bi1 + ai2 * br1 + bi2
    return (ar, ai, br, bi)

def s5_branch(u, s_re0, s_im0, lam_re, lam_im, log_dt, b_re, b_im, c_re, c_im, d_skip, w_glu):
    f32 = jnp.float32
    bsz, L, _ = u.shape
    ug = u.astype(f32).reshape(bsz, L, S5_GROUPS, S5_GROUP)
    lr, li = lam_re.astype(f32), lam_im.astype(f32)
    step = jnp.exp(log_dt.astype(f32))[:, None]
    mag = jnp.exp(lr * step)
    ar, ai = mag * jnp.cos(li * step), mag * jnp.sin(li * step)
    den = lr * lr + li * li
    qr = ((ar - 1.0) * lr + ai * li) / den
    qi = (ai * lr - (ar - 1.0) * li) / den
    br, bi = b_re.astype(f32), b_im.astype(f32)
    bbar_re = qr[..., None] * br - qi[..., None] * bi
    bbar_im = qr[..., None] * bi + qi[..., None] * br
    bu_re = jnp.einsum('blgc,gnc->blgn', ug, bbar_re)
    bu_im = jnp.einsum('blgc,gnc->blgn', ug, bbar_im)
    a_re = jnp.broadcast_to(ar, (1, L, S5_GROUPS, S5_STATE))
    a_im = jnp.broadcast_to(ai, (1, L, S5_GROUPS, S5_STATE))
    acum_re, acum_im, s_re, s_im = lax.associative_scan(s5_combine, (a_re, a_im, bu_re, bu_im), axis=1)
    s0r = s_re0.astype(f32)[:, None]
    s0i = s_im0.astype(f32)[:, None]
    s_re = s_re + acum_re * s0r - acum_im * s0i
    s_im = s_im + acum_re * s0i + acum_im * s0r
    y = (jnp.einsum('blgn,gcn->blgc', s_re, c_re.astype(f32))
         - jnp.einsum('blgn,gcn->blgc', s_im, c_im.astype(f32)))
    y = y.reshape(bsz, L, S5_WIDTH) + d_skip.astype(f32) * u.astype(f32)
    v = jax.nn.gelu(y).astype(u.dtype) @ w_glu
    v1, v2 = jnp.split(v, 2, axis=-1)
    return v1 * jax.nn.sigmoid(v2), s_re[:, -1], s_im[:, -1]

def mixer(h, conv0, ssm0, s5r0, s5i0, lp):
    f32 = jnp.float32
    bsz, L, _ = h.shape
    proj = h @ lp['w_in']
    z = proj[..., :OFF_XBC]
    xbc = proj[..., OFF_XBC:OFF_DT]
    dt_raw = proj[..., OFF_DT:OFF_U]
    u = proj[..., OFF_U:OFF_GA]
    g_a = proj[..., OFF_GA:OFF_GB]
    g_b = proj[..., OFF_GB:]
    xbc, conv_new = causal_conv(xbc, conv0, lp['conv_w'], lp['conv_b'])
    xbc = jax.nn.silu(xbc)
    xs = xbc[..., :D_INNER].reshape(bsz, L, SSM_HEADS, HEAD_DIM).astype(f32)
    bm = xbc[..., D_INNER:D_INNER + N_GROUPS * D_STATE].reshape(bsz, L, N_GROUPS, D_STATE).astype(f32)
    cm = xbc[..., D_INNER + N_GROUPS * D_STATE:].reshape(bsz, L, N_GROUPS, D_STATE).astype(f32)
    dt = jax.nn.softplus(dt_raw.astype(f32) + lp['dt_bias'].astype(f32))
    a = -jnp.exp(lp['a_log'].astype(f32))
    y, ssm_new = ssd_chunked(xs, dt, a, bm, cm, ssm0.astype(f32))
    y = y + xs * lp['d_ssm'].astype(f32)[:, None]
    y = y.reshape(bsz, L, D_INNER) * jax.nn.silu(z.astype(f32))
    y_a = rms_norm(y, lp['norm_ssm']).astype(h.dtype) @ lp['w_ssm_out']
    y_b, s5r, s5i = s5_branch(u, s5r0, s5i0, lp['s5_lambda_re'], lp['s5_lambda_im'], lp['s5_log_dt'],
                              lp['s5_b_re'], lp['s5_b_im'], lp['s5_c_re'], lp['s5_c_im'], lp['s5_d'], lp['w_glu'])
    merged = jax.nn.sigmoid(g_a) * y_a + jax.nn.sigmoid(g_b) * y_b.astype(h.dtype)
    return merged @ lp['w_out'], ssm_new, conv_new, s5r, s5i

def swiglu(h, w_up, w_down):
    g, v = jnp.split(h @ w_up, 2, axis=-1)
    return (jax.nn.silu(g) * v) @ w_down

def trunk(x, ssm, conv, s5r, s5i, layers):
    new_ssm, new_conv, new_s5r, new_s5i = [], [], [], []
    for l in range(DEPTH):
        lp = layers[l]
        m, st_ssm, st_conv, st_r, st_i = mixer(rms_norm(x, lp['norm_mix_pre']), conv[l], ssm[l], s5r[l], s5i[l], lp)
        x = x + rms_norm(m, lp['norm_mix_post'])
        f = swiglu(rms_norm(x, lp['norm_ffn_pre']), lp['w_ffn_up'], lp['w_ffn_down'])
        x = x + rms_norm(f, lp['norm_ffn_post'])
        new_ssm.append(st_ssm)
        new_conv.append(st_conv)
        new_s5r.append(st_r)
        new_s5i.append(st_i)
    return x, jnp.stack(new_ssm), jnp.stack(new_conv), jnp.stack(new_s5r), jnp.stack(new_s5i)

def setup_inputs(seed: int = 0) -> dict:
    key = jax.random.key(seed)
    ks = iter(list(jax.random.split(key, 40)))
    f32 = jnp.float32

    def nrm(shape, scale):
        return scale * jax.random.normal(next(ks), shape, f32)

    def unif(shape, lo, hi):
        return jax.random.uniform(next(ks), shape, f32, lo, hi)

    dt0 = jnp.exp(unif((DEPTH, SSM_HEADS), float(np.log(1e-3)), float(np.log(1e-1))))
    lam_im = jnp.pi * jnp.arange(S5_STATE, dtype=f32)
    return {
        'x_prompt': nrm((BATCH, SEQ, D_MODEL), 1.0),
        'x_sample': nrm((DEC_BATCH, DEC_SEQ, D_MODEL), 1.0),
        'state_ssm': nrm((DEPTH, DEC_BATCH, SSM_HEADS, HEAD_DIM, D_STATE), 0.3),
        'state_conv': nrm((DEPTH, DEC_BATCH, CONV_WIDTH - 1, CONV_DIM), 1.0),
        'state_s5_re': nrm((DEPTH, DEC_BATCH, S5_GROUPS, S5_STATE), 0.3),
        'state_s5_im': nrm((DEPTH, DEC_BATCH, S5_GROUPS, S5_STATE), 0.3),
        'norm_mix_pre': 1.0 + nrm((DEPTH, D_MODEL), 0.02),
        'norm_mix_post': 1.0 + nrm((DEPTH, D_MODEL), 0.02),
        'norm_ffn_pre': 1.0 + nrm((DEPTH, D_MODEL), 0.02),
        'norm_ffn_post': 1.0 + nrm((DEPTH, D_MODEL), 0.02),
        'w_in': nrm((DEPTH, D_MODEL, IN_DIM), D_MODEL ** -0.5),
        'conv_w': nrm((DEPTH, CONV_WIDTH, CONV_DIM), CONV_WIDTH ** -0.5),
        'conv_b': nrm((DEPTH, CONV_DIM), 0.01),
        'dt_bias': dt0 + jnp.log(-jnp.expm1(-dt0)),
        'a_log': jnp.log(unif((DEPTH, SSM_HEADS), 1.0, 16.0)),
        'd_ssm': 1.0 + nrm((DEPTH, SSM_HEADS), 0.1),
        'norm_ssm': 1.0 + nrm((DEPTH, D_INNER), 0.02),
        'w_ssm_out': nrm((DEPTH, D_INNER, D_MODEL), D_INNER ** -0.5),
        's5_lambda_re': -0.5 + nrm((DEPTH, S5_GROUPS, S5_STATE), 0.01),
        's5_lambda_im': lam_im + nrm((DEPTH, S5_GROUPS, S5_STATE), 0.01),
        's5_log_dt': unif((DEPTH, S5_GROUPS), float(np.log(1e-3)), float(np.log(1e-1))),
        's5_b_re': nrm((DEPTH, S5_GROUPS, S5_STATE, S5_GROUP), (2 * S5_GROUP) ** -0.5),
        's5_b_im': nrm((DEPTH, S5_GROUPS, S5_STATE, S5_GROUP), (2 * S5_GROUP) ** -0.5),
        's5_c_re': nrm((DEPTH, S5_GROUPS, S5_GROUP, S5_STATE), (2 * S5_STATE) ** -0.5),
        's5_c_im': nrm((DEPTH, S5_GROUPS, S5_GROUP, S5_STATE), (2 * S5_STATE) ** -0.5),
        's5_d': nrm((DEPTH, S5_WIDTH), 0.5),
        'w_glu': nrm((DEPTH, S5_WIDTH, 2 * D_MODEL), S5_WIDTH ** -0.5),
        'w_out': nrm((DEPTH, D_MODEL, D_MODEL), D_MODEL ** -0.5),
        'w_ffn_up': nrm((DEPTH, D_MODEL, 2 * D_FF), D_MODEL ** -0.5),
        'w_ffn_down': nrm((DEPTH, D_FF, D_MODEL), D_FF ** -0.5),
    }

def reference(x_prompt, x_sample, state_ssm, state_conv, state_s5_re, state_s5_im,
              norm_mix_pre, norm_mix_post, norm_ffn_pre, norm_ffn_post,
              w_in, conv_w, conv_b, dt_bias, a_log, d_ssm, norm_ssm, w_ssm_out,
              s5_lambda_re, s5_lambda_im, s5_log_dt, s5_b_re, s5_b_im, s5_c_re, s5_c_im, s5_d, w_glu,
              w_out, w_ffn_up, w_ffn_down):
    layers = [dict(norm_mix_pre=norm_mix_pre[l], norm_mix_post=norm_mix_post[l],
                   norm_ffn_pre=norm_ffn_pre[l], norm_ffn_post=norm_ffn_post[l],
                   w_in=w_in[l], conv_w=conv_w[l], conv_b=conv_b[l], dt_bias=dt_bias[l],
                   a_log=a_log[l], d_ssm=d_ssm[l], norm_ssm=norm_ssm[l], w_ssm_out=w_ssm_out[l],
                   s5_lambda_re=s5_lambda_re[l], s5_lambda_im=s5_lambda_im[l], s5_log_dt=s5_log_dt[l],
                   s5_b_re=s5_b_re[l], s5_b_im=s5_b_im[l], s5_c_re=s5_c_re[l], s5_c_im=s5_c_im[l],
                   s5_d=s5_d[l], w_glu=w_glu[l], w_out=w_out[l],
                   w_ffn_up=w_ffn_up[l], w_ffn_down=w_ffn_down[l]) for l in range(DEPTH)]
    bp = x_prompt.shape[0]
    z_ssm = jnp.zeros((DEPTH, bp, SSM_HEADS, HEAD_DIM, D_STATE), jnp.float32)
    z_conv = jnp.zeros((DEPTH, bp, CONV_WIDTH - 1, CONV_DIM), x_prompt.dtype)
    z_s5 = jnp.zeros((DEPTH, bp, S5_GROUPS, S5_STATE), jnp.float32)
    y_prompt, ssm_p, conv_p, s5r_p, s5i_p = trunk(x_prompt, z_ssm, z_conv, z_s5, z_s5, layers)
    y_sample, ssm_s, conv_s, s5r_s, s5i_s = trunk(x_sample, state_ssm, state_conv, state_s5_re, state_s5_im, layers)
    return (y_prompt, y_sample, ssm_p, conv_p, s5r_p, s5i_p, ssm_s, conv_s, s5r_s, s5i_s)


_drawn_inputs = setup_inputs


def setup_inputs(seed=0):
    import zlib

    import numpy as np

    out = dict(_drawn_inputs(seed))
    spreads = {}
    factors = {'norm_mix_post': 3.461,
     'norm_ffn_pre': 3.351,
     'norm_ffn_post': 17.291,
     'conv_b': 3.58,
     'norm_ssm': 3.591,
     's5_lambda_re': 17.652,
     's5_c_re': 2.831,
     's5_c_im': 2.852}
    for name, (base, spread) in spreads.items():
        noise = np.random.default_rng([zlib.crc32(name.encode()), seed]).standard_normal(out[name].shape)
        drawn = base * np.exp(spread * noise) if base else spread * noise
        out[name] = __import__('jax').numpy.asarray(drawn.astype(out[name].dtype))
    for name, factor in factors.items():
        out[name] = (out[name] * factor).astype(out[name].dtype)
    return out
```

```python
from contextlib import ExitStack

import numpy as np

import concourse.bass as bass
from concourse import mybir

F32 = mybir.dt.float32
F32R = mybir.dt.float32r
ALU = mybir.AluOpType
ACT = mybir.ActivationFunctionType
ds = bass.ds

P = 128
D_MODEL = 2048
SEQ = 256
DB = 8
DL = 4
T = SEQ + DB * DL
TOK = [(0, 128), (128, 128), (256, 32)]
D_INNER = 2 * D_MODEL
HD = 64
HEADS = D_INNER // HD
NG = 8
HG = HEADS // NG
NS = 128
CW = 4
CONV_DIM = D_INNER + 2 * NG * NS
S5G = 128
S5N = 64
S5C = 16
D_FF = 5632
EPS = 1e-6
OFF_XBC = D_INNER
OFF_B = OFF_XBC + D_INNER
OFF_DT = OFF_XBC + CONV_DIM
OFF_U = OFF_DT + HEADS
OFF_GA = OFF_U + D_MODEL
OFF_GB = OFF_GA + D_MODEL

KT = D_MODEL // P
RING = 4
LEAD = 3
SPL = 5
FT = D_FF // P
XR = 3 + SEQ + DB * (3 + DL)
XO = XR - 3
PAIRS = S5G // 2
NK = T // DL
PB = 8
TWO_PI_HI = 6.28125
TWO_PI_LO = float(2 * np.pi - 6.28125)
ROUND = 12582912.0
PI_IN = 3.1415925
GELU_C = float(np.sqrt(2 / np.pi))

C_G0 = 4
C_IT0 = 24
C_IT1 = 44
C_TAIL = C_IT1 + 28 * 7 + 40 - 28
C_GATE = C_TAIL + 8
C_GLU = C_GATE + 64
C_OUT = C_GLU + 64
C_UP = C_OUT + 32
C_DOWN = C_UP + 4 * FT
C_END = C_DOWN + 96
assert C_TAIL == 252 and C_END == 692

SHARED = {
    'lam_turned': ('vec_turned', 1), 'lam_ready': ('rstd_copied', 1), 'ldt_spread': ('dt_turned', 1),
    's5_step': ('dt_biased', 1), 's5_exponents': ('dt_u', 1), 's5_mag': ('dta_ready', 1),
    's5_abs': ('dec_ready', 1), 's5_sin': ('dt_copied', 1), 's5_scanned': ('acs_ready', 1),
    's5_bd_zero': ('dec_raw', 1), 'bbar_ready': ('a_exp', 1), 'u2_landed': ('x_landed', 48),
    'ut_landed': ('params_landed', 192), 's5_states_turned': ('x_rms', 2), 's5_states_ready': ('x_rstd', 2),
    's5_finals_turned': ('x_squared', 3), 'fo_copied': ('dt_act', 3), 'glu_tanh': ('z_tanh', 32),
    'glu_gated': ('z_done', 32), 'gate_tanh': ('conv_tanh', 48), 'gate_done': ('conv_out', 48),
    'f_tanh': ('conv_tap0', 48), 'f_silu': ('seg_clamped', 24), 'f_out': ('seg_exp', 24),
    'f_rounded': ('m_ready', 24), 'f_split': ('xdt_ready', 24), 'glu_summed': ('b_turned', 8),
    'glu_rounded': ('cb_ready', 8), 'merged': ('x01_turned', 8), 'm_squared': ('x2_turned', 8),
    'm_summed': ('acs0_spread', 8), 'f_squared': ('acs1_spread', 8), 'f_summed': ('e1_ready', 8),
    'm_normed': ('y0_ready', 8), 'x1_ready': ('y1_ready', 8), 'v_rounded': ('h_rounded', 16),
    'v_ready': ('h_ready', 16), 'h2_scaled': ('h_scaled', 16), 'h2_rounded': ('h_rounded', 32),
    'h2_ready': ('h_ready', 32), 'x1_landed': ('xT_landed', 16), 'gelu_arg': ('ht_ready', 8),
    'gelu_tanh': ('ht_copied', 8), 'gelu_out': ('off1_ready', 8),
}

NAMES = ['x_prompt', 'x_sample', 'state_ssm', 'state_conv', 'state_s5_re', 'state_s5_im',
         'norm_mix_pre', 'norm_mix_post', 'norm_ffn_pre', 'norm_ffn_post', 'w_in', 'conv_w', 'conv_b',
         'dt_bias', 'a_log', 'd_ssm', 'norm_ssm', 'w_ssm_out', 's5_lambda_re', 's5_lambda_im',
         's5_log_dt', 's5_b_re', 's5_b_im', 's5_c_re', 's5_c_im', 's5_d', 'w_glu', 'w_out',
         'w_ffn_up', 'w_ffn_down']
OUTS = [('y_prompt', (1, SEQ, D_MODEL)), ('y_sample', (DB, DL, D_MODEL)),
        ('ssm_prompt', (1, 1, HEADS, HD, NS)), ('conv_prompt', (1, 1, CW - 1, CONV_DIM)),
        ('s5_re_prompt', (1, 1, S5G, S5N)), ('s5_im_prompt', (1, 1, S5G, S5N)),
        ('ssm_sample', (1, DB, HEADS, HD, NS)), ('conv_sample', (1, DB, CW - 1, CONV_DIM)),
        ('s5_re_sample', (1, DB, S5G, S5N)), ('s5_im_sample', (1, DB, S5G, S5N))]


def chunk_at(g, t):
    if isinstance(g, int) and g < 1:
        return (C_G0 if g < 0 else C_IT0) + t - 8
    return g * 28 + (C_IT1 - 28 + t)


def quarter(g, t):
    if isinstance(g, int) and g < 1:
        return ((C_G0 if g < 0 else C_IT0) + t - 8) // RING
    return g * 7 + ((C_IT1 - 28) // RING + t // RING)


def build(nc, a, o):
    w_in = a['w_in'][0]
    w_ssm_out = a['w_ssm_out'][0]
    w_glu = a['w_glu'][0]
    w_out = a['w_out'][0]
    w_up = a['w_ffn_up'][0]
    w_down = a['w_ffn_down'][0]

    xT_dram = nc.dram_tensor("xT_scratch", (P, KT * T), F32, kind="Internal").ap()
    x1_dram = nc.dram_tensor("x1_scratch", (P, KT * T), F32, kind="Internal").ap()
    u_dram = nc.dram_tensor("u_scratch", (D_MODEL, DL * NK), F32, kind="Internal").ap()
    y5_dram = nc.dram_tensor("y5_scratch", (D_MODEL, DL * NK), F32, kind="Internal").ap()

    base = 16512
    top = nc.sbuf_usable_end
    used = {}

    def sb(name, shape, dt, at):
        n = 4
        for s in shape[1:]:
            n *= s
        end = (at + n + 31) // 32 * 32
        assert end <= top, (name, end, top)
        used[name] = (at, end)
        return nc.alloc_sbuf_tensor_at(name, list(shape), dt, offset=at), end

    at = base
    ident, at = sb("ident", [P, P], F32, at)
    ones, at = sb("ones", [P, P], F32, at)
    tri, at = sb("tri", [P, P], F32, at)
    btri, at = sb("btri", [32, 32], F32, at)
    bones, at = sb("bones", [32, 32], F32, at)
    bmask, at = sb("bmask", [32, DB], F32, at)
    eps1, at = sb("eps1", [P, 4], F32, at)
    vec, at = sb("vec", [P, 64 + 48 + 192 + 48], F32, at)
    dcol, at = sb("dcol", [P, HEADS // 2], F32, at)
    sx2, at = sb("sx2", [P, 2], F32, at)
    tokv, at = sb("tokv", [P, 13, HEADS], F32, at)
    DT, DTA, ACS, DEC, CDEC = 0, 3, 6, 9, 12
    gtv, at = sb("gtv", [P, 13, HG], F32, at)
    gcv, at = sb("gcv", [P, 5, 6], F32, at)
    gnv, at = sb("gnv", [P, 2, 4], F32, at)
    rstd, at = sb("rstd", [P, T], F32, at)
    sst, at = sb("sst", [P, T], F32, at)
    raw, at = sb("raw", [P, RING, 1024], F32, at)
    ring_raw_at = used["raw"][0]
    w_hi, at = sb("w_hi", [P, RING, 1024], F32R, at)
    w_lo, at = sb("w_lo", [P, RING, 1024], F32R, at)
    h_at = at
    h_hi, at = sb("h_hi", [P, KT, T], F32R, at)
    h_lo, at = sb("h_lo", [P, KT, T], F32R, at)
    free_at = at
    N_PRE, N_POST, N_FPRE, N_FPOST, V_CB, V_CW, V_NS, V_D5 = 0, 16, 32, 48, 64, 112, 304, 336

    ya, at = sb("ya", [P, KT, T], F32, at)
    ya_end = at
    y_hi, at = sb("y_hi", [P, 4, T], F32R, at)
    y_lo, at = sb("y_lo", [P, 4, T], F32R, at)
    craw, at = sb("craw", [P, 2, XR + 1], F32, at)
    cacc, at = sb("cacc", [P, 2, XO], F32, at)
    hist, at = sb("hist", [P, 6, 24], F32, at)
    cnew, at = sb("cnew", [P, 6, 27], F32, at)
    xc, at = sb("xc", [P, 2, 6, T], F32, at)
    zs, at = sb("zs", [P, 2, 4, T], F32, at)
    ssd_at = at
    xdt, at = sb("xdt", [P, 3, 512], F32, at)
    xw, at = sb("xw", [P, 4, 512], F32, at)
    btok, at = sb("btok", [P, 3, NS], F32, at)
    bm, at = sb("bm", [32, DB, NS], F32, at)
    cbm, at = sb("cbm", [P, T], F32, at)
    seg, at = sb("seg", [P, 2, HG * P], F32, at)
    ee, at = sb("ee", [P, 4, 160], F32, at)
    ht, at = sb("ht", [P, 512], F32, at)
    offe, at = sb("offe", [P, 512], F32, at)
    yb, at = sb("yb", [P, 4, T], F32, at)
    h0, at = sb("h0", [P, 4, 4, NS], F32, at)
    h0t, at = sb("h0t", [P, 2, 512], F32, at)
    cst, _ = sb("cst", [24, 768], F32, used["h0t"][0])
    cout, at = sb("cout", [27, 768], F32, at)
    pout, at = sb("pout", [P, 512], F32, at)
    dta2, at = sb("dta2", [32, 512], F32, at)
    dta1 = offe
    uo, _ = sb("uo", [P, 2, T], F32, used["cacc"][0])
    cth = craw[:, :, 3:3 + XO]
    th = craw[:, :, 3:3 + T]

    at = ssd_at
    xnat, at = sb("xnat", [P, 3, D_MODEL], F32, at)
    xts, at = sb("xts", [P, 2, T], F32, at)
    hf, at = sb("hf", [P, 2, T], F32, at)
    vraw, at = sb("vraw", [P, 4, P], F32, at)
    rowv, at = sb("rowv", [P, 3, HEADS], F32, at)
    dw, at = sb("dw", [P, 7, 3 * HEADS], F32, at)
    sx, at = sb("sx", [P, 4], F32, at)
    dtT, at = sb("dtT", [HEADS, T], F32, at)
    seg_sq, at = sb("seg_sq", [P, D_MODEL], F32, at)

    sgb, at = sb("sgb", [P, KT, T], F32, ya_end)
    gth, _ = sb("gth", [P, 2, T], F32, at)
    u2, at = sb("u2", [P, PAIRS, NK], F32, at)
    s5_s_at = at
    st5, at = sb("st5", [P, 2, PAIRS, NK], F32, at)
    en5, at = sb("en5", [P, 2, PAIRS, 9], F32, at)
    tt5, at = sb("tt5", [P, DL, PAIRS, S5C], F32, at)
    s5_end = at
    at = h_at
    qbd, at = sb("qbd", [P, 2, PB, P], F32, at)
    pw5, at = sb("pw5", [P, 2, PB, P], F32, at)
    ct5, at = sb("ct5", [P, 2, PAIRS, S5C], F32, at)
    bb5, at = sb("bb5", [P, 2, PAIRS, S5C], F32, at)
    tm5, at = sb("tm5", [P, 2, 512], F32, at)
    assert at <= free_at
    tbd = pw5[:, 0]
    at = ring_raw_at
    cn5, at = sb("cn5", [P, 2, 8, P], F32, at)
    sn5, at = sb("sn5", [PAIRS, 2, DB, P], F32, at)
    ln5, at = sb("ln5", [PAIRS, 3, P], F32, at)
    ldt, at = sb("ldt", [PAIRS, 2], F32, at)
    lam, at = sb("lam", [P, 3, PAIRS], F32, at)
    pr5, at = sb("pr5", [P, 14, PAIRS], F32, at)
    pq5, at = sb("pq5", [P, 2, DL, PAIRS], F32, at)
    po5, at = sb("po5", [P, 2, DL, PAIRS], F32, at)
    a4x, at = sb("a4x", [P, 2, PAIRS], F32, at)
    sh5, at = sb("sh5", [P, 3, P], F32, at)
    fin5, at = sb("fin5", [P, 2, 9, PAIRS], F32, at)
    fo5, at = sb("fo5", [PAIRS, 18, P], F32, at)
    gs5, at = sb("gs5", [P, PAIRS, S5C], F32, at)
    assert at <= h_at
    ut5, _ = sb("ut5", [P, KT, T], F32, s5_s_at)
    yt5, at = sb("yt5", [P, KT, T], F32, s5_s_at + KT * T * 4)
    gt5, at = sb("gt5", [P, 3, T], F32, at)

    mg_hi, at = sb("mg_hi", [P, KT, T], F32R, used["u2"][1])
    mg_lo, at = sb("mg_lo", [P, KT, T], F32R, at)
    gl, at = sb("gl", [P, 2, 2, T], F32, at)
    assert at <= top
    mt, at = sb("mt", [P, KT, T], F32, ya_end)
    msq, at = sb("msq", [P, 2, T], F32, at)
    x1, _ = sb("x1", [P, KT, T], F32, used["ya"][0])
    f_hi, at = sb("f_hi", [P, FT, T], F32R, free_at)
    f_lo, at = sb("f_lo", [P, FT, T], F32R, at)
    fg, at = sb("fg", [P, 2, 2, T], F32, at)
    fsq, at = sb("fsq", [P, 2, T], F32, at)
    fT, at = sb("fT", [P, KT, T], F32, h_at)
    x1r, at = sb("x1r", [P, KT, T], F32, at)
    assert at <= free_at
    on, at = sb("on", [P, 3, D_MODEL], F32, free_at)

    with ExitStack() as ctx:
        acc = [ctx.enter_context(nc.psum_tensor(f"acc{i}", [P, 512], F32)) for i in range(4)]
        side = [ctx.enter_context(nc.psum_tensor(f"side{i}", [P, 512], F32)) for i in range(4)]
        s0, s1, s2, s3 = side
        sems = {}

        def sem(name):
            name, _ = SHARED.get(name, (name, 0))
            if name not in sems:
                sems[name] = ctx.enter_context(nc.semaphore(name))
            return sems[name]

        landed = [sem(f"chunk_landed{i}") for i in range(RING)]
        h0_landed = [sem(f"h0_landed{i}") for i in range(4)]
        h0_stored = [sem(f"h0_stored{i}") for i in range(4)]
        xT_stored = [sem(f"xT_stored{i}") for i in range(2)]
        hi_ready = sem("w_hi_ready")
        lo_ready = sem("w_lo_ready")
        multiplied = sem("chunk_multiplied")
        freed = sem("acc_freed")

        def reach(name, v):
            return sem(name), v + SHARED.get(name, (name, 0))[1]

        def wait(eng, name, v):
            if not isinstance(v, int) or v > 0:
                eng.wait_ge(*reach(name, v))

        def bc(ap, n, axis):
            ap = ap.unsqueeze(axis)
            shape = list(ap.shape)
            shape[axis] = n
            return ap.to_broadcast(shape)

        def acc_of(par, og):
            k = 2 * ((par + og) % 2)
            return acc[k], acc[k + 1]

        block = ctx.enter_context(nc.Block())

        @block.sync
        def _(sp):
            for c, (t0, n) in enumerate(TOK[:2]):
                sp.dma_start(xnat[:, c, :], a['x_prompt'][0, t0:t0 + n, :]).then_inc(sem("x_landed"), 16)
            sp.dma_start(xnat[0:32, 2, :], a['x_sample'].rearrange("b t d -> (b t) d")).then_inc(sem("x_landed"), 16)

            def load(c, q, slot, src, n=1024, two=False):
                if not isinstance(c, int) or c >= RING:
                    sp.wait_ge(lo_ready, c - (RING - 1))
                dst = raw[:, slot, 0:n]
                if two:
                    dst = dst.rearrange("p (t s n) -> p t s n", t=n // 256, s=2)
                    halves = [(dst[:, :, k, :], src[:, :, k, :]) for k in range(2)]
                else:
                    dst = dst.rearrange("p (t n) -> p t n", n=src.shape[-1])
                    halves = [(dst[:, 0:2], src[:, 0:2]), (dst[:, 2:], src[:, 2:])]
                for to, of in halves:
                    sp.dma_start(to, of).then_inc(landed[slot], 16)

            def rows(w, kc):
                return w[kc * 512:(kc + 1) * 512, :].rearrange("(t p) n -> p t n", p=P)

            def rows2(w, kc):
                return w[kc * 512:(kc + 1) * 512, :].rearrange("(t p) (s n) -> p t s n", p=P, s=2)

            st = a['state_ssm'][0].rearrange("b (g h) p n -> b g (h p) n", g=NG)
            so = o['ssm_sample'][0].rearrange("b (g h) p n -> b g (h p) n", g=NG)
            po = o['ssm_prompt'][0, 0].rearrange("(g h) p n -> g (h p) n", g=NG)
            cs_in = a['state_conv'][0].rearrange("b k c -> (b k) c")
            cs_out = o['conv_sample'][0].rearrange("b k c -> (b k) c")
            cp_out = o['conv_prompt'][0, 0]

            def conv_history(n):
                wait(sp, "history_turned", n)
                wait(sp, "h0_read", n * 8 - 8)
                sp.dma_start(cst[:, 0:P], cs_in[:, ds(n * P + D_INNER, P)]).then_inc(sem("history_landed"), 16)
                sp.dma_start(cst[:, P:2 * P], cs_in[:, ds(n * P + (D_INNER + NG * NS), P)]).then_inc(sem("history_landed"), 16)
                sp.dma_start(cst[:, 2 * P:], cs_in[:, ds(n * 512, 512)]).then_inc(sem("history_landed"), 16)

            def conv_store(n):
                sp.wait_ge(sem("conv_rows_ready"), n + 1)
                for dst, r0, r1 in ((cp_out, 0, 3), (cs_out, 3, 27)):
                    sp.dma_start(dst[:, ds(n * P + D_INNER, P)], cout[r0:r1, 0:P]).then_inc(sem("conv_stored"), 16)
                    sp.dma_start(dst[:, ds(n * P + (D_INNER + NG * NS), P)], cout[r0:r1, P:2 * P]).then_inc(sem("conv_stored"), 16)
                    sp.dma_start(dst[:, ds(n * 512, 512)], cout[r0:r1, 2 * P:]).then_inc(sem("conv_stored"), 16)

            def side_dmas(t, g, ssd, conv):
                if ssd and t == 3:
                    conv_store(g)
                if conv and t == 2:
                    conv_history(g + 1)
                if not ssd:
                    return
                if 6 <= t < 10:
                    b = t - 6
                    if not isinstance(g, int) or g > 0:
                        sp.wait_ge(h0_stored[b], g * 32)
                    sp.dma_start(h0[:, b], st[b, g].rearrange("(i q) n -> q i n", q=P)).then_inc(h0_landed[b], 16)
                if t == 15:
                    sp.wait_ge(sem("prompt_state_ready"), g + 1)
                    sp.dma_start(po[g].rearrange("(i q) n -> q i n", q=P), pout[:, :].rearrange("q (i n) -> q i n", i=4)).then_inc(sem("prompt_state_stored"), 16)
                if 18 <= t < 26:
                    b = t - 18
                    sp.wait_ge(sem("h0_updated"), g * 8 + (b + 1))
                    sp.dma_start(so[b, g].rearrange("(i q) n -> q i n", q=P), h0[:, b % 4]).then_inc(h0_stored[b % 4], 16)
                if 20 <= t < 24:
                    b = t - 16
                    sp.wait_ge(h0_stored[b % 4], g * 32 + 16)
                    sp.dma_start(h0[:, b % 4], st[b, g].rearrange("(i q) n -> q i n", q=P)).then_inc(h0_landed[b % 4], 16)

            def group_chunk(t, g):
                j, kc, n = (t - 8) // 4, (t - 8) % 4, g + 1
                c, q = chunk_at(g, t), quarter(g, t)
                if j == 0:
                    src = w_in[kc * 512:(kc + 1) * 512, OFF_B:OFF_B + 2 * NG * NS].rearrange(
                        "(t p) (s n) -> p t s n", p=P, s=2)[:, :, :, ds(n * P, P)]
                    load(c, q, t % 4, src, two=True)
                else:
                    col = n * 512 + (OFF_XBC + (j - 1) * 256 if j < 3 else (j - 3) * 256)
                    load(c, q, t % 4, rows(w_in, kc)[:, :, ds(col, 256)])

            def g2_chunk(t, c, q, m):
                src = w_ssm_out.rearrange("(g t p) n -> g p t n", t=4, p=P)[m, :, :, t * 256:(t + 1) * 256]
                load(c, q, t % 4, src)

            conv_history(0)
            for c in range(4):
                load(c, 0, c, rows(w_in, c)[:, :, OFF_DT:OFF_DT + P], n=512)
            for t in range(8, 28):
                group_chunk(t, -1)
            for t in range(8, 8 + LEAD):
                group_chunk(t, 0)
            for t in range(28):
                if t >= 8 + LEAD:
                    group_chunk(t, 0)
                side_dmas(t, 0, True, True)

            def iteration(g):
                for t in range(28):
                    if t < 8:
                        g2_chunk(t, chunk_at(g, t), quarter(g, t), g - 1)
                    else:
                        group_chunk(t, g)
                    side_dmas(t, g, True, True)

            with sp.Fori(0, 3) as i:
                iteration(i * 2 + 1)
                iteration(i * 2 + 2)
            def u_store(k):
                sp.wait_ge(sem("u_ready"), 2 * k + 2)
                sp.dma_start(u_dram[k * 256:(k + 1) * 256, :].rearrange("(i p) t -> p i t", p=P), uo[:, :, :]).then_inc(sem("u_stored"), 16)

            for t in range(40):
                c = chunk_at(7, t)
                if t < 8:
                    g2_chunk(t, c, c // 4, 6)
                else:
                    k, kc = (t - 8) // 4, t % 4
                    load(c, c // 4, t % 4, rows(w_in, kc)[:, :, OFF_U + k * 256:OFF_U + (k + 1) * 256])
                side_dmas(t, 7, True, False)
                if t >= 18 and t % 4 == 2:
                    u_store((t - 18) // 4)
            for t in range(8):
                c = C_TAIL + t
                g2_chunk(t, c, c // 4, 7)
                if t % 4 == 2:
                    u_store(6 + t // 4)
            def gate_chunks(k, c):
                for kc in range(4):
                    load(c + kc, 0, kc, rows(w_in, kc)[:, :, ds(k * 256 + OFF_GA, 256)])

            with sp.Fori(0, 16) as k:
                gate_chunks(k, k * 4 + C_GATE)
            sp.wait_ge(lo_ready, C_GLU)
            sp.wait_ge(multiplied, C_GLU)
            prm = sem("s5_params_landed")
            for k, nm in enumerate(('s5_lambda_re', 's5_lambda_im')):
                sp.dma_start(ln5[:, k, :], a[nm][0].rearrange("(p g) n -> p (g n)", g=2)).then_inc(prm, 16)
            sp.dma_start(ldt[:, :], a['s5_log_dt'][0].rearrange("(p g) -> p g", g=2)).then_inc(prm, 16)
            for k, nm in enumerate(('s5_b_re', 's5_b_im')):
                sp.dma_start(bb5[:, k], a[nm][0].rearrange("(p g) n c -> (g n) p c", g=2)).then_inc(prm, 16)
            for k, nm in enumerate(('s5_c_re', 's5_c_im')):
                v = a[nm][0].rearrange("(b p g) c n -> p g c b n", p=8, g=2)
                for p in range(8):
                    for g2 in range(2):
                        sp.dma_start(cn5[p * 16:(p + 1) * 16, k, :, g2 * S5N:(g2 + 1) * S5N], v[p, g2]).then_inc(prm, 16)
            sp.wait_ge(sem("u_stored"), 16 * 8)
            sp.wait_ge(*reach("gate_done", 32))
            for g2 in range(2):
                for j in range(4):
                    src = u_dram.rearrange("(p f) (j k) -> f p j k", f=32, j=4)[g2 * 16:(g2 + 1) * 16, :, j, :]
                    r = g2 * 64 + j * 16
                    sp.dma_start(u2[r:r + 16, :, :], src).then_inc(sem("u2_landed"), 16)
            for k, nm in enumerate(('state_s5_re', 'state_s5_im')):
                sp.dma_start(sn5[:, k], a[nm][0].rearrange("b (p g) n -> p b (g n)", g=2)).then_inc(sem("s5_states_landed"), 16)
            sp.wait_ge(sem("s5_y_copied"), 16)
            for g2 in range(2):
                for j in range(4):
                    dst = y5_dram.rearrange("(p f) (j k) -> f p j k", f=32, j=4)[g2 * 16:(g2 + 1) * 16, :, j, :]
                    r = g2 * 64 + j * 16
                    sp.dma_start(dst, u2[r:r + 16, :, :]).then_inc(sem("y5_stored"), 16)
            sp.dma_start(ut5[:, :, :], u_dram.rearrange("(i p) t -> p i t", p=P)).then_inc(sem("ut_landed"), 16)
            sp.wait_ge(sem("y5_stored"), 16 * 8)
            sp.dma_start(yt5[:, :, :], y5_dram.rearrange("(i p) t -> p i t", p=P)).then_inc(sem("yt_landed"), 16)
            sp.wait_ge(*reach("fo_copied", 5))
            for k, (nm, nm2) in enumerate((('s5_re_prompt', 's5_re_sample'), ('s5_im_prompt', 's5_im_sample'))):
                sp.dma_start(o[nm][0, 0].rearrange("(p g) n -> p (g n)", g=2), fo5[:, k * 9, :]).then_inc(sem("s5_finals_stored"), 16)
                sp.dma_start(o[nm2][0].rearrange("b (p g) n -> p b (g n)", g=2), fo5[:, k * 9 + 1:k * 9 + 9, :]).then_inc(sem("s5_finals_stored"), 16)
            sp.wait_ge(sem("s5_finals_stored"), 64)

            with sp.Fori(0, 16) as k:
                for kc in range(4):
                    load(k * 4 + (C_GLU + kc), 0, kc, rows2(w_glu, kc)[:, :, :, ds(k * P, P)], two=True)
            with sp.Fori(0, 8) as k:
                for kc in range(4):
                    load(k * 4 + (C_OUT + kc), 0, kc, rows(w_out, kc)[:, :, ds(k * 256, 256)])
            sp.wait_ge(*reach("merged", 16))
            for s in xT_stored:
                sp.wait_ge(s, 16 * KT // 2)
            sp.dma_start(x1[:, :, :], xT_dram.rearrange("p (i t) -> p i t", i=KT)).then_inc(sem("xT_landed"), 16)
            for c in range(4):
                load(C_UP + c, 0, c, rows2(w_up, c)[:, :, :, 0:P], two=True)
            sp.wait_ge(sem("x1_squared"), 16)
            sp.dma_start(x1_dram.rearrange("p (i t) -> p i t", i=KT), x1[:, :, :]).then_inc(sem("x1_stored"), 16)
            with sp.Fori(1, FT) as k:
                for kc in range(4):
                    load(k * 4 + (C_UP + kc), 0, kc, rows2(w_up, kc)[:, :, :, ds(k * P, P)], two=True)

            def down(k, i):
                r0, n = (i * 4, 4) if i < 8 else (32 + (i - 8) * 3, 3)
                src = w_down[r0 * P:(r0 + n) * P, :].rearrange("(t p) n -> p t n", p=P)[:, :, ds(k * 256, 256)]
                load(k * 12 + (C_DOWN + i), 0, i % 4, src, n=n * 256)

            for i in range(12):
                down(0, i)
            sp.wait_ge(sem("x1_stored"), 16)
            sp.wait_ge(multiplied, C_DOWN)
            sp.dma_start(x1r[:, :, :], x1_dram.rearrange("p (i t) -> p i t", i=KT)).then_inc(sem("x1_landed"), 16)
            with sp.Fori(1, 8) as k:
                for i in range(12):
                    down(k, i)
            sp.wait_ge(sem("out_rows"), 12)
            for c, (t0, n) in enumerate(TOK[:2]):
                sp.dma_start(o['y_prompt'][0, t0:t0 + n, :], on[:, c, :]).then_inc(sem("y_stored"), 16)
            sp.dma_start(o['y_sample'].rearrange("b t d -> (b t) d"), on[0:32, 2, :]).then_inc(sem("y_stored"), 16)
            sp.wait_ge(sem("y_stored"), 48)
            sp.wait_ge(sem("conv_stored"), 96 * NG)
            sp.wait_ge(sem("prompt_state_stored"), 16 * NG)
            for s in h0_stored:
                sp.wait_ge(s, 32 * NG)

        @block.gpsimd
        def _(pool):
            made = sem("masks_made")
            for m, v in ((ident, 0.0), (ones, 1.0), (tri, 1.0), (btri, 1.0), (bones, 1.0), (bmask, 1.0), (sh5, None)):
                if v is not None:
                    pool.memset(m[:, :], v).then_inc(made, 1)
            pool.wait_ge(made, 6)
            pool.affine_select(out=ident[:, :], in_=ident[:, :], compare_op=ALU.not_equal, fill=1.0,
                               base=0, pattern=[[-1, P]], channel_multiplier=1).then_inc(made, 1)
            pool.affine_select(out=tri[:, :], in_=tri[:, :], compare_op=ALU.is_ge, fill=0.0,
                               base=0, pattern=[[1, P]], channel_multiplier=-1).then_inc(made, 1)
            pool.affine_select(out=btri[:, :], in_=btri[:, :], compare_op=ALU.is_ge, fill=0.0,
                               base=0, pattern=[[1, 32]], channel_multiplier=-1).then_inc(made, 1)
            pool.affine_select(out=bones[:, :], in_=bones[:, :], compare_op=ALU.is_ge, fill=0.0,
                               base=DL - 1, pattern=[[DL, DB], [0, DL]], channel_multiplier=-1).then_inc(made, 1)
            pool.affine_select(out=bmask[:, :], in_=bmask[:, :], compare_op=ALU.is_ge, fill=0.0,
                               base=DL - 1, pattern=[[DL, DB]], channel_multiplier=-1).then_inc(made, 1)
            pool.wait_ge(made, 11)
            pool.affine_select(out=btri[:, :], in_=btri[:, :], compare_op=ALU.is_ge, fill=0.0,
                               base=0, pattern=[[-DL, DB], [0, DL]], channel_multiplier=1).then_inc(made, 1)
            pool.affine_select(out=bones[:, :], in_=bones[:, :], compare_op=ALU.is_ge, fill=0.0,
                               base=0, pattern=[[-DL, DB], [0, DL]], channel_multiplier=1).then_inc(made, 1)
            pool.affine_select(out=bmask[:, :], in_=bmask[:, :], compare_op=ALU.is_ge, fill=0.0,
                               base=0, pattern=[[-DL, DB]], channel_multiplier=1).then_inc(made, 1)
            pool.memset(eps1[:, 0:1], EPS).then_inc(made, 1)
            pool.memset(eps1[:, 1:2], 4 * EPS).then_inc(made, 1)
            pool.memset(eps1[:, 2:3], float(np.pi / 2)).then_inc(made, 1)
            pool.memset(ya[:, :, :], 0.0).then_inc(made, 1)
            pool.memset(craw[:, :, :], 0.0).then_inc(made, 1)
            pool.memset(sst[:, :], 0.0).then_inc(made, 1)

            def squares(g):
                pool.wait_ge(sem("y_split"), g * 4 + 4)
                pool.tensor_tensor(yb[:, :, :], yb[:, :, :], yb[:, :, :], ALU.mult).then_inc(sem("y_squared"), 1)
                pool.wait_ge(sem("y_squared"), g + 1)
                for i in range(4):
                    pool.wait_ge(sem("y_summed"), g * 4 + i) if not (isinstance(g, int) and g * 4 + i == 0) else None
                    pool.tensor_tensor(sst[:, :], sst[:, :], yb[:, i, :], ALU.add).then_inc(sem("y_summed"), 1)

            pool.wait_ge(made, 20)
            squares(0)
            with pool.Fori(1, NG) as g:
                squares(g)

            pool.wait_ge(multiplied, C_GLU)
            z = sem("s5_zeros")
            pool.memset(qbd[:, :, :, :], 0.0).then_inc(z, 1)
            pool.memset(sh5[:, :, :], 0.0).then_inc(z, 1)
            pool.memset(st5[:, :, :, 0:1], 0.0).then_inc(z, 1)
            pool.wait_ge(z, 3)
            for k in range(3):
                n = 64 - 16 * (k + 1)
                for r in range(2):
                    v = sh5[:, k, r * 64:r * 64 + n]
                    pool.affine_select(out=v, in_=v, compare_op=ALU.not_equal, fill=1.0,
                                       base=-(r * 64 + 16 * (k + 1)), pattern=[[-1, n]],
                                       channel_multiplier=1).then_inc(z, 1)

        @block.scalar
        def _(act):
            copy = lambda out, in_, **k: nc.scalar.activation(out, in_, ACT.Copy, **k)

            pl = sem("params_landed")
            act.dma_start(vraw[0:96, 0, :], a['conv_w'][0, 0:2].rearrange("k (i p) -> (k i) p", p=P)).then_inc(pl, 16)
            act.dma_start(vraw[0:96, 1, :], a['conv_w'][0, 2:4].rearrange("k (i p) -> (k i) p", p=P)).then_inc(pl, 16)
            for k, nm in enumerate(('norm_mix_pre', 'norm_mix_post', 'norm_ffn_pre', 'norm_ffn_post')):
                act.dma_start(vraw[k * 16:(k + 1) * 16, 2, :], a[nm][0].rearrange("(i p) -> i p", p=P)).then_inc(pl, 16)
            act.dma_start(vraw[64:112, 2, :], a['conv_b'][0].rearrange("(i p) -> i p", p=P)).then_inc(pl, 16)
            act.dma_start(vraw[0:32, 3, :], a['norm_ssm'][0].rearrange("(i p) -> i p", p=P)).then_inc(pl, 16)
            act.dma_start(vraw[32:48, 3, :], a['s5_d'][0].rearrange("(i p) -> i p", p=P)).then_inc(pl, 16)
            for k, nm in enumerate(('dt_bias', 'a_log', 'd_ssm')):
                act.dma_start(rowv[:, k, :], a[nm].to_broadcast([P, HEADS])).then_inc(pl, 16)

            act.wait_ge(sem("x_landed"), 48)
            for c, (t0, n) in enumerate(TOK):
                wait(act, "x_squared", c)
                nc.scalar.activation(seg_sq[0:n, :], xnat[0:n, c, :], ACT.Square, accum_out=sx[0:n, c:c + 1]).then_inc(sem("x_squared"), 1)
            act.wait_ge(sem("x_squared"), 3)
            act.wait_ge(sem("masks_made"), 20)
            nc.scalar.activation(sx[:, 0:2], sx[:, 0:2], ACT.Sqrt, scale=1.0 / D_MODEL, bias=eps1[:, 0:1]).then_inc(sem("x_rms"), 1)
            nc.scalar.activation(sx[0:32, 2:3], sx[0:32, 2:3], ACT.Sqrt, scale=1.0 / D_MODEL, bias=eps1[0:32, 0:1]).then_inc(sem("x_rms"), 1)
            act.wait_ge(sem("x_rstd_spread"), 1)
            copy(rstd[:, :], s3[:, 0:T]).then_inc(sem("rstd_copied"), 1)
            for i in range(KT):
                act.wait_ge(sem("x_turned"), i + 1)
                if i >= 2:
                    act.wait_ge(xT_stored[i % 2], 16 * (i // 2))
                copy(xts[:, i % 2, :], acc[i % 4][:, 0:T]).then_inc(sem("xT_copied"), 1)
                act.wait_ge(sem("xT_copied"), i + 1)
                act.dma_start(xT_dram[:, i * T:(i + 1) * T], xts[:, i % 2, :]).then_inc(xT_stored[i % 2], 16)
                act.wait_ge(sem("h_scaled"), i + 1)
                copy(h_hi[:, i, :], hf[:, i % 2, :]).then_inc(sem("h_rounded"), 1)

            def split(c, q, slot, n=1024):
                act.wait_ge(landed[slot], q * 32 + 32)
                if not isinstance(c, int) or c >= RING:
                    act.wait_ge(multiplied, c - (RING - 1))
                copy(w_hi[:, slot, 0:n], raw[:, slot, 0:n]).then_inc(hi_ready, 1)

            def split_at(g, t):
                split(chunk_at(g, t) + LEAD, quarter(g, t + LEAD), (t + LEAD) % 4)

            def conv_in(k, n, c_last, par):
                act.wait_ge(multiplied, c_last + 1)
                wait(act, "conv_tapped", n * 18 + 3 * (k - 1))
                wait(act, "conv_out", n * 6 + (k - 1))
                if k < 2:
                    wait(act, "z_done", n * 4)
                b = k % 2
                src = acc_of(par, 8 + k // 2)[k % 2]
                copy(craw[:, b, 3:3 + SEQ], src[:, 0:SEQ])
                row = craw[:, b, SEQ + 3:XR].rearrange("p (b t) -> p b t", t=7)
                copy(row[:, :, 3:7], src[:, SEQ:T].rearrange("p (b t) -> p b t", t=DL))
                copy(row[:, :, 0:3], hist[:, k, :].rearrange("p (b t) -> p b t", t=3)).then_inc(sem("conv_in_ready"), 1)
                act.wait_ge(sem("conv_in_ready"), n * 6 + (k + 1))
                act.wait_ge(sem("conv_vectors"), n + 1)
                nc.scalar.activation(cacc[:, b, :], craw[:, b, 0:XO], ACT.Identity, bias=gcv[:, 0, k:k + 1],
                                     scale=gcv[:, 1, k:k + 1]).then_inc(sem("conv_tap0"), 1)

            def conv_tanh(k, n):
                act.wait_ge(sem("conv_tapped"), n * 18 + 3 * (k + 1))
                nc.scalar.activation(cth[:, k % 2, :], cacc[:, k % 2, :], ACT.Tanh).then_inc(sem("conv_tanh"), 1)

            def z_tanh(k, n, c_last, par):
                act.wait_ge(multiplied, c_last + 1)
                wait(act, "z_done", n * 4 + (k - 1))
                if k < 2:
                    act.wait_ge(sem("conv_out"), n * 6 + 6)
                nc.scalar.activation(th[:, k % 2, :], acc_of(par, 11 + k // 2)[k % 2][:, 0:T], ACT.Tanh, scale=0.5).then_inc(sem("z_tanh"), 1)

            def seg_exp(c, g):
                act.wait_ge(sem("seg_clamped"), g * 3 + (c + 1))
                v = seg[:, c, :] if c < 2 else seg[0:32, 0, 0:HG * 32]
                nc.scalar.activation(v, v, ACT.Exp).then_inc(sem("seg_exp"), 1)

            def side_work(t, g, par, ssd, conv):
                n = g + 1
                c0 = chunk_at(g, 0)
                if ssd:
                    for k in (2, 3) if t == 0 else ():
                        z_tanh(k, g, c0 - 1 if not (isinstance(g, int) and g == 0) else C_IT0 - 1, 1 - par)
                    if t == 1:
                        act.wait_ge(sem("b_turned"), g + 1)
                        copy(btok[:, 0:2, :], s0[:, 0:256].rearrange("p (c n) -> p c n", c=2))
                        copy(btok[0:32, 2, :], s0[0:32, 256:384]).then_inc(sem("btok_ready"), 1)
                    if t == 4:
                        seg_exp(0, g)
                    if t == 5:
                        act.wait_ge(sem("e1_ready"), g + 1)
                        nc.scalar.activation(ee[:, :, 0:P], s1[:, :].rearrange("p (i q) -> p i q", i=4), ACT.Exp).then_inc(sem("e1_exp"), 1)
                    if t == 6:
                        seg_exp(1, g)
                    if t == 7:
                        act.wait_ge(sem("es_ready"), g + 1)
                        nc.scalar.activation(ee[:, :, P:160], s0[:, 0:P].rearrange("p (i q) -> p i q", i=4), ACT.Exp).then_inc(sem("es_exp"), 1)
                        act.wait_ge(sem("ht_ready"), g + 1)
                        copy(ht[:, :], s1[:, :]).then_inc(sem("ht_copied"), 1)
                    if t == 8:
                        seg_exp(2, g)
                    if t == 9:
                        act.wait_ge(sem("prompt_state"), g + 1)
                        wait(act, "prompt_state_stored", g * 16)
                        copy(pout[:, :], s3[:, :]).then_inc(sem("prompt_state_ready"), 1)
                    if 13 <= t < 21:
                        b = t - 13
                        act.wait_ge(sem("h0_turned"), g * 8 + (b + 1))
                        copy(h0t[:, b % 2, :], (s3 if b % 2 == 0 else s1)[:, :]).then_inc(sem("h0t_copied"), 1)
                    if t == 24:
                        act.wait_ge(sem("y_gated"), g + 1)
                        act.wait_ge(multiplied, chunk_at(g, 8)) if not (isinstance(g, int) and g == 0) else None
                        for i in range(4):
                            copy(y_hi[:, i, :], yb[:, i, :], scale=gnv[:, 0, i:i + 1]).then_inc(sem("y_rounded"), 1)
                if conv:
                    if t == 5:
                        act.wait_ge(sem("history_turned"), n + 1)
                        wait(act, "conv_in_ready", n * 6)
                        copy(hist[:, :, :], s0[:, 0:144].rearrange("p (k b) -> p k b", k=6)).then_inc(sem("history_ready"), 1)
                        act.wait_ge(sem("history_ready"), n + 1)
                    for j in range(3):
                        if t in (12 + 4 * j, 13 + 4 * j):
                            conv_in(2 * j + t % 4, n, chunk_at(g, 11 + 4 * j), par)
                        if t in (14 + 4 * j, 15 + 4 * j):
                            conv_tanh(2 * j + t % 4 - 2, n)
                    if t in (24, 25):
                        z_tanh(t - 24, n, chunk_at(g, 23), par)
                    if t == 26:
                        act.wait_ge(sem("conv_rows_turned"), n + 1)
                        wait(act, "conv_stored", n * 96)
                        copy(cout[:, 0:512], s2[0:27, :])
                        copy(cout[:, 512:768], s3[0:27, 0:256]).then_inc(sem("conv_rows_ready"), 1)

            for c in range(4):
                if c < LEAD:
                    split(c, 0, c, 512)
            for t in range(4):
                split(t + LEAD, (t + LEAD) // 4, (t + LEAD) % 4, 512 if t == 0 else 1024)
            side_work(5, -1, 1, False, True)
            act.wait_ge(multiplied, 4)
            copy(dtT[:, :], acc[0][0:HEADS, 0:T]).then_inc(sem("dt_copied"), 1)
            act.wait_ge(sem("dt_biased"), 1)
            nc.scalar.activation(dw[:, 1, :], dw[:, 0, :], ACT.Abs).then_inc(sem("dt_act"), 1)
            act.wait_ge(sem("dt_act"), 1)
            nc.scalar.activation(dw[:, 2, :], dw[:, 1, :], ACT.Exp, scale=-1.0).then_inc(sem("dt_act"), 1)
            nc.scalar.activation(rowv[:, 1, :], rowv[:, 1, :], ACT.Exp).then_inc(sem("a_exp"), 1)
            act.wait_ge(sem("dt_u"), 1)
            nc.scalar.activation(dw[:, 4, :], dw[:, 3, :], ACT.Ln).then_inc(sem("dt_act"), 1)
            act.wait_ge(sem("dec_raw"), 1)
            nc.scalar.activation(tokv[:, DEC:CDEC + 1, :], tokv[:, DEC:CDEC + 1, :], ACT.Exp).then_inc(sem("dec_ready"), 1)
            for t in range(8, 28):
                split_at(-1, t)
                side_work(t, -1, 1, False, True)
            for t in range(28):
                if t >= 8:
                    split_at(0, t)
                side_work(t, 0, 0, True, True)

            def iteration(g, par):
                for t in range(28):
                    split_at(g, t)
                    side_work(t, g, par, True, True)

            with act.Fori(0, 3) as i:
                iteration(i * 2 + 1, 1)
                iteration(i * 2 + 2, 0)

            def u_copy(k, m):
                act.wait_ge(multiplied, chunk_at(7, 8) + 4 * k + 4)
                if k:
                    act.wait_ge(sem("u_stored"), 16 * k)
                copy(uo[:, m, :].rearrange("p (j k) -> p j k", j=DL),
                     acc[2 * ((7 + 8 + k) % 2) + m][:, 0:T].rearrange("p (k j) -> p j k", j=DL)).then_inc(sem("u_ready"), 1)

            for t in range(40):
                split_at(7, t)
                side_work(t, 7, 1, True, False)
                if t >= 12 and t % 4 < 2:
                    u_copy((t - 12) // 4, t % 4)
            for t in range(8):
                split(C_TAIL + t + LEAD, (C_TAIL + t + LEAD) // 4, (t + LEAD) % 4)
                if t < 2:
                    u_copy(7, t)

            def norm(k, scale, eps):
                act.wait_ge(sem("squares_summed"), k)
                act.activation(rstd[:, :], s0[:, 0:T], ACT.Sqrt, scale=scale, bias=eps1[:, eps:eps + 1]).then_inc(sem("rms_ready"), 1)

            norm(1, 1.0 / D_INNER, 1)

            def splits(k, c0, t):
                act_c = k * 4 + (c0 + t + LEAD)
                split(act_c, k + (c0 + t + LEAD) // 4, (t + LEAD) % 4)

            def gate(k, b, lead=4):
                for t in range(lead):
                    splits(k, C_GATE, t)
                for m in range(2):
                    act.wait_ge(multiplied, k * 4 + (C_GATE + 4))
                    wait(act, "gate_done", k * 2 + (m - 1))
                    nc.scalar.activation(gth[:, m, :], acc[2 * ((113 + b) % 2) + m][:, 0:T], ACT.Tanh, scale=0.5).then_inc(sem("gate_tanh"), 1)

            gate(0, 0)
            gate(1, 1)
            with act.Fori(1, 7) as i:
                gate(i * 2, 0)
                gate(i * 2 + 1, 1)
            gate(14, 0)
            gate(15, 1, lead=1)

            act.wait_ge(*reach("lam_turned", 1))
            copy(lam[:, :, :], s0[:, 0:3 * PAIRS].rearrange("p (k g) -> p k g", k=3)).then_inc(sem("lam_ready"), 1)
            act.wait_ge(*reach("lam_ready", 1))
            nc.scalar.activation(pr5[:, 0, :], lam[:, 2, :], ACT.Exp).then_inc(sem("s5_step"), 1)
            act.wait_ge(*reach("s5_exponents", 1))
            nc.scalar.activation(pr5[:, 3, :], pr5[:, 1, :], ACT.Exp).then_inc(sem("s5_mag"), 1)
            nc.scalar.activation(pr5[:, 6, :], pr5[:, 5, :], ACT.Abs).then_inc(sem("s5_abs"), 1)
            act.wait_ge(*reach("s5_abs", 1))
            nc.scalar.activation(pr5[:, 7, :], pr5[:, 5, :], ACT.Sin).then_inc(sem("s5_sin"), 1)
            nc.scalar.activation(pr5[:, 8, :], pr5[:, 6, :], ACT.Sin, scale=-1.0, bias=eps1[:, 2:3]).then_inc(sem("s5_sin"), 1)
            for k in range(2):
                for h in range(2):
                    act.wait_ge(sem("c_turned"), 2 * k + h + 1)
                    copy(ct5[:, k, 32 * h:32 * h + 32, :], (s2 if h == 0 else s3)[:, :].rearrange("p (g c) -> p g c", c=S5C), scale=(1.0, -1.0)[k]).then_inc(sem("c_ready"), 1)
            for k in range(2):
                act.wait_ge(*reach("s5_states_turned", k + 1))
                copy(st5[:, k, :, 64:72], (s0 if k == 0 else s1)[:, :].rearrange("p (b g) -> p g b", b=DB)).then_inc(sem("s5_states_ready"), 1)

            def s5_pass1(i):
                for k in range(2):
                    act.wait_ge(sem("q_turned"), i * 2 + (k + 1))
                    wait(act, "p_product", i * PB)
                    for h in range(2):
                        copy(pw5[:, k, 4 * h:4 * h + 4, :], (s2 if h == 0 else s3)[:, :].rearrange("p (g m) -> p g m", m=P)).then_inc(sem("p_ready"), 1)

                for p in range(PB):
                    act.wait_ge(sem("p_product"), i * PB + (p + 1))
                    src = acc[p % 4][:, 0:2 * NK].rearrange("p (c k) -> p c k", c=2)
                    copy(st5[:, :, ds(i * PB + p, 1), 1:64].rearrange("p c o k -> p c (o k)"), src[:, :, 0:63])
                    copy(en5[:, :, ds(i * PB + p, 1), :].rearrange("p c o k -> p c (o k)"), src[:, :, 63:72]).then_inc(sem("p_copied"), 1)

            act.wait_ge(sem("s5_zeros"), 9)
            s5_pass1(0)
            with act.Fori(1, 8) as i:
                s5_pass1(i)
            for k in range(3):
                for h in range(2):
                    act.wait_ge(sem("t_shifted"), 2 * k + h + 1)
                    copy(tt5[:, 2 - k, 32 * h:32 * h + 32, :], (acc[h])[:, :].rearrange("p (g c) -> p g c", c=S5C)).then_inc(sem("t_ready"), 1)
            act.wait_ge(sem("t_ready"), 6)
            act.wait_ge(sem("gs_ready"), 8)
            copy(tt5[:, 3, :, :], gs5[:, :, :]).then_inc(sem("t_ready"), 1)
            act.wait_ge(sem("t_ready"), 7)
            act.wait_ge(*reach("s5_bd_zero", 1))
            def s5_out(i):
                wait(act, "y5_product", i * 2)
                for g2 in range(2):
                    r = slice(64 * g2, 64 * g2 + 64)
                    for j in range(DL):
                        last = copy(tbd[r, :, 64 * g2 + 16 * j:64 * g2 + 16 * j + 16], tt5[r, j, ds(i * PB, PB), :])
                last.then_inc(sem("tbd_ready"), 1)
                for h in range(2):
                    act.wait_ge(sem("y5_product"), i * 2 + (h + 1))
                    copy(u2[:, ds(i * PB + 4 * h, 4), :], acc[h][:, 0:4 * NK].rearrange("p (g k) -> p g k", k=NK)).then_inc(sem("s5_y_copied"), 1)

            s5_out(0)
            with act.Fori(1, 8) as i:
                s5_out(i)
            for n in range(5):
                act.wait_ge(*reach("s5_finals_turned", n + 1))
                m = 4 if n < 4 else 2
                copy(fo5[:, 4 * n:4 * n + m, :], acc[n % 4][0:PAIRS, 0:m * P].rearrange("p (b n) -> p b n", n=P)).then_inc(sem("fo_copied"), 1)
            for i in range(KT):
                act.wait_ge(*reach("gelu_arg", i + 1))
                nc.scalar.activation(gt5[:, 2, :], gt5[:, 1, :], ACT.Tanh).then_inc(sem("gelu_tanh"), 1)
                act.wait_ge(*reach("gelu_out", i + 1))
                copy(h_hi[:, i, :], gt5[:, 0, :]).then_inc(sem("v_rounded"), 1)

            for c in range(LEAD):
                split(C_GLU + c, C_GLU // 4, c)

            def glu(k, b):
                for t in range(4):
                    splits(k, C_GLU, t)
                act.wait_ge(multiplied, k * 4 + (C_GLU + 4))
                wait(act, "merged", k - 1)
                nc.scalar.activation(gl[:, b, 0, :], acc[2 * ((129 + b) % 2) + 1][:, 0:T], ACT.Tanh, scale=0.25).then_inc(sem("glu_tanh"), 1)
                act.wait_ge(*reach("glu_summed", k + 1))
                copy(mg_hi[:, ds(k, 1), :].rearrange("p o t -> p (o t)"), gl[:, b, 1, :]).then_inc(sem("glu_rounded"), 1)

            glu(0, 0)
            glu(1, 1)
            with act.Fori(1, 8) as i:
                glu(i * 2, 0)
                glu(i * 2 + 1, 1)

            def squared(k, b, c_last, s_sq, s_sum, sq, base_og):
                for m in range(2):
                    act.wait_ge(multiplied, c_last + 1)
                    wait(act, s_sum, k * 2 + (m - 1))
                    nc.scalar.activation(sq[:, m, :], acc[2 * ((base_og + b) % 2) + m][:, 0:T], ACT.Square).then_inc(sem(s_sq), 1)

            def proj(k, b):
                for t in range(4):
                    splits(k, C_OUT, t)
                squared(k, b, k * 4 + (C_OUT + 3), "m_squared", "m_summed", msq, 145)

            proj(0, 0)
            proj(1, 1)
            with act.Fori(1, 4) as i:
                proj(i * 2, 0)
                proj(i * 2 + 1, 1)
            norm(2, 1.0 / D_MODEL, 1)
            for i in range(KT):
                act.wait_ge(*reach("x1_ready", i + 1))
                wait(act, "x1_summed", i - 1)
                nc.scalar.activation(msq[:, i % 2, :], x1[:, i, :], ACT.Square).then_inc(sem("x1_squared"), 1)
            norm(3, 1.0 / D_MODEL, 0)
            for i in range(KT):
                act.wait_ge(*reach("h2_scaled", i + 1))
                copy(h_hi[:, i, :], msq[:, i % 2, :]).then_inc(sem("h2_rounded"), 1)

            def up(k, b, last=False):
                for t in range(4):
                    n = 1024
                    splits(k, C_UP, t)
                act.wait_ge(multiplied, k * 4 + (C_UP + 4))
                wait(act, "f_split", k - 1)
                nc.scalar.activation(fg[:, b, 0, :], acc[2 * ((153 + b) % 2)][:, 0:T], ACT.Tanh, scale=0.5).then_inc(sem("f_tanh"), 1)
                act.wait_ge(*reach("f_out", k + 1))
                copy(f_hi[:, ds(k, 1), :].rearrange("p o t -> p (o t)"), fg[:, b, 1, :]).then_inc(sem("f_rounded"), 1)

            act.wait_ge(sem("x1_stored"), 16)
            up(0, 0)
            up(1, 1)
            with act.Fori(1, FT // 2) as i:
                up(i * 2, 0)
                up(i * 2 + 1, 1)

            def down(k, b, last=False):
                for t in range(12):
                    tt = t + LEAD
                    if last and tt >= 12:
                        continue
                    n = 1024 if tt % 12 < 8 else 768
                    split(k * 12 + (C_DOWN + tt), k * 3 + (C_DOWN + tt) // 4, tt % 4, n)
                squared(k, b, k * 12 + (C_DOWN + 11), "f_squared", "f_summed", fsq, 197)

            down(0, 0)
            down(1, 1)
            with act.Fori(1, 3) as i:
                down(i * 2, 0)
                down(i * 2 + 1, 1)
            down(6, 0)
            down(7, 1, last=True)
            norm(4, 1.0 / D_MODEL, 1)
            for c, (t0, n) in enumerate(TOK):
                for j in range(4):
                    act.wait_ge(sem("out_turned"), 4 * c + j + 1)
                    copy(on[0:n, c, j * 512:(j + 1) * 512], side[j][0:n, :]).then_inc(sem("out_rows"), 1)

        @block.vector
        def _(dve):
            tt, stt, ts = dve.tensor_tensor, dve.scalar_tensor_tensor, dve.tensor_scalar

            def split(c, slot, n=1024):
                dve.wait_ge(hi_ready, c + 1)
                tt(w_lo[:, slot, 0:n], raw[:, slot, 0:n], w_hi[:, slot, 0:n].bitcast(F32), ALU.subtract).then_inc(lo_ready, 1)

            def split_at(g, t):
                split(chunk_at(g, t) + LEAD, (t + LEAD) % 4)

            dve.wait_ge(sem("vec_turned"), 1)
            vs = sem("vec_ready")
            dve.tensor_copy(vec[:, 0:64], s0[:, 0:64]).then_inc(vs, 1)
            ts(vec[:, 64:304], s0[:, 64:304], 0.5, None, ALU.mult).then_inc(vs, 1)
            dve.tensor_copy(vec[:, 304:352], s0[:, 304:352]).then_inc(vs, 1)
            d2 = rowv[:, 2, :].rearrange("p (i h) -> p i h", h=2)
            dve.tensor_copy(dcol[0:64, :], d2[0:64, :, 0]).then_inc(vs, 1)
            dve.tensor_copy(dcol[64:P, :], d2[64:P, :, 1]).then_inc(vs, 1)
            dve.wait_ge(sem("x_rms"), 2)
            dve.reciprocal(sx[:, 0:2], sx[:, 0:2]).then_inc(sem("x_rstd"), 1)
            dve.reciprocal(sx[0:32, 2:3], sx[0:32, 2:3]).then_inc(sem("x_rstd"), 1)
            dve.wait_ge(vs, 5)
            dve.wait_ge(sem("rstd_copied"), 1)
            for i in range(KT):
                dve.wait_ge(sem("xT_copied"), i + 1)
                stt(hf[:, i % 2, :], xts[:, i % 2, :], vec[:, N_PRE + i:N_PRE + i + 1], rstd[:, :],
                    ALU.mult, ALU.mult).then_inc(sem("h_scaled"), 1)
                dve.wait_ge(sem("h_rounded"), i + 1)
                tt(h_lo[:, i, :], hf[:, i % 2, :], h_hi[:, i, :].bitcast(F32), ALU.subtract).then_inc(sem("h_ready"), 1)

            def conv_taps(k, n):
                b = k % 2
                dve.wait_ge(sem("conv_in_ready"), n * 6 + (k + 1))
                wait(dve, "conv_rows_turned", n)
                dve.tensor_copy(cnew[:, k, 0:3], craw[:, b, SEQ:SEQ + 3])
                row = craw[:, b, SEQ + 3:XR].rearrange("p (b t) -> p b t", t=7)
                dve.tensor_copy(cnew[:, k, 3:27].rearrange("p (b t) -> p b t", t=3), row[:, :, 4:7]).then_inc(sem("conv_rows"), 1)
                dve.wait_ge(sem("conv_tap0"), n * 6 + (k + 1))
                for j in range(1, CW):
                    stt(cacc[:, b, :], craw[:, b, j:j + XO], gcv[:, 1 + j, k:k + 1], cacc[:, b, :],
                        ALU.mult, ALU.add).then_inc(sem("conv_tapped"), 1)
                    dve.wait_ge(sem("conv_tapped"), n * 18 + (3 * k + j))

            def conv_silu(k, n, parn):
                b = k % 2
                dve.wait_ge(sem("conv_tanh"), n * 6 + (k + 1))
                dst = xc[:, parn, k, :]
                stt(dst[:, 0:SEQ], cth[:, b, 0:SEQ], 1.0, cacc[:, b, 0:SEQ], ALU.add, ALU.mult)
                smp = lambda v: v[:, SEQ + 3:XR].rearrange("p (b t) -> p b t", t=7)[:, :, 0:DL]
                th7 = cth[:, b, SEQ + 3:XO]
                stt(dst[:, SEQ:T - DL].rearrange("p (b t) -> p b t", t=DL),
                    cth[:, b, SEQ + 3:SEQ + 52].rearrange("p (b t) -> p b t", t=7)[:, :, 0:DL], 1.0,
                    cacc[:, b, SEQ + 3:SEQ + 52].rearrange("p (b t) -> p b t", t=7)[:, :, 0:DL], ALU.add, ALU.mult)
                stt(dst[:, T - DL:T], cth[:, b, XO - DL:XO], 1.0, cacc[:, b, XO - DL:XO],
                    ALU.add, ALU.mult).then_inc(sem("conv_out"), 1)

            def z_silu(k, n, parn, par):
                dve.wait_ge(sem("z_tanh"), n * 4 + (k + 1))
                stt(zs[:, parn, k, :], th[:, k % 2, :], 1.0, acc_of(par, 11 + k // 2)[k % 2][:, 0:T],
                    ALU.add, ALU.mult).then_inc(sem("z_done"), 1)

            def ya_add(og, m, c_last, pair, count):
                dve.wait_ge(multiplied, c_last + 1)
                v = ya[:, 2 * og + m, :]
                tt(v, acc[2 * pair + m][:, 0:T], v, ALU.add).then_inc(sem("ya_added"), 1)

            def clamp(c, g):
                n, w = TOK[c][1], TOK[c][1]
                if c == 0:
                    dve.wait_ge(sem("acs0_spread"), g + 1)
                if c == 1:
                    dve.wait_ge(sem("acs1_spread"), g + 1)
                if c == 2:
                    dve.wait_ge(sem("es_exp"), g + 1)
                    dve.wait_ge(sem("y0_ready"), g + 1)
                else:
                    wait(dve, "y2_ready" if c == 0 else "y1_ready", g)
                for j in range(HG):
                    src = (s2, s3)[j // 4][0:n, (j % 4) * P:(j % 4) * P + w] if c < 2 else s0[0:n, P + j * w:P + (j + 1) * w]
                    last = ts(seg[0:n, c % 2, j * w:(j + 1) * w], src, gtv[0:n, ACS + c, j:j + 1], 0.0,
                              ALU.subtract, ALU.min)
                last.then_inc(sem("seg_clamped"), 1)

            def mask(c, g):
                n, t0 = TOK[c][1], TOK[c][0]
                dve.wait_ge(sem("seg_exp"), g * 3 + (c + 1))
                v = seg[0:n, c % 2, 0:HG * n].rearrange("s (j q) -> s j q", j=HG)
                tt(v, v, bc(cbm[0:n, t0:t0 + n], HG, 1), ALU.mult).then_inc(sem("m_ready"), 1)

            def by_head(ap):
                return ap.rearrange("s (j p) -> s j p", j=HG)

            def skip(c, bank, g, par):
                t0, n = TOK[c]
                for i in range(4):
                    last = stt(yb[:, i, t0:t0 + n], xc[:, par, 2 + i, t0:t0 + n], gnv[:, 1, i:i + 1],
                               bank[:, i * n:(i + 1) * n], ALU.mult, ALU.add)
                last.then_inc(sem("y_skip"), 1)

            def side_work(t, g, par, ssd, conv):
                n = g + 1
                if ssd:
                    if t == 0:
                        for k in (2, 3):
                            z_silu(k, g, par, 1 - par)
                        wait(dve, "y_split", g * 4)
                        dve.tensor_copy(gtv[:, :, :], tokv[:, :, ds(g * HG, HG)])
                        dve.tensor_copy(gnv[:, 0, :], vec[:, ds(g * 4 + V_NS, 4)])
                        dve.tensor_copy(gnv[:, 1, :], dcol[:, ds(g * 4, 4)]).then_inc(sem("group_vectors"), 1)
                        dve.wait_ge(sem("group_vectors"), g + 1)
                        dve.tensor_copy(by_head(dta1[:, :]), bc(gtv[:, DTA + 1, :], HD, 2))
                        dve.tensor_copy(by_head(dta2[:, :]), bc(gtv[0:32, DTA + 2, :], HD, 2)).then_inc(sem("dta_spread"), 1)
                    if t == 1:
                        dve.wait_ge(sem("cb_ready"), g + 1)
                        tt(cbm[:, 0:SEQ].rearrange("s (c q) -> s c q", c=2), s1[:, 0:SEQ].rearrange("s (c q) -> s c q", c=2),
                           bc(tri[:, :], 2, 1), ALU.mult)
                        tt(cbm[0:32, SEQ:T], s1[0:32, SEQ:T], btri[:, :], ALU.mult).then_inc(sem("cb_masked"), 1)
                        dve.wait_ge(sem("x01_turned"), g + 1)
                        for c in range(2):
                            tt(by_head(xdt[:, c, :]), by_head((s2, s3)[c][:, :]), bc(gtv[:, DT + c, :], HD, 2),
                               ALU.mult).then_inc(sem("xdt_ready"), 1)
                    if t == 2:
                        dve.wait_ge(sem("xdt_ready"), g * 3 + 2)
                        for c in range(2):
                            tt(by_head(xw[:, c, :]), by_head(xdt[:, c, :]), bc(gtv[:, DEC + c, :], HD, 2),
                               ALU.mult).then_inc(sem("xw_ready"), 1)
                        dve.wait_ge(sem("xw_ready"), g * 4 + 2)
                        tt(by_head(xw[:, 3, :]), by_head(xw[:, 0, :]), bc(gtv[:, CDEC, :], HD, 2),
                           ALU.mult).then_inc(sem("xw_ready"), 1)
                    if t == 3:
                        clamp(0, g)
                        dve.wait_ge(sem("x2_turned"), g + 1)
                        tt(by_head(xdt[0:32, 2, :]), by_head(s0[0:32, :]), bc(gtv[0:32, DT + 2, :], HD, 2),
                           ALU.mult).then_inc(sem("xdt_ready"), 1)
                    if t == 4:
                        dve.wait_ge(sem("xdt_ready"), g * 3 + 3)
                        tt(by_head(xw[0:32, 2, :]), by_head(xdt[0:32, 2, :]), bc(gtv[0:32, DEC + 2, :], HD, 2),
                           ALU.mult).then_inc(sem("xw_ready"), 1)
                        dve.wait_ge(sem("btok_ready"), g + 1)
                        tt(bm[:, :, :], bc(btok[0:32, 2, :], DB, 1), bc(bmask[:, :], NS, 2), ALU.mult).then_inc(sem("bm_ready"), 1)
                    if t == 5:
                        mask(0, g)
                        clamp(1, g)
                    if t == 7:
                        mask(1, g)
                        clamp(2, g)
                    if t == 9:
                        dve.wait_ge(sem("y0_ready"), g + 1)
                        wait(dve, "y_summed", g * 4)
                        skip(0, s2, g, par)
                        mask(2, g)
                    if t == 11:
                        dve.wait_ge(sem("off1_ready"), g + 1)
                        tt(offe[:, :].rearrange("p (i q) -> p i q", i=4), s1[:, :].rearrange("p (i q) -> p i q", i=4),
                           ee[:, :, 0:P], ALU.mult).then_inc(sem("off1_scaled"), 1)
                        dve.wait_ge(sem("y1_ready"), g + 1)
                        skip(1, s2, g, par)
                    if t == 12:
                        dve.wait_ge(sem("y_skip"), g * 3 + 2)
                        v = yb[:, :, P:SEQ]
                        tt(v, v, offe[:, :].rearrange("p (i q) -> p i q", i=4), ALU.add).then_inc(sem("off1_added"), 1)
                    if 13 <= t < 21:
                        b = t - 13
                        dve.wait_ge(sem("h0_product"), g * 8 + (b + 1))
                        for i in range(4):
                            q = P + DL * b + DL - 1
                            last = stt(h0[:, b % 4, i, :], h0[:, b % 4, i, :], ee[:, i, q:q + 1],
                                       s2[:, i * P:(i + 1) * P], ALU.mult, ALU.add)
                        last.then_inc(sem("h0_updated"), 1)
                    if t == 21:
                        dve.wait_ge(sem("h0_read"), g * 8 + 8)
                        skip(2, s0, g, par)
                        tt(offe[:, 0:P].rearrange("p (i q) -> p i q", i=4), s0[:, P:2 * P].rearrange("p (i q) -> p i q", i=4),
                           ee[:, :, P:160], ALU.mult).then_inc(sem("off2_scaled"), 1)
                        dve.wait_ge(sem("off2_scaled"), g + 1)
                        dve.wait_ge(sem("y_skip"), g * 3 + 3)
                        v = yb[:, :, SEQ:T]
                        tt(v, v, offe[:, 0:P].rearrange("p (i q) -> p i q", i=4), ALU.add).then_inc(sem("off2_added"), 1)
                    if t == 22:
                        dve.wait_ge(sem("off2_added"), g + 1)
                        dve.wait_ge(sem("off1_added"), g + 1)
                        tt(yb[:, :, :], yb[:, :, :], zs[:, par, :, :], ALU.mult).then_inc(sem("y_gated"), 1)
                    if t == 25:
                        for i in range(4):
                            dve.wait_ge(sem("y_rounded"), g * 4 + (i + 1))
                            stt(y_lo[:, i, :], yb[:, i, :], gnv[:, 0, i:i + 1], y_hi[:, i, :].bitcast(F32),
                                ALU.mult, ALU.subtract).then_inc(sem("y_split"), 1)
                    if not (isinstance(g, int) and g == 0) and 1 <= t < 9:
                        og = t - 1
                        for m in range(2):
                            ya_add(og, m, chunk_at(g, og), (par + og) % 2, None)
                if conv:
                    if t == 11:
                        cv = vec[:, V_CB:V_CB + 240].rearrange("p (k i) -> p k i", k=5)
                        dve.tensor_copy(gcv[:, :, 0:1], cv[:, :, ds(n + 32, 1)])
                        dve.tensor_copy(gcv[:, :, 1:2], cv[:, :, ds(n + 40, 1)])
                        dve.tensor_copy(gcv[:, :, 2:6], cv[:, :, ds(n * 4, 4)]).then_inc(sem("conv_vectors"), 1)
                        dve.wait_ge(sem("conv_vectors"), n + 1)
                    for j in range(3):
                        if t in (13 + 4 * j, 14 + 4 * j):
                            conv_taps(2 * j + (t - 13) % 4, n)
                        if t in (15 + 4 * j, 16 + 4 * j):
                            conv_silu(2 * j + (t - 15) % 4, n, 1 - par)
                    if t in (25, 26):
                        z_silu(t - 25, n, 1 - par, par)

            for c in range(LEAD):
                split(c, c, 512)
            for t in range(4):
                split(t + LEAD, (t + LEAD) % 4, 512 if t == 0 else 1024)
            st = sem("vector_steps")
            step = [0]

            def link(ins):
                step[0] += 1
                ins.then_inc(st, 1)
                dve.wait_ge(st, step[0])

            three = lambda v: v.rearrange("p (c h) -> p c h", c=3)
            link(dve.memset(dw[:, 0, :], 0.0))
            link(dve.memset(tokv[:, :, :], 0.0))
            dve.wait_ge(sem("dt_turned"), 1)
            tt(dw[:, 0, 0:128].rearrange("p (c h) -> p c h", c=2), s1[:, 0:128].rearrange("p (c h) -> p c h", c=2),
               bc(rowv[:, 0, :], 2, 1), ALU.add)
            tt(dw[0:32, 0, 128:192], s1[0:32, 128:192], rowv[0:32, 0, :], ALU.add).then_inc(sem("dt_biased"), 1)
            dve.wait_ge(sem("dt_act"), 2)
            ts(dw[:, 3, :], dw[:, 2, :], 1.0, None, ALU.add).then_inc(sem("dt_u"), 1)
            dve.wait_ge(sem("dt_u"), 1)
            link(ts(dw[:, 5, :], dw[:, 3, :], 1.0, None, ALU.subtract))
            link(ts(dw[:, 6, :], dw[:, 5, :], 1e-30, None, ALU.max))
            link(dve.reciprocal(dw[:, 6, :], dw[:, 6, :]))
            link(tt(dw[:, 6, :], dw[:, 6, :], dw[:, 2, :], ALU.mult))
            link(stt(dw[:, 5, :], dw[:, 5, :], 0.0, dw[:, 2, :], ALU.is_equal, ALU.mult))
            dve.wait_ge(sem("dt_act"), 3)
            link(tt(dw[:, 6, :], dw[:, 6, :], dw[:, 4, :], ALU.mult))
            link(tt(dw[:, 6, :], dw[:, 6, :], dw[:, 5, :], ALU.add))
            link(stt(tokv[:, DT:DT + 3, :], three(dw[:, 0, :]), 0.0, three(dw[:, 6, :]), ALU.max, ALU.add))
            dve.wait_ge(sem("a_exp"), 1)
            stt(tokv[:, DTA:DTA + 3, :], tokv[:, DT:DT + 3, :], -1.0, bc(rowv[:, 1, :], 3, 1),
                ALU.mult, ALU.mult).then_inc(sem("dta_ready"), 1)
            dve.wait_ge(sem("acs_ready"), 1)
            dve.tensor_copy(tokv[:, ACS:ACS + 2, :], s2[:, 0:128].rearrange("p (c h) -> p c h", c=2))
            link(dve.tensor_copy(tokv[0:32, ACS + 2, :], s2[0:32, 128:192]))
            tt(tokv[:, DEC:DEC + 2, :], s3[:, 0:128].rearrange("p (c h) -> p c h", c=2), tokv[:, ACS:ACS + 2, :], ALU.subtract)
            tt(tokv[0:32, DEC + 2, :], s3[0:32, 128:192], tokv[0:32, ACS + 2, :], ALU.subtract)
            dve.tensor_copy(tokv[:, CDEC, :], s3[:, 64:128]).then_inc(sem("dec_raw"), 1)

            for t in range(8, 28):
                split_at(-1, t)
                side_work(t, -1, 1, False, True)
            dve.wait_ge(sem("dec_ready"), 1)
            for s in xT_stored:
                dve.wait_ge(s, 16 * KT // 2)
            for t in range(28):
                if t >= 8:
                    split_at(0, t)
                side_work(t, 0, 0, True, True)

            def iteration(g, par):
                for t in range(28):
                    split_at(g, t)
                    side_work(t, g, par, True, True)

            with dve.Fori(0, 3) as i:
                iteration(i * 2 + 1, 1)
                iteration(i * 2 + 2, 0)
            for t in range(40):
                split_at(7, t)
                side_work(t, 7, 1, True, False)
            for t in range(8):
                split(C_TAIL + t + LEAD, (t + LEAD) % 4)
                if t >= 1:
                    for m in range(2):
                        ya_add(t - 1, m, C_TAIL + t - 1, (105 + t - 1) % 2, None)
            for m in range(2):
                ya_add(7, m, C_TAIL + 7, (105 + 7) % 2, None)

            def norm(k):
                dve.wait_ge(sem("rms_ready"), k)
                dve.reciprocal(rstd[:, :], rstd[:, :]).then_inc(sem("rstd_ready"), 1)
                dve.wait_ge(sem("rstd_ready"), k)

            def splits(k, c0, t):
                split(k * 4 + (c0 + t + LEAD), (t + LEAD) % 4)

            norm(1)
            dve.wait_ge(sem("ya_added"), 16 * NG)
            tt(ya[:, :, :], ya[:, :, :], bc(rstd[:, :], KT, 1), ALU.mult).then_inc(sem("ya_normed"), 1)
            dve.wait_ge(sem("ya_normed"), 1)

            def tile(v, i):
                return v[:, ds(i, 1), :].rearrange("p o t -> p (o t)")

            def gate(k, b, second, lead=4):
                for t in range(lead):
                    splits(k, C_GATE, t)
                for m in range(2):
                    dve.wait_ge(*reach("gate_tanh", k * 2 + (m + 1)))
                    i = k * 2 + m
                    if second:
                        ins = ts(tile(sgb, i - KT), gth[:, m, :], 0.25, 0.25, ALU.mult, ALU.add)
                    else:
                        ins = stt(tile(ya, i), gth[:, m, :], 1.0, tile(ya, i), ALU.add, ALU.mult)
                    ins.then_inc(sem("gate_done"), 1)

            with dve.Fori(0, 4) as i:
                gate(i * 2, 0, False)
                gate(i * 2 + 1, 1, False)
            with dve.Fori(4, 7) as i:
                gate(i * 2, 0, True)
                gate(i * 2 + 1, 1, True)
            gate(14, 0, True)
            gate(15, 1, True, lead=1)

            dve.wait_ge(sem("s5_params_landed"), 16 * 37)
            dve.tensor_copy(ln5[:, 2, :].rearrange("p (g n) -> p g n", g=2), bc(ldt[:, :], S5N, 2)).then_inc(sem("ldt_spread"), 1)
            dve.wait_ge(*reach("s5_step", 1))
            pr = lambda k: pr5[:, k, :]
            link(tt(pr(1), lam[:, 0, :], pr(0), ALU.mult))
            link(tt(pr(2), lam[:, 1, :], pr(0), ALU.mult))
            link(ts(pr(4), pr(2), float(1 / (2 * np.pi)), None, ALU.mult))
            link(ts(pr(4), pr(4), ROUND, None, ALU.add))
            link(ts(pr(4), pr(4), ROUND, None, ALU.subtract))
            link(stt(pr(5), pr(4), -TWO_PI_HI, pr(2), ALU.mult, ALU.add))
            link(stt(pr(5), pr(4), -TWO_PI_LO, pr(5), ALU.mult, ALU.add))
            ts(pr(5), pr(5), PI_IN, -PI_IN, ALU.min, ALU.max).then_inc(sem("s5_exponents"), 1)
            dve.wait_ge(*reach("s5_sin", 2))
            dve.wait_ge(*reach("s5_mag", 1))
            link(tt(pr(9), pr(3), pr(8), ALU.mult))
            link(tt(pr(10), pr(3), pr(7), ALU.mult))
            lr, li, ar, ai = lam[:, 0, :], lam[:, 1, :], pr(9), pr(10)
            link(tt(pr(11), lr, lr, ALU.mult))
            link(tt(pr(0), li, li, ALU.mult))
            link(tt(pr(11), pr(11), pr(0), ALU.add))
            link(dve.reciprocal(pr(11), pr(11)))
            link(stt(pr(12), ar, 1.0, lr, ALU.subtract, ALU.mult))
            link(tt(pr(0), ai, li, ALU.mult))
            link(tt(pr(12), pr(12), pr(0), ALU.add))
            link(tt(pr(12), pr(12), pr(11), ALU.mult))
            link(stt(pr(13), ar, 1.0, li, ALU.subtract, ALU.mult))
            link(tt(pr(0), ai, lr, ALU.mult))
            link(tt(pr(13), pr(0), pr(13), ALU.subtract))
            link(tt(pr(13), pr(13), pr(11), ALU.mult))
            link(dve.memset(pq5[:, 0, 3, :], 1.0))
            link(dve.memset(pq5[:, 1, 3, :], 0.0))
            link(dve.tensor_copy(po5[:, 0, 0, :], ar))
            link(dve.tensor_copy(po5[:, 1, 0, :], ai))
            for k, (x, y) in ((1, (0, 0)), (2, (1, 0)), (3, (1, 1))):
                xr, xi, yr, yi = po5[:, 0, x, :], po5[:, 1, x, :], po5[:, 0, y, :], po5[:, 1, y, :]
                link(tt(pr(0), xr, yr, ALU.mult))
                link(tt(pr(1), xi, yi, ALU.mult))
                link(tt(po5[:, 0, k, :], pr(0), pr(1), ALU.subtract))
                link(tt(pr(0), xr, yi, ALU.mult))
                link(tt(pr(1), xi, yr, ALU.mult))
                link(tt(po5[:, 1, k, :], pr(0), pr(1), ALU.add))
            for k in range(3):
                link(dve.tensor_copy(pq5[:, :, 2 - k, :], po5[:, :, k, :]))
            link(ts(a4x[:, 0, :], po5[:, 1, 3, :], -1.0, None, ALU.mult))
            link(dve.tensor_copy(a4x[:, 1, :], po5[:, 1, 3, :]))
            br, bi = bb5[:, 0], bb5[:, 1]
            t0, t1, t2, t3 = [tt5[:, k] for k in range(4)]
            qr, qi = bc(pr(12), S5C, 2), bc(pr(13), S5C, 2)
            link(tt(t0, br, qr, ALU.mult))
            link(tt(t1, bi, qi, ALU.mult))
            link(tt(t2, bi, qr, ALU.mult))
            link(tt(t3, br, qi, ALU.mult))
            link(tt(br, t0, t1, ALU.subtract))
            tt(bi, t2, t3, ALU.add).then_inc(sem("bbar_ready"), 1)
            dve.wait_ge(*reach("bbar_ready", 1))
            dve.wait_ge(sem("s5_zeros"), 9)
            dve.wait_ge(sem("c_ready"), 4)

            def block_diag(i, src, pows, re_sub, im_rev, s, base):
                xr, xi = [bc(src[:, k, ds(i * PB, PB), :], DL, 2) for k in range(2)]
                qr, qi = [bc(pows[:, k, :, ds(i * PB, PB)].rearrange("x j p -> x p j"), S5C, 3) for k in range(2)]
                v = [tm5[:, k, :].rearrange("x (p j c) -> x p j c", p=PB, j=DL) for k in range(2)]
                n = i * 4
                for part, (x0, q0, x1, q1, op) in enumerate(((xr, qr, xi, qi, re_sub), (xi, qr, xr, qi, im_rev))):
                    tt(v[0], x0, q0, ALU.mult).then_inc(sem(s + "_products"), 1)
                    tt(v[1], x1, q1, ALU.mult).then_inc(sem(s + "_products"), 1)
                    dve.wait_ge(sem(s + "_products"), n + (2 * part + 2))
                    for g2 in range(2):
                        r = slice(64 * g2, 64 * g2 + 64)
                        dst = qbd[r, part, :, 64 * g2:64 * g2 + 64].rearrange("x p (j c) -> x p j c", j=DL)
                        last = tt(dst, v[0][r], v[1][r], op)
                    last.then_inc(sem(s + "_matrices"), 1)
                    dve.wait_ge(sem(s + "_matrices"), i * 2 + (part + 1))

            def q_block(i):
                wait(dve, "g_product", i)
                block_diag(i, bb5, pq5, ALU.subtract, ALU.add, "q", 0)
                dve.wait_ge(sem("g_product"), i + 1)
                dve.tensor_copy(gs5[:, ds(i * PB, PB), :], s0[:, 0:P].rearrange("p (g c) -> p g c", c=S5C)).then_inc(sem("gs_ready"), 1)

            q_block(0)
            with dve.Fori(1, 8) as i:
                q_block(i)
            dve.wait_ge(sem("p_product"), PAIRS)
            dve.memset(tbd[:, :, :], 0.0).then_inc(sem("s5_bd_zero"), 1)
            dve.wait_ge(sem("p_copied"), PAIRS)
            dve.wait_ge(*reach("s5_states_ready", 2))
            col = lambda k: st5[:, :, :, ds(k, 1)].rearrange("p c g o -> p c (g o)")
            scr = [tm5[:, k, 0:128].rearrange("p (c g) -> p c g", c=2) for k in range(2)]
            a4r = bc(po5[:, 0, 3, :], 2, 1)
            with dve.Fori(1, 63) as k:
                now = col(k)
                tt(scr[0], now, a4r, ALU.mult).then_inc(sem("scan_products"), 1)
                tt(scr[1][:, 0], now[:, 1, :], a4x[:, 0, :], ALU.mult)
                tt(scr[1][:, 1], now[:, 0, :], a4x[:, 1, :], ALU.mult).then_inc(sem("scan_products"), 1)
                dve.wait_ge(sem("scan_products"), k * 2)
                tt(scr[0], scr[0], scr[1], ALU.add).then_inc(sem("scan_decayed"), 1)
                dve.wait_ge(sem("scan_decayed"), k)
                tt(col(k + 1), col(k + 1), scr[0], ALU.add).then_inc(sem("scan_stepped"), 1)
                dve.wait_ge(sem("scan_stepped"), k)
            f9 = lambda v: v.rearrange("p g b -> p b g")
            tmf = tm5[:, :, :].rearrange("p k n -> p (k n)")[:, 0:9 * PAIRS].rearrange("p (b g) -> p b g", b=9)
            a4i = bc(po5[:, 1, 3, :], 9, 1)
            a4rr = bc(po5[:, 0, 3, :], 9, 1)
            sre, sim = f9(st5[:, 0, :, 63:72]), f9(st5[:, 1, :, 63:72])
            for part, (x, y, op) in enumerate(((sre, sim, ALU.subtract), (sim, sre, ALU.add))):
                link(tt(fin5[:, part], x, a4rr, ALU.mult))
                link(tt(tmf, y, a4i, ALU.mult))
                link(tt(fin5[:, part], fin5[:, part], tmf, op))
                link(tt(fin5[:, part], fin5[:, part], f9(en5[:, part]), ALU.add))
            dve.drain().then_inc(sem("s5_scanned"), 1)

            def o_block(i):
                wait(dve, "y5_product", i * 2)
                block_diag(i, ct5, po5, ALU.add, ALU.subtract, "o", 0)

            o_block(0)
            with dve.Fori(1, 8) as i:
                o_block(i)
            dve.wait_ge(*reach("ut_landed", 16))
            dve.wait_ge(sem("yt_landed"), 16)
            for i in range(KT):
                y = yt5[:, i, :]
                link(stt(y, ut5[:, i, :], vec[:, V_D5 + i:V_D5 + i + 1], y, ALU.mult, ALU.add))
                link(tt(gt5[:, 1, :], y, y, ALU.mult))
                link(ts(gt5[:, 1, :], gt5[:, 1, :], GELU_C * 0.044715, GELU_C, ALU.mult, ALU.add))
                tt(gt5[:, 1, :], gt5[:, 1, :], y, ALU.mult).then_inc(sem("gelu_arg"), 1)
                dve.wait_ge(*reach("gelu_tanh", i + 1))
                stt(gt5[:, 0, :].rearrange("p (k j) -> p j k", j=DL), gt5[:, 2, :].rearrange("p (j k) -> p j k", j=DL), 1.0,
                    y.rearrange("p (j k) -> p j k", j=DL), ALU.add, ALU.mult).then_inc(sem("gelu_out"), 1)
                dve.wait_ge(*reach("v_rounded", i + 1))
                tt(h_lo[:, i, :], gt5[:, 0, :], h_hi[:, i, :].bitcast(F32), ALU.subtract).then_inc(sem("v_ready"), 1)

            for c in range(LEAD):
                split(C_GLU + c, c)

            def glu(k, b):
                for t in range(4):
                    splits(k, C_GLU, t)
                v = gl[:, b, 1, :]
                dve.wait_ge(*reach("glu_tanh", k + 1))
                stt(v, gl[:, b, 0, :], 1.0, acc[2 * ((129 + b) % 2)][:, 0:T], ALU.add, ALU.mult).then_inc(freed, 1)
                dve.wait_ge(freed, k + 1)
                tt(v, v, tile(sgb, k), ALU.mult).then_inc(sem("glu_gated"), 1)
                dve.wait_ge(*reach("glu_gated", k + 1))
                tt(v, v, tile(ya, k), ALU.add).then_inc(sem("glu_summed"), 1)
                dve.wait_ge(*reach("glu_summed", k + 1))
                dve.wait_ge(*reach("glu_rounded", k + 1))
                tt(tile(mg_lo, k), v, tile(mg_hi, k).bitcast(F32), ALU.subtract).then_inc(sem("merged"), 1)

            with dve.Fori(0, 8) as i:
                glu(i * 2, 0)
                glu(i * 2 + 1, 1)

            dve.memset(sst[:, :], 0.0).then_inc(sem("sst_zero"), 1)

            def summed(k, b, s_sq, s_sum, sq, dst, base_og, prev):
                for m in range(2):
                    dve.wait_ge(*reach(s_sq, k * 2 + (m + 1)))
                    dve.tensor_copy(tile(dst, k * 2 + m), acc[2 * ((base_og + b) % 2) + m][:, 0:T]).then_inc(sem(s_sum + "_copied"), 1)
                    wait(dve, s_sum, k * 2 + m)
                    tt(sst[:, :], sst[:, :], sq[:, m, :], ALU.add).then_inc(sem(s_sum), 1)
                dve.wait_ge(sem(s_sum + "_copied"), k * 2 + 2)
                dve.wait_ge(*reach(s_sum, k * 2 + 2))
                dve.tensor_copy(sx2[:, 0:1], eps1[:, 0:1]).then_inc(freed, 1)

            def proj(k, b):
                for t in range(4):
                    splits(k, C_OUT, t)
                summed(k, b, "m_squared", "m_summed", msq, mt, 145, None)

            dve.wait_ge(sem("sst_zero"), 1)
            proj(0, 0)
            proj(1, 1)
            with dve.Fori(1, 4) as i:
                proj(i * 2, 0)
                proj(i * 2 + 1, 1)
            norm(2)
            dve.memset(sst[:, :], 0.0).then_inc(sem("sst_zero"), 1)
            dve.wait_ge(sem("xT_landed"), 16)
            dve.wait_ge(sem("sst_zero"), 2)
            for i in range(KT):
                stt(mt[:, i, :], mt[:, i, :], vec[:, N_POST + i:N_POST + i + 1], rstd[:, :], ALU.mult, ALU.mult).then_inc(sem("m_normed"), 1)
                dve.wait_ge(*reach("m_normed", i + 1))
                tt(x1[:, i, :], x1[:, i, :], mt[:, i, :], ALU.add).then_inc(sem("x1_ready"), 1)
                if i:
                    dve.wait_ge(sem("x1_squared"), i)
                    wait(dve, "x1_summed", i - 1)
                    tt(sst[:, :], sst[:, :], msq[:, (i - 1) % 2, :], ALU.add).then_inc(sem("x1_summed"), 1)
            dve.wait_ge(sem("x1_squared"), KT)
            dve.wait_ge(sem("x1_summed"), KT - 1)
            tt(sst[:, :], sst[:, :], msq[:, (KT - 1) % 2, :], ALU.add).then_inc(sem("x1_summed"), 1)
            norm(3)
            for i in range(KT):
                if i >= 2:
                    dve.wait_ge(*reach("h2_ready", i - 1))
                stt(msq[:, i % 2, :], x1[:, i, :], vec[:, N_FPRE + i:N_FPRE + i + 1], rstd[:, :],
                    ALU.mult, ALU.mult).then_inc(sem("h2_scaled"), 1)
                dve.wait_ge(*reach("h2_scaled", i + 1))
                dve.wait_ge(*reach("h2_rounded", i + 1))
                tt(h_lo[:, i, :], msq[:, i % 2, :], h_hi[:, i, :].bitcast(F32), ALU.subtract).then_inc(sem("h2_ready"), 1)

            def up(k, b):
                for t in range(4):
                    splits(k, C_UP, t)
                pair = (153 + b) % 2
                v = fg[:, b, 1, :]
                dve.wait_ge(*reach("f_tanh", k + 1))
                stt(v, fg[:, b, 0, :], 1.0, acc[2 * pair][:, 0:T], ALU.add, ALU.mult).then_inc(sem("f_silu"), 1)
                dve.wait_ge(*reach("f_silu", k + 1))
                tt(v, v, acc[2 * pair + 1][:, 0:T], ALU.mult).then_inc(sem("f_out"), 1)
                dve.wait_ge(*reach("f_out", k + 1))
                dve.tensor_copy(sx2[:, 1:2], eps1[:, 0:1]).then_inc(freed, 1)
                dve.wait_ge(*reach("f_rounded", k + 1))
                tt(tile(f_lo, k), v, tile(f_hi, k).bitcast(F32), ALU.subtract).then_inc(sem("f_split"), 1)

            dve.wait_ge(sem("x1_stored"), 16)
            with dve.Fori(0, FT // 2) as i:
                up(i * 2, 0)
                up(i * 2 + 1, 1)

            def down(k, b, last=False):
                for t in range(12):
                    tt_ = t + LEAD
                    if last and tt_ >= 12:
                        continue
                    split(k * 12 + (C_DOWN + tt_), tt_ % 4, 1024 if tt_ % 12 < 8 else 768)
                summed(k, b, "f_squared", "f_summed", fsq, fT, 197, None)

            dve.memset(sst[:, :], 0.0).then_inc(sem("sst_zero"), 1)
            dve.wait_ge(sem("sst_zero"), 3)
            down(0, 0)
            down(1, 1)
            with dve.Fori(1, 3) as i:
                down(i * 2, 0)
                down(i * 2 + 1, 1)
            down(6, 0)
            down(7, 1, last=True)
            norm(4)
            dve.wait_ge(*reach("x1_landed", 16))
            for i in range(KT):
                stt(fT[:, i, :], fT[:, i, :], vec[:, N_FPOST + i:N_FPOST + i + 1], rstd[:, :], ALU.mult, ALU.mult).then_inc(sem("f_normed"), 1)
                dve.wait_ge(sem("f_normed"), i + 1)
                tt(x1r[:, i, :], x1r[:, i, :], fT[:, i, :], ALU.add).then_inc(sem("y_ready"), 1)

        @block.tensor
        def _(pe):
            mm = pe.matmul
            one = dict(start=True, stop=True)

            def turn(out, in_):
                k = in_.shape[0]
                return pe.transpose(out, in_, ident[0:k, 0:k])

            def chunk(c, slot, pair, xh, xl, tiles, first, last, width=2 * P):
                pe.wait_ge(lo_ready, c + 1)
                n = len(tiles)
                for i, kt in enumerate(tiles):
                    for m in range(width // P):
                        o_ = acc[2 * pair + m][:, 0:T]
                        at_ = i * width + m * P
                        wh, wl = w_hi[:, slot, at_:at_ + P], w_lo[:, slot, at_:at_ + P]
                        mm(o_, wh, xh[:, kt, :], start=first and i == 0, stop=False)
                        mm(o_, wh, xl[:, kt, :], start=False, stop=False)
                        done = mm(o_, wl, xh[:, kt, :], start=False, stop=last and i == n - 1)
                done.then_inc(multiplied, 1)

            pe.wait_ge(sem("masks_made"), 20)
            pe.wait_ge(sem("params_landed"), 16 * 12)
            for src, n, col in ((2, 112, 0), (0, 96, 112), (1, 96, 208), (3, 48, 304)):
                last = turn(s0[:, col:col + n], vraw[0:n, src, :])
            last.then_inc(sem("vec_turned"), 1)
            pe.wait_ge(sem("x_rstd"), 2)
            for c, (t0, n) in enumerate(TOK):
                last = mm(s3[:, t0:t0 + n], sx[0:n, c:c + 1].to_broadcast([n, P]), ident[0:n, 0:n], **one)
            last.then_inc(sem("x_rstd_spread"), 1)
            for i in range(KT):
                if i >= 4:
                    pe.wait_ge(sem("xT_copied"), i - 3)
                for c, (t0, n) in enumerate(TOK):
                    last = turn(acc[i % 4][:, t0:t0 + n], xnat[0:n, c, i * P:(i + 1) * P])
                last.then_inc(sem("x_turned"), 1)

            def history(n):
                pe.wait_ge(sem("history_landed"), n * 48 + 48)
                for k in range(6):
                    last = mm(s0[:, k * 24:(k + 1) * 24], cst[:, k * P:(k + 1) * P], ident[0:24, 0:24], **one)
                last.then_inc(sem("history_turned"), 1)

            pe.wait_ge(sem("vec_ready"), 3)
            history(0)
            pe.wait_ge(sem("h_ready"), KT)
            for c in range(4):
                chunk(c, c, 0, h_hi, h_lo, range(4 * c, 4 * c + 4), c == 0, c == 3, width=P)
            pe.wait_ge(sem("dt_copied"), 1)
            for c, (t0, n) in enumerate(TOK):
                last = turn(s1[0:n, c * HEADS:(c + 1) * HEADS], dtT[:, t0:t0 + n])
            last.then_inc(sem("dt_turned"), 1)

            def running_sums():
                pe.wait_ge(sem("dta_ready"), 1)
                for c, (t0, n) in enumerate(TOK):
                    dta = tokv[0:n, DTA + c, :]
                    mm(s2[0:n, c * HEADS:(c + 1) * HEADS], tri[:, :] if c < 2 else btri[:, :], dta, **one)
                    last = mm(s3[0:n, c * HEADS:(c + 1) * HEADS], ones[:, :] if c < 2 else bones[:, :], dta, **one)
                last.then_inc(sem("acs_ready"), 1)

            def freed_for(l, g):
                if isinstance(g, int) and g == -1:
                    if l == 9:
                        pe.wait_ge(sem("dt_copied"), 1)
                elif isinstance(g, int) and g == 0:
                    if l == 8:
                        pe.wait_ge(sem("z_done"), 2)
                    if l == 9:
                        pe.wait_ge(sem("z_done"), 4)
                else:
                    if l < 2:
                        pe.wait_ge(sem("z_done"), g * 4 + (2 + 2 * l))
                    elif l < 10:
                        pe.wait_ge(sem("ya_added"), g * 16 + (2 * (l - 1) - 16))
                if l >= 10:
                    if isinstance(g, int) and g == 7:
                        pe.wait_ge(sem("u_ready"), 2 * (l - 9))
                    else:
                        pe.wait_ge(sem("conv_in_ready"), g * 6 + (6 + 2 * (l - 9)))

            def spread(bank, c, g):
                n = TOK[c][1]
                for j in range(HG):
                    lhs = gtv[0:n, DTA + c, j:j + 1].to_broadcast([n, n])
                    if c < 2:
                        last = mm(bank[j // 4][:, (j % 4) * P:(j % 4 + 1) * P], lhs, tri[:, :], **one)
                    else:
                        last = mm(bank[0:n, P + j * n:P + (j + 1) * n], lhs, btri[:, :], **one)
                return last

            def by_feature(bank, c):
                n = TOK[c][1]
                for i in range(4):
                    lhs = (dta1, dta2)[c - 1][0:n, i * P:(i + 1) * P]
                    last = mm(bank[:, i * n:(i + 1) * n], lhs, tri[:, :] if c < 2 else btri[:, :], **one)
                return last

            def within(bank, c, g):
                n = TOK[c][1]
                pe.wait_ge(sem("m_ready"), g * 3 + (c + 1))
                for j in range(HG):
                    r = 64 * (j % 2)
                    last = mm(bank[r:r + 64, (j // 2) * n:(j // 2 + 1) * n], xdt[0:n, c, j * HD:(j + 1) * HD],
                              seg[0:n, c % 2, j * n:(j + 1) * n], **one)
                return last

            def side_work(t, g, par, ssd, conv):
                n = g + 1
                bT, cT = xc[:, par, 0, :], xc[:, par, 1, :]
                if ssd:
                    if t == 0:
                        wait(pe, "off2_scaled", g)
                        wait(pe, "conv_rows_ready", n)
                        pe.wait_ge(sem("conv_out"), g * 6 + 6)
                        for c, (t0, m) in enumerate(TOK):
                            last = turn(s0[0:m, c * P:(c + 1) * P], bT[:, t0:t0 + m])
                        last.then_inc(sem("b_turned"), 1)
                        for c, (t0, m) in enumerate(TOK):
                            last = mm(s1[0:m, t0:t0 + m], bT[:, t0:t0 + m], cT[:, t0:t0 + m], **one)
                        last.then_inc(sem("cb_ready"), 1)
                        for c in range(2):
                            for i in range(4):
                                last = turn((s2, s3)[c][:, i * P:(i + 1) * P], xc[:, par, 2 + i, c * P:(c + 1) * P])
                        last.then_inc(sem("x01_turned"), 1)
                    if t == 2:
                        pe.wait_ge(sem("btok_ready"), g + 1)
                        for i in range(4):
                            last = turn(s0[0:32, i * P:(i + 1) * P], xc[:, par, 2 + i, SEQ:T])
                        last.then_inc(sem("x2_turned"), 1)
                        pe.wait_ge(sem("xdt_ready"), g * 3 + 2)
                        pe.wait_ge(sem("group_vectors"), g + 1)
                        spread((s2, s3), 0, g).then_inc(sem("acs0_spread"), 1)
                    if t == 4:
                        pe.wait_ge(sem("cb_masked"), g + 1)
                        pe.wait_ge(sem("dta_spread"), g + 1)
                        by_feature(s1, 1).then_inc(sem("e1_ready"), 1)
                        pe.wait_ge(sem("seg_clamped"), g * 3 + 1)
                        spread((s2, s3), 1, g).then_inc(sem("acs1_spread"), 1)
                    if t == 6:
                        pe.wait_ge(sem("xdt_ready"), g * 3 + 3)
                        if conv:
                            pe.wait_ge(sem("history_ready"), n + 1)
                        by_feature(s0, 2)
                        spread(s0, 2, g).then_inc(sem("es_ready"), 1)
                        pe.wait_ge(sem("e1_exp"), g + 1)
                        pe.wait_ge(sem("xw_ready"), g * 4 + 4)
                        mm(s1[:, :], btok[:, 0, :], xw[:, 0, :], **one).then_inc(sem("ht_ready"), 1)
                    if t == 7:
                        pe.wait_ge(sem("seg_clamped"), g * 3 + 2)
                        within(s2, 0, g).then_inc(sem("y0_ready"), 1)
                    if t == 8:
                        for i in range(4):
                            v = s3[:, i * P:(i + 1) * P]
                            mm(v, xw[:, 3, i * P:(i + 1) * P], btok[:, 0, :], start=True, stop=False)
                            last = mm(v, xw[:, 1, i * P:(i + 1) * P], btok[:, 1, :], start=False, stop=True)
                        last.then_inc(sem("prompt_state"), 1)
                    if t == 9:
                        pe.wait_ge(sem("ht_copied"), g + 1)
                        for i in range(4):
                            last = mm(s1[:, i * P:(i + 1) * P], ht[:, i * P:(i + 1) * P], cT[:, P:SEQ], **one)
                        last.then_inc(sem("off1_ready"), 1)
                    if t == 10:
                        pe.wait_ge(sem("y_skip"), g * 3 + 1)
                        within(s2, 1, g).then_inc(sem("y1_ready"), 1)
                    if t == 11:
                        pe.wait_ge(sem("es_exp"), g + 1)
                        pe.wait_ge(sem("seg_clamped"), g * 3 + 3)
                        within(s0, 2, g).then_inc(sem("y2_ready"), 1)
                    if 12 <= t < 20:
                        b = t - 12
                        pe.wait_ge(h0_landed[b % 4], g * 32 + 16 * (b // 4 + 1))
                        if b == 0:
                            pe.wait_ge(sem("prompt_state_ready"), g + 1)
                        if b == 1:
                            pe.wait_ge(sem("off1_scaled"), g + 1)
                        if b >= 2:
                            pe.wait_ge(sem("h0t_copied"), g * 8 + (b - 1))
                        for i in range(4):
                            last = turn((s3 if b % 2 == 0 else s1)[:, i * P:(i + 1) * P], h0[:, b % 4, i, :])
                        last.then_inc(sem("h0_turned"), 1)
                        if b == 0:
                            pe.wait_ge(sem("y_skip"), g * 3 + 2)
                            pe.wait_ge(sem("bm_ready"), g + 1)
                        else:
                            pe.wait_ge(sem("h0_updated"), g * 8 + b)
                        for i in range(4):
                            last = mm(s2[:, i * P:(i + 1) * P], xw[0:32, 2, i * P:(i + 1) * P], bm[:, b, :], **one)
                        last.then_inc(sem("h0_product"), 1)
                    if 13 <= t < 21:
                        b = t - 13
                        pe.wait_ge(sem("h0t_copied"), g * 8 + (b + 1))
                        for i in range(4):
                            col = P + 32 * i + DL * b
                            last = mm(s0[:, col:col + DL], h0t[:, b % 2, i * P:(i + 1) * P],
                                      cT[:, SEQ + DL * b:SEQ + DL * b + DL], **one)
                        last.then_inc(sem("h0_read"), 1)
                if conv:
                    if t == 4 and ssd:
                        pe.wait_ge(sem("xdt_ready"), g * 3 + 3)
                        history(n)
                    if t == 25:
                        pe.wait_ge(sem("conv_rows"), n * 6 + 6)
                        if ssd:
                            pe.wait_ge(sem("h0_updated"), g * 8 + 8)
                            pe.wait_ge(sem("h0t_copied"), g * 8 + 7)
                        for k in range(6):
                            bank = s2 if k < 4 else s3
                            last = turn(bank[0:27, (k % 4) * P:(k % 4 + 1) * P], cnew[:, k, :])
                        last.then_inc(sem("conv_rows_turned"), 1)

            def group_chunk(t, g, par):
                l = 8 + (t - 8) // 4
                if t % 4 == 0:
                    freed_for(l, g)
                kc = t % 4
                chunk(chunk_at(g, t), kc, (par + l) % 2, h_hi, h_lo, range(4 * kc, 4 * kc + 4), kc == 0, kc == 3)

            def g2_chunk(t, g, par):
                freed_for(t, g)
                if t == 0:
                    pe.wait_ge(sem("y_split"), g * 4)
                chunk(chunk_at(g, t), t % 4, (par + t) % 2, y_hi, y_lo, range(4), True, True)

            for t in range(8, 28):
                if t == 10:
                    running_sums()
                group_chunk(t, -1, 1)
                side_work(t, -1, 1, False, True)
            for t in range(28):
                if t >= 8:
                    group_chunk(t, 0, 0)
                side_work(t, 0, 0, True, True)

            def iteration(g, par):
                for t in range(28):
                    if t < 8:
                        g2_chunk(t, g, par)
                    else:
                        group_chunk(t, g, par)
                    side_work(t, g, par, True, True)

            with pe.Fori(0, 3) as i:
                iteration(i * 2 + 1, 1)
                iteration(i * 2 + 2, 0)
            for t in range(40):
                if t < 8:
                    g2_chunk(t, 7, 1)
                else:
                    group_chunk(t, 7, 1)
                side_work(t, 7, 1, True, False)
            pe.wait_ge(sem("y_split"), 32)
            for t in range(8):
                if t < 2:
                    pe.wait_ge(sem("u_ready"), 14 + 2 * t)
                else:
                    pe.wait_ge(sem("ya_added"), 112 + 2 * (t - 1))
                chunk(C_TAIL + t, t % 4, (105 + t) % 2, y_hi, y_lo, range(4), True, True)

            def sum_squares():
                mm(s0[:, 0:T], ones[:, :], sst[:, :], **one).then_inc(sem("squares_summed"), 1)

            pe.wait_ge(sem("y_summed"), 4 * NG)
            sum_squares()

            def outgroup(k, c0, pair, xh, xl):
                for kc in range(4):
                    chunk(k * 4 + (c0 + kc), kc, pair, xh, xl, range(4 * kc, 4 * kc + 4), kc == 0, kc == 3)

            def gate(k, b):
                if isinstance(k, int) and k < 2:
                    pe.wait_ge(sem("ya_added"), 126 + 2 * k)
                else:
                    pe.wait_ge(*reach("gate_done", k * 2 - 2))
                outgroup(k, C_GATE, (113 + b) % 2, h_hi, h_lo)

            gate(0, 0)
            gate(1, 1)
            with pe.Fori(1, 8) as i:
                gate(i * 2, 0)
                gate(i * 2 + 1, 1)

            pe.wait_ge(sem("s5_params_landed"), 16 * 37)
            pe.wait_ge(*reach("ldt_spread", 1))
            for k in range(3):
                last = turn(s0[:, k * PAIRS:(k + 1) * PAIRS], ln5[:, k, :])
            last.then_inc(sem("lam_turned"), 1)
            for k in range(2):
                for b in range(8):
                    if k == 1 and b % 4 == 0:
                        pe.wait_ge(sem("c_ready"), b // 4 + 1)
                    last = turn((s2 if b < 4 else s3)[:, (b % 4) * P:(b % 4 + 1) * P], cn5[:, k, b, :])
                    if b % 4 == 3:
                        last.then_inc(sem("c_turned"), 1)
            pe.wait_ge(sem("s5_states_landed"), 32)
            pe.wait_ge(*reach("lam_ready", 1))
            for k in range(2):
                for b in range(DB):
                    last = turn((s0 if k == 0 else s1)[:, b * PAIRS:(b + 1) * PAIRS], sn5[:, k, b, :])
                last.then_inc(sem("s5_states_turned"), 1)
            pe.wait_ge(*reach("gate_done", 32))
            pe.wait_ge(*reach("s5_states_ready", 2))
            pe.wait_ge(*reach("u2_landed", 16 * 8))
            pe.wait_ge(sem("c_ready"), 4)

            def s5_pass1(i):
                for k in range(2):
                    pe.wait_ge(sem("q_matrices"), i * 2 + (k + 1))
                    for p in range(PB):
                        if p % 4 == 0:
                            if not (isinstance(i, int) and i == 0 and k == 0):
                                pe.wait_ge(sem("p_ready"), i * 4 + (2 * k + p // 4 - 1))
                        last = turn((s2 if p < 4 else s3)[:, (p % 4) * P:(p % 4 + 1) * P], qbd[:, k, p, :])
                    last.then_inc(sem("q_turned"), 1)
                wait(pe, "gs_ready", i)
                for p in range(PB):
                    v = s0[:, p * S5C:(p + 1) * S5C]
                    for k in range(2):
                        last = mm(v, qbd[:, k, p, :], ct5[:, k, ds(i * PB + p, 1), :].rearrange("x o c -> x (o c)"),
                                  start=k == 0, stop=k == 1)
                last.then_inc(sem("g_product"), 1)
                for p in range(PB):
                    if p == 0:
                        pe.wait_ge(sem("p_ready"), i * 4 + 4)
                    wait(pe, "p_copied", i * PB + (p - 3))
                    for k in range(2):
                        last = mm(acc[p % 4][:, k * NK:(k + 1) * NK], pw5[:, k, p, :],
                                  u2[:, ds(i * PB + p, 1), :].rearrange("x o c -> x (o c)"), **one)
                    last.then_inc(sem("p_product"), 1)

            s5_pass1(0)
            with pe.Fori(1, 8) as i:
                s5_pass1(i)
            pe.wait_ge(sem("gs_ready"), 8)
            pe.wait_ge(sem("p_copied"), PAIRS)
            for k in range(3):
                for h in range(2):
                    wait(pe, "t_ready", 2 * k + h - 1)
                    mm(acc[h][:, :], sh5[:, k, :], gs5[:, 32 * h:32 * h + 32, :].rearrange("p g c -> p (g c)"),
                       **one).then_inc(sem("t_shifted"), 1)
            pe.wait_ge(sem("t_ready"), 7)
            pe.wait_ge(*reach("s5_scanned", 1))

            def s5_out(i):
                pe.wait_ge(sem("tbd_ready"), i + 1)
                pe.wait_ge(sem("o_matrices"), i * 2 + 2)
                for p in range(PB):
                    if p % 4 == 0:
                        wait(pe, "s5_y_copied", i * 2 + (p // 4 - 1))
                    v = acc[p // 4][:, (p % 4) * NK:(p % 4 + 1) * NK]
                    pair = ds(i * PB + p, 1)
                    mm(v, tbd[:, p, :], u2[:, pair, :].rearrange("x o c -> x (o c)"), start=True, stop=False)
                    mm(v, qbd[:, 0, p, :], st5[:, 0, pair, :].rearrange("x o c -> x (o c)"), start=False, stop=False)
                    last = mm(v, qbd[:, 1, p, :], st5[:, 1, pair, :].rearrange("x o c -> x (o c)"), start=False, stop=True)
                    if p % 4 == 3:
                        last.then_inc(sem("y5_product"), 1)

            s5_out(0)
            with pe.Fori(1, 8) as i:
                s5_out(i)
            pe.wait_ge(sem("s5_y_copied"), 16)
            for n in range(5):
                if n == 4:
                    pe.wait_ge(*reach("fo_copied", 1))
                for m in range(4 if n < 4 else 2):
                    k, b = (4 * n + m) // 9, (4 * n + m) % 9
                    last = turn(acc[n % 4][0:PAIRS, m * P:(m + 1) * P], fin5[:, k, b, :])
                last.then_inc(sem("s5_finals_turned"), 1)

            pe.wait_ge(*reach("v_ready", KT))
            pe.wait_ge(*reach("fo_copied", 5))

            def glu(k, b):
                wait(pe, "acc_freed", k - 1)
                outgroup(k, C_GLU, (129 + b) % 2, h_hi, h_lo)

            glu(0, 0)
            glu(1, 1)
            with pe.Fori(1, 8) as i:
                glu(i * 2, 0)
                glu(i * 2 + 1, 1)

            def proj(k, b):
                pe.wait_ge(freed, k + 15)
                outgroup(k, C_OUT, (145 + b) % 2, mg_hi, mg_lo)

            pe.wait_ge(*reach("merged", 16))
            with pe.Fori(0, 4) as i:
                proj(i * 2, 0)
                proj(i * 2 + 1, 1)
            pe.wait_ge(*reach("m_summed", 16))
            sum_squares()
            pe.wait_ge(sem("x1_summed"), 16)
            pe.wait_ge(sem("rms_ready"), 2)
            sum_squares()
            pe.wait_ge(*reach("h2_ready", KT))

            def up(k, b):
                pe.wait_ge(freed, k + 23)
                outgroup(k, C_UP, (153 + b) % 2, h_hi, h_lo)

            with pe.Fori(0, FT // 2) as i:
                up(i * 2, 0)
                up(i * 2 + 1, 1)
            pe.wait_ge(*reach("f_split", FT))

            def down(k, b):
                pe.wait_ge(freed, k + (24 + FT - 1))
                for i in range(12):
                    tiles = range(4 * i, 4 * i + 4) if i < 8 else range(32 + 3 * (i - 8), 35 + 3 * (i - 8))
                    chunk(k * 12 + (C_DOWN + i), i % 4, (197 + b) % 2, f_hi, f_lo, tiles, i == 0, i == 11)

            with pe.Fori(0, 4) as i:
                down(i * 2, 0)
                down(i * 2 + 1, 1)
            pe.wait_ge(*reach("f_summed", 16))
            pe.wait_ge(sem("rms_ready"), 3)
            sum_squares()
            pe.wait_ge(sem("rstd_ready"), 4)
            pe.wait_ge(sem("y_ready"), KT)
            for c, (t0, n) in enumerate(TOK):
                for j in range(4):
                    if c:
                        pe.wait_ge(sem("out_rows"), 4 * (c - 1) + j + 1)
                    for i in range(4):
                        last = turn(side[j][0:n, i * P:(i + 1) * P], x1r[:, 4 * j + i, t0:t0 + n])
                    last.then_inc(sem("out_turned"), 1)


def kernel(**inputs):
    import numpy as _np
    import concourse.bacc as _bacc
    from concourse.bass_utils import run_bass_kernel_spmd as _run

    nc = _bacc.Bacc("TRN2", target_bir_lowering=False, num_devices=1)
    arrays, a, o = {}, {}, {}
    for name in NAMES:
        x = _np.ascontiguousarray(inputs[name])
        arrays[f"in_{name}_dram"] = x
        a[name] = nc.dram_tensor(f"in_{name}_dram", x.shape, mybir.dt.from_np(x.dtype), kind="ExternalInput").ap()
    for name, shape in OUTS:
        o[name] = nc.dram_tensor(f"out_{name}_dram", shape, F32, kind="ExternalOutput").ap()
    build(nc, a, o)
    r = _run(nc, [arrays], core_ids=[0])
    return tuple(r.results[0][f"out_{name}_dram"] for name, _ in OUTS)
```

```python
from contextlib import ExitStack

import numpy as np

import concourse.bass as bass
from concourse import mybir

F32 = mybir.dt.float32
F32R = mybir.dt.float32r
ALU = mybir.AluOpType
ACT = mybir.ActivationFunctionType
ds = bass.ds

P = 128
D_MODEL = 2048
SEQ = 256
DB = 8
DL = 4
T = SEQ + DB * DL
TOK = [(0, 128), (128, 128), (256, 32)]
D_INNER = 2 * D_MODEL
HD = 64
HEADS = D_INNER // HD
NG = 8
HG = HEADS // NG
NS = 128
CW = 4
CONV_DIM = D_INNER + 2 * NG * NS
S5G = 128
S5N = 64
S5C = 16
D_FF = 5632
EPS = 1e-6
OFF_XBC = D_INNER
OFF_B = OFF_XBC + D_INNER
OFF_DT = OFF_XBC + CONV_DIM
OFF_U = OFF_DT + HEADS
OFF_GA = OFF_U + D_MODEL
OFF_GB = OFF_GA + D_MODEL

KT = D_MODEL // P
RING = 4
LEAD = 3
SPL = 5
FT = D_FF // P
XR = 3 + SEQ + DB * (3 + DL)
XO = XR - 3
PAIRS = S5G // 2
NK = T // DL
PB = 8
TRIPLES = [(0, 3), (3, 3), (6, 2)]
TWO_PI_HI = 6.28125
TWO_PI_LO = float(2 * np.pi - 6.28125)
ROUND = 12582912.0
PI_IN = 3.1415925
GELU_C = float(np.sqrt(2 / np.pi))
GELU_A = 0.044715

C_G0 = 4
C_IT0 = 24
C_IT1 = 44
C_TAIL = C_IT1 + 28 * 7 + 40 - 28
C_GATE = C_TAIL + 8
C_GLU = C_GATE + 64
C_OUT = C_GLU + 64
C_UP = C_OUT + 32
C_DOWN = C_UP + 4 * FT
C_END = C_DOWN + 96
assert C_TAIL == 252 and C_END == 692

SHARED = {
    'lambda_landed': ('history_landed', 48 * 8),
    'gelu_y': ('off1_scaled', 8), 'gelu_squared': ('off1_added', 8),
    'lam_turned': ('vec_turned', 1), 'lam_ready': ('rstd_copied', 1), 'ldt_spread': ('dt_turned', 1),
    's5_step': ('dt_biased', 1), 's5_exponents': ('dt_u', 1), 's5_mag': ('dta_ready', 1),
    's5_abs': ('dec_ready', 1), 's5_sin': ('dt_copied', 1), 's5_scanned': ('acs_ready', 1),
    's5_bd_zero': ('dec_raw', 1), 'bbar_ready': ('a_exp', 1), 'u2_landed': ('x_landed', 48),
    'ut_landed': ('params_landed', 192), 's5_states_turned': ('x_rms', 2), 's5_states_ready': ('x_rstd', 2),
    's5_finals_turned': ('x_squared', 3), 'fo_copied': ('dt_act', 3), 'glu_tanh': ('z_tanh', 32),
    'glu_gated': ('z_done', 32), 'gate_tanh': ('conv_tanh', 48), 'gate_done': ('conv_out', 48),
    'f_tanh': ('conv_tap0', 48), 'f_silu': ('seg_clamped', 24), 'f_out': ('seg_exp', 24),
    'f_rounded': ('m_ready', 24), 'f_split': ('xdt_ready', 24), 'glu_summed': ('b_turned', 8),
    'glu_rounded': ('cb_ready', 8), 'merged': ('x01_turned', 8), 'm_squared': ('x2_turned', 8),
    'm_summed': ('acs0_spread', 8), 'f_squared': ('acs1_spread', 8), 'f_summed': ('e1_ready', 8),
    'm_normed': ('y0_ready', 8), 'x1_ready': ('y1_ready', 8), 'v_rounded': ('h_rounded', 16),
    'v_ready': ('h_ready', 16), 'h2_scaled': ('h_scaled', 16), 'h2_rounded': ('h_rounded', 32),
    'h2_ready': ('h_ready', 32), 'x1_landed': ('xT_landed', 16), 'gelu_arg': ('ht_ready', 8),
    'gelu_tanh': ('ht_copied', 8), 'gelu_out': ('off1_ready', 8),
}

NAMES = ['x_prompt', 'x_sample', 'state_ssm', 'state_conv', 'state_s5_re', 'state_s5_im',
         'norm_mix_pre', 'norm_mix_post', 'norm_ffn_pre', 'norm_ffn_post', 'w_in', 'conv_w', 'conv_b',
         'dt_bias', 'a_log', 'd_ssm', 'norm_ssm', 'w_ssm_out', 's5_lambda_re', 's5_lambda_im',
         's5_log_dt', 's5_b_re', 's5_b_im', 's5_c_re', 's5_c_im', 's5_d', 'w_glu', 'w_out',
         'w_ffn_up', 'w_ffn_down']
OUTS = [('y_prompt', (1, SEQ, D_MODEL)), ('y_sample', (DB, DL, D_MODEL)),
        ('ssm_prompt', (1, 1, HEADS, HD, NS)), ('conv_prompt', (1, 1, CW - 1, CONV_DIM)),
        ('s5_re_prompt', (1, 1, S5G, S5N)), ('s5_im_prompt', (1, 1, S5G, S5N)),
        ('ssm_sample', (1, DB, HEADS, HD, NS)), ('conv_sample', (1, DB, CW - 1, CONV_DIM)),
        ('s5_re_sample', (1, DB, S5G, S5N)), ('s5_im_sample', (1, DB, S5G, S5N))]


def chunk_at(g, t):
    if isinstance(g, int) and g < 1:
        return (C_G0 if g < 0 else C_IT0) + t - 8
    return g * 28 + (C_IT1 - 28 + t)


def quarter(g, t):
    if isinstance(g, int) and g < 1:
        return ((C_G0 if g < 0 else C_IT0) + t - 8) // RING
    return g * 7 + ((C_IT1 - 28) // RING + t // RING)


def build(nc, a, o):
    w_in = a['w_in'][0]
    w_ssm_out = a['w_ssm_out'][0]
    w_glu = a['w_glu'][0]
    w_out = a['w_out'][0]
    w_up = a['w_ffn_up'][0]
    w_down = a['w_ffn_down'][0]

    xT_dram = nc.dram_tensor("xT_scratch", (P, KT * T), F32, kind="Internal").ap()
    x1_dram = nc.dram_tensor("x1_scratch", (P, KT * T), F32, kind="Internal").ap()
    u_dram = nc.dram_tensor("u_scratch", (D_MODEL, DL * NK), F32, kind="Internal").ap()
    y5_dram = nc.dram_tensor("y5_scratch", (D_MODEL, DL * NK), F32, kind="Internal").ap()

    base = 16512
    top = nc.sbuf_usable_end
    used = {}

    def sb(name, shape, dt, at):
        n = 4
        for s in shape[1:]:
            n *= s
        end = (at + n + 31) // 32 * 32
        assert end <= top, (name, end, top)
        used[name] = (at, end)
        return nc.alloc_sbuf_tensor_at(name, list(shape), dt, offset=at), end

    at = base
    ident, at = sb("ident", [P, P], F32, at)
    ones, at = sb("ones", [P, P], F32, at)
    tri, at = sb("tri", [P, P], F32, at)
    btri, at = sb("btri", [32, 32], F32, at)
    bones, at = sb("bones", [32, 32], F32, at)
    bmask, at = sb("bmask", [32, DB], F32, at)
    eps1, at = sb("eps1", [P, 4], F32, at)
    vec, at = sb("vec", [P, 64 + 48 + 192 + 48], F32, at)
    dcol, at = sb("dcol", [P, HEADS // 2], F32, at)
    sx2, at = sb("sx2", [P, 2], F32, at)
    tokv, at = sb("tokv", [P, 13, HEADS], F32, at)
    DT, DTA, ACS, DEC, CDEC = 0, 3, 6, 9, 12
    gtv, at = sb("gtv", [P, 13, HG], F32, at)
    gcv, at = sb("gcv", [P, 5, 6], F32, at)
    gnv, at = sb("gnv", [P, 2, 4], F32, at)
    rstd, at = sb("rstd", [P, T], F32, at)
    sst, at = sb("sst", [P, T], F32, at)
    raw, at = sb("raw", [P, RING, 1024], F32, at)
    ring_raw_at = used["raw"][0]
    w_hi, at = sb("w_hi", [P, RING, 1024], F32R, at)
    w_lo, at = sb("w_lo", [P, RING, 1024], F32R, at)
    h_at = at
    h_hi, at = sb("h_hi", [P, KT, T], F32R, at)
    h_lo, at = sb("h_lo", [P, KT, T], F32R, at)
    free_at = at
    N_PRE, N_POST, N_FPRE, N_FPOST, V_CB, V_CW, V_NS, V_D5 = 0, 16, 32, 48, 64, 112, 304, 336

    ya, at = sb("ya", [P, KT, T], F32, at)
    ya_end = at
    y_hi, at = sb("y_hi", [P, 4, T], F32R, at)
    y_lo, at = sb("y_lo", [P, 4, T], F32R, at)
    craw, at = sb("craw", [P, 2, XR + 1], F32, at)
    cacc, at = sb("cacc", [P, 2, XO], F32, at)
    hist, at = sb("hist", [P, 6, 24], F32, at)
    cnew, at = sb("cnew", [P, 6, 27], F32, at)
    xc, at = sb("xc", [P, 2, 6, T], F32, at)
    zs, at = sb("zs", [P, 2, 4, T], F32, at)
    ssd_at = at
    xdt, at = sb("xdt", [P, 3, 512], F32, at)
    xw, at = sb("xw", [P, 4, 512], F32, at)
    btok, at = sb("btok", [P, 3, NS], F32, at)
    bm, at = sb("bm", [32, DB, NS], F32, at)
    cbm, at = sb("cbm", [P, T], F32, at)
    seg, at = sb("seg", [P, 2, HG * P], F32, at)
    ee, at = sb("ee", [P, 4, 160], F32, at)
    ht, at = sb("ht", [P, 512], F32, at)
    offe, at = sb("offe", [P, 512], F32, at)
    yb, at = sb("yb", [P, 4, T], F32, at)
    h0, at = sb("h0", [P, 4, 4, NS], F32, at)
    h0t, at = sb("h0t", [P, 2, 512], F32, at)
    cst, _ = sb("cst", [24, 768], F32, used["h0t"][0])
    cout, at = sb("cout", [27, 768], F32, at)
    pout, at = sb("pout", [P, 512], F32, at)
    dta2, at = sb("dta2", [32, 512], F32, at)
    dta1 = offe
    uo, _ = sb("uo", [P, 2, T], F32, used["cacc"][0])
    cth = craw[:, :, 3:3 + XO]
    th = craw[:, :, 3:3 + T]

    at = ssd_at
    xnat, at = sb("xnat", [P, 3, D_MODEL], F32, at)
    xts, at = sb("xts", [P, 3, T], F32, at)
    hf, at = sb("hf", [P, 3, T], F32, at)
    vraw, at = sb("vraw", [P, 4, P], F32, at)
    rowv, at = sb("rowv", [P, 3, HEADS], F32, at)
    dw, at = sb("dw", [P, 7, 3 * HEADS], F32, at)
    sx, at = sb("sx", [P, 4], F32, at)
    dtT, at = sb("dtT", [HEADS, T], F32, at)
    x_sq, _ = sb("x_sq", [P, D_MODEL], F32, h_at)

    sgb, at = sb("sgb", [P, KT, T], F32, ya_end)
    u2, at = sb("u2", [P, PAIRS, NK], F32, at)
    s5_s_at = at
    st5, at = sb("st5", [P, 2, PAIRS, NK], F32, at)
    en5, at = sb("en5", [P, 2, PAIRS, 9], F32, at)
    ct5, at = sb("ct5", [P, 2, PAIRS, S5C], F32, at)
    gs5, at = sb("gs5", [P, PAIRS, S5C], F32, at)
    gth, at = sb("gth", [P, 2, T], F32, at)
    scr5, at = sb("scr5", [P, 2, 2 * PAIRS], F32, at)
    sh5, at = sb("sh5", [P, 3, P], F32, at)
    assert at <= top
    po5, at = sb("po5", [P, 2, DL, PAIRS], F32, used["tokv"][0])
    a4x, at = sb("a4x", [P, 2, PAIRS], F32, at)
    assert at <= used["tokv"][1]
    at = ring_raw_at
    sn5, at = sb("sn5", [PAIRS, 2, DB, P], F32, at)
    ln5, at = sb("ln5", [PAIRS, 3, P], F32, at)
    ldt, at = sb("ldt", [PAIRS, 2], F32, at)
    lam, at = sb("lam", [P, 3, PAIRS], F32, at)
    pr5, at = sb("pr5", [P, 14, PAIRS], F32, at)
    assert at >= ring_raw_at + LEAD * 4096
    cn5, at = sb("cn5", [P, 2, 8, P], F32, at)
    qbd2, _ = sb("qbd2", [P, 2, PB, P], F32, used["cn5"][0])
    qbd, at = sb("qbd", [P, 2, PB, P], F32, at)
    pq5, at = sb("pq5", [P, 2, DL, PAIRS], F32, at)
    tm5, at = sb("tm5", [P, 2, 512], F32, at)
    pw5, at = sb("pw5", [P, 2, PB, P], F32, at)
    assert at <= h_at
    bb5, _ = sb("bb5", [P, 2, PAIRS, S5C], F32, ya_end)
    obd, at = sb("obd", [P, 2, PB, P], F32, h_at)
    obd2, at = sb("obd2", [P, 2, PB, P], F32, at)
    tbd, at = sb("tbd", [P, 2, PB, P], F32, at)
    tmo, at = sb("tmo", [P, 2, 512], F32, at)
    assert at <= free_at
    tt5, at = sb("tt5", [P, DL, PAIRS, S5C], F32, ring_raw_at)
    fin5, at = sb("fin5", [P, 2, 9, PAIRS], F32, at)
    fo5, at = sb("fo5", [PAIRS, 18, P], F32, at)
    yt5, at = sb("yt5", [P, KT, T], F32, at)
    assert at <= h_at
    ut5, _ = sb("ut5", [P, KT, T], F32, s5_s_at)
    ut4, _ = sb("ut4", [P, 4, T], F32, used["gth"][0])
    assert used["ut4"][1] <= used["sh5"][1]
    at = s5_s_at + 2 * KT * T * 4
    gsq, at = sb("gsq", [P, 2, T], F32, at)
    gar, at = sb("gar", [P, 2, T], F32, at)
    gou, at = sb("gou", [P, 2, T], F32, at)

    mg_hi, at = sb("mg_hi", [P, KT, T], F32R, used["u2"][1])
    mg_lo, at = sb("mg_lo", [P, KT, T], F32R, at)
    gl, at = sb("gl", [P, 2, 2, T], F32, at)
    assert at <= top
    mt, at = sb("mt", [P, KT, T], F32, ya_end)
    msq, at = sb("msq", [P, 3, T], F32, at)
    x1, _ = sb("x1", [P, KT, T], F32, used["ya"][0])
    f_hi, at = sb("f_hi", [P, FT, T], F32R, free_at)
    f_lo, at = sb("f_lo", [P, FT, T], F32R, at)
    fg, at = sb("fg", [P, 2, 2, T], F32, at)
    fsq, at = sb("fsq", [P, 2, T], F32, at)
    fT, at = sb("fT", [P, KT, T], F32, h_at)
    x1r, at = sb("x1r", [P, KT, T], F32, at)
    assert at <= free_at
    on, at = sb("on", [P, 3, D_MODEL], F32, free_at)

    with ExitStack() as ctx:
        acc = [ctx.enter_context(nc.psum_tensor(f"acc{i}", [P, 512], F32)) for i in range(4)]
        side = [ctx.enter_context(nc.psum_tensor(f"side{i}", [P, 512], F32)) for i in range(4)]
        s0, s1, s2, s3 = side
        sems = {}

        def sem(name):
            name, _ = SHARED.get(name, (name, 0))
            if name not in sems:
                sems[name] = ctx.enter_context(nc.semaphore(name))
            return sems[name]

        landed = [sem(f"chunk_landed{i}") for i in range(RING)]
        h0_landed = [sem(f"h0_landed{i}") for i in range(4)]
        h0_stored = [sem(f"h0_stored{i}") for i in range(4)]
        xT_stored = [sem(f"xT_stored{i}") for i in range(3)]
        hi_ready = sem("w_hi_ready")
        lo_ready = sem("w_lo_ready")
        multiplied = sem("chunk_multiplied")
        freed = sem("acc_freed")

        def reach(name, v):
            return sem(name), v + SHARED.get(name, (name, 0))[1]

        def wait(eng, name, v):
            if not isinstance(v, int) or v > 0:
                eng.wait_ge(*reach(name, v))

        def bc(ap, n, axis):
            ap = ap.unsqueeze(axis)
            shape = list(ap.shape)
            shape[axis] = n
            return ap.to_broadcast(shape)

        turned = ((s2, s3), (s1, acc[3]))

        def acc_of(par, og):
            k = 2 * ((par + og) % 2)
            return acc[k], acc[k + 1]

        def groups_stored(eng):
            eng.wait_ge(sem("conv_stored"), 96 * NG)
            eng.wait_ge(sem("prompt_state_stored"), 16 * NG)
            for s in h0_stored:
                eng.wait_ge(s, 32 * NG)
            eng.wait_ge(sem("u_stored"), 16 * 8)

        block = ctx.enter_context(nc.Block())

        @block.sync
        def _(sp):
            for c, (t0, n) in enumerate(TOK[:2]):
                sp.dma_start(xnat[:, c, :], a['x_prompt'][0, t0:t0 + n, :]).then_inc(sem("x_landed"), 16)
            sp.dma_start(xnat[0:32, 2, :], a['x_sample'].rearrange("b t d -> (b t) d")).then_inc(sem("x_landed"), 16)

            def load(c, q, slot, src, n=1024, two=False):
                if not isinstance(c, int) or c >= RING:
                    sp.wait_ge(lo_ready, c - (RING - 1))
                dst = raw[:, slot, 0:n]
                if two:
                    dst = dst.rearrange("p (t s n) -> p t s n", t=n // 256, s=2)
                    halves = [(dst[:, :, k, :], src[:, :, k, :]) for k in range(2)]
                else:
                    dst = dst.rearrange("p (t n) -> p t n", n=src.shape[-1])
                    halves = [(dst[:, 0:2], src[:, 0:2]), (dst[:, 2:], src[:, 2:])]
                for to, of in halves:
                    sp.dma_start(to, of).then_inc(landed[slot], 16)

            def rows(w, kc):
                return w[kc * 512:(kc + 1) * 512, :].rearrange("(t p) n -> p t n", p=P)

            def rows2(w, kc):
                return w[kc * 512:(kc + 1) * 512, :].rearrange("(t p) (s n) -> p t s n", p=P, s=2)

            st = a['state_ssm'][0].rearrange("b (g h) p n -> b g (h p) n", g=NG)
            so = o['ssm_sample'][0].rearrange("b (g h) p n -> b g (h p) n", g=NG)
            po = o['ssm_prompt'][0, 0].rearrange("(g h) p n -> g (h p) n", g=NG)
            cs_in = a['state_conv'][0].rearrange("b k c -> (b k) c")
            cs_out = o['conv_sample'][0].rearrange("b k c -> (b k) c")
            cp_out = o['conv_prompt'][0, 0]

            def conv_history(n):
                wait(sp, "history_turned", n)
                wait(sp, "h0_read", n * 8 - 8)
                sp.dma_start(cst[:, 0:P], cs_in[:, ds(n * P + D_INNER, P)]).then_inc(sem("history_landed"), 16)
                sp.dma_start(cst[:, P:2 * P], cs_in[:, ds(n * P + (D_INNER + NG * NS), P)]).then_inc(sem("history_landed"), 16)
                sp.dma_start(cst[:, 2 * P:], cs_in[:, ds(n * 512, 512)]).then_inc(sem("history_landed"), 16)

            def conv_store(n):
                sp.wait_ge(sem("conv_rows_ready"), n + 1)
                for dst, r0, r1 in ((cp_out, 0, 3), (cs_out, 3, 27)):
                    sp.dma_start(dst[:, ds(n * P + D_INNER, P)], cout[r0:r1, 0:P]).then_inc(sem("conv_stored"), 16)
                    sp.dma_start(dst[:, ds(n * P + (D_INNER + NG * NS), P)], cout[r0:r1, P:2 * P]).then_inc(sem("conv_stored"), 16)
                    sp.dma_start(dst[:, ds(n * 512, 512)], cout[r0:r1, 2 * P:]).then_inc(sem("conv_stored"), 16)

            def side_dmas(t, g, ssd, conv):
                if ssd and t == 3:
                    conv_store(g)
                if conv and t == 2:
                    conv_history(g + 1)
                if not ssd:
                    return
                if 6 <= t < 10:
                    b = t - 6
                    if not isinstance(g, int) or g > 0:
                        sp.wait_ge(h0_stored[b], g * 32)
                    sp.dma_start(h0[:, b], st[b, g].rearrange("(i q) n -> q i n", q=P)).then_inc(h0_landed[b], 16)
                if t == 15:
                    sp.wait_ge(sem("prompt_state_ready"), g + 1)
                    sp.dma_start(po[g].rearrange("(i q) n -> q i n", q=P), pout[:, :].rearrange("q (i n) -> q i n", i=4)).then_inc(sem("prompt_state_stored"), 16)
                if 18 <= t < 26:
                    b = t - 18
                    sp.wait_ge(sem("h0_updated"), g * 8 + (b + 1))
                    sp.dma_start(so[b, g].rearrange("(i q) n -> q i n", q=P), h0[:, b % 4]).then_inc(h0_stored[b % 4], 16)
                if 20 <= t < 24:
                    b = t - 16
                    sp.wait_ge(h0_stored[b % 4], g * 32 + 16)
                    sp.dma_start(h0[:, b % 4], st[b, g].rearrange("(i q) n -> q i n", q=P)).then_inc(h0_landed[b % 4], 16)

            def group_chunk(t, g):
                j, kc, n = (t - 8) // 4, (t - 8) % 4, g + 1
                c, q = chunk_at(g, t), quarter(g, t)
                if j == 0:
                    src = w_in[kc * 512:(kc + 1) * 512, OFF_B:OFF_B + 2 * NG * NS].rearrange(
                        "(t p) (s n) -> p t s n", p=P, s=2)[:, :, :, ds(n * P, P)]
                    load(c, q, t % 4, src, two=True)
                else:
                    col = n * 512 + (OFF_XBC + (j - 1) * 256 if j < 3 else (j - 3) * 256)
                    load(c, q, t % 4, rows(w_in, kc)[:, :, ds(col, 256)])

            def g2_chunk(t, c, q, m):
                src = w_ssm_out.rearrange("(g t p) n -> g p t n", t=4, p=P)[m, :, :, t * 256:(t + 1) * 256]
                load(c, q, t % 4, src)

            conv_history(0)
            for c in range(4):
                load(c, 0, c, rows(w_in, c)[:, :, OFF_DT:OFF_DT + P], n=512)
            for t in range(8, 28):
                group_chunk(t, -1)
            for t in range(8, 8 + LEAD):
                group_chunk(t, 0)
            for t in range(28):
                if t >= 8 + LEAD:
                    group_chunk(t, 0)
                side_dmas(t, 0, True, True)

            def iteration(g):
                for t in range(28):
                    if t < 8:
                        g2_chunk(t, chunk_at(g, t), quarter(g, t), g - 1)
                    else:
                        group_chunk(t, g)
                    side_dmas(t, g, True, True)

            with sp.Fori(0, 3) as i:
                iteration(i * 2 + 1)
                iteration(i * 2 + 2)
            def u_store(k):
                sp.wait_ge(sem("u_ready"), 2 * k + 2)
                sp.dma_start(u_dram[k * 256:(k + 1) * 256, :].rearrange("(i p) t -> p i t", p=P), uo[:, :, :]).then_inc(sem("u_stored"), 16)

            for t in range(40):
                c = chunk_at(7, t)
                if t < 8:
                    g2_chunk(t, c, c // 4, 6)
                else:
                    k, kc = (t - 8) // 4, t % 4
                    load(c, c // 4, t % 4, rows(w_in, kc)[:, :, OFF_U + k * 256:OFF_U + (k + 1) * 256])
                side_dmas(t, 7, True, False)
                if t >= 18 and t % 4 == 2:
                    u_store((t - 18) // 4)
            for t in range(8):
                c = C_TAIL + t
                g2_chunk(t, c, c // 4, 7)
                if t % 4 == 2:
                    u_store(6 + t // 4)
            sp.wait_ge(lo_ready, C_GATE)
            for k, nm in enumerate(('s5_lambda_re', 's5_lambda_im')):
                sp.dma_start(ln5[:, k, :], a[nm][0].rearrange("(p g) n -> p (g n)", g=2)).then_inc(sem("lambda_landed"), 16)
            sp.dma_start(ldt[:, :], a['s5_log_dt'][0].rearrange("(p g) -> p g", g=2)).then_inc(sem("lambda_landed"), 16)
            sp.wait_ge(multiplied, C_GATE)
            sp.wait_ge(sem("y_summed"), 4 * NG)
            groups_stored(sp)
            prm = sem("s5_params_landed")
            for k, nm in enumerate(('s5_b_re', 's5_b_im')):
                sp.dma_start(bb5[:, k], a[nm][0].rearrange("(p g) n c -> (g n) p c", g=2)).then_inc(prm, 16)
            for k, nm in enumerate(('s5_c_re', 's5_c_im')):
                v = a[nm][0].rearrange("(b p g) c n -> p g c b n", p=8, g=2)
                for p in range(8):
                    for g2 in range(2):
                        sp.dma_start(cn5[p * 16:(p + 1) * 16, k, :, g2 * S5N:(g2 + 1) * S5N], v[p, g2]).then_inc(prm, 16)
            sp.wait_ge(sem("u_stored"), 16 * 8)
            for g2 in range(2):
                for j in range(4):
                    src = u_dram.rearrange("(p f) (j k) -> f p j k", f=32, j=4)[g2 * 16:(g2 + 1) * 16, :, j, :]
                    r = g2 * 64 + j * 16
                    sp.dma_start(u2[r:r + 16, :, :], src).then_inc(sem("u2_landed"), 16)
            for k, nm in enumerate(('state_s5_re', 'state_s5_im')):
                sp.dma_start(sn5[:, k], a[nm][0].rearrange("b (p g) n -> p b (g n)", g=2)).then_inc(sem("s5_states_landed"), 16)
            sp.wait_ge(*reach("s5_states_turned", 2))
            sp.wait_ge(*reach("bbar_ready", 1))
            for c in range(LEAD):
                load(C_GATE + c, 0, c, rows(w_in, c)[:, :, OFF_GA:OFF_GA + 256])
            sp.wait_ge(sem("p_copied"), 24)
            sp.wait_ge(sem("gs_ready"), 8)
            load(C_GATE + 3, 0, 3, rows(w_in, 3)[:, :, OFF_GA:OFF_GA + 256])
            with sp.Fori(1, 16) as k:
                for kc in range(4):
                    load(k * 4 + (C_GATE + kc), 0, kc, rows(w_in, kc)[:, :, ds(k * 256 + OFF_GA, 256)])
            sp.wait_ge(sem("t_ready"), 7)
            u_tiles = u_dram.rearrange("(i p) t -> p i t", p=P)
            sp.dma_start(ut4[:, :, :], u_tiles[:, 0:4, :]).then_inc(sem("ut_landed"), 16)
            for q in range(4):
                sp.wait_ge(sem("s5_y_copied"), 4 * q + 4)
                if q == 3:
                    sp.wait_ge(*reach("ut_landed", 16))
                    sp.dma_start(ut5[:, 4:, :], u_tiles[:, 4:, :]).then_inc(sem("ut_landed"), 16)
                n = PAIRS // 4
                for g2 in range(2):
                    for j in range(4):
                        dst = y5_dram.rearrange("(p f) (j k) -> f p j k", f=32, j=4)[g2 * 16:(g2 + 1) * 16, q * n:(q + 1) * n, j, :]
                        r = g2 * 64 + j * 16
                        sp.dma_start(dst, u2[r:r + 16, q * n:(q + 1) * n, :]).then_inc(sem("y5_stored"), 16)
                sp.wait_ge(sem("y5_stored"), 16 * 8 * (q + 1))
                wait(sp, "yt_landed", 16 * q)
                sp.dma_start(yt5[:, 4 * q:4 * q + 4, :], y5_dram.rearrange("(i p) t -> p i t", p=P)[:, 4 * q:4 * q + 4, :]).then_inc(sem("yt_landed"), 16)
            sp.wait_ge(*reach("fo_copied", 5))
            for k, (nm, nm2) in enumerate((('s5_re_prompt', 's5_re_sample'), ('s5_im_prompt', 's5_im_sample'))):
                sp.dma_start(o[nm][0, 0].rearrange("(p g) n -> p (g n)", g=2), fo5[:, k * 9, :]).then_inc(sem("s5_finals_stored"), 16)
                sp.dma_start(o[nm2][0].rearrange("b (p g) n -> p b (g n)", g=2), fo5[:, k * 9 + 1:k * 9 + 9, :]).then_inc(sem("s5_finals_stored"), 16)
            sp.wait_ge(sem("s5_finals_stored"), 64)

            with sp.Fori(0, 16) as k:
                for kc in range(4):
                    load(k * 4 + (C_GLU + kc), 0, kc, rows2(w_glu, kc)[:, :, :, ds(k * P, P)], two=True)
            with sp.Fori(0, 8) as k:
                for kc in range(4):
                    load(k * 4 + (C_OUT + kc), 0, kc, rows(w_out, kc)[:, :, ds(k * 256, 256)])
            sp.wait_ge(*reach("merged", 16))
            for k, s in enumerate(xT_stored):
                sp.wait_ge(s, 16 * len(range(k, KT, 3)))
            sp.dma_start(x1[:, :, :], xT_dram.rearrange("p (i t) -> p i t", i=KT)).then_inc(sem("xT_landed"), 16)
            for c in range(4):
                load(C_UP + c, 0, c, rows2(w_up, c)[:, :, :, 0:P], two=True)
            sp.wait_ge(sem("x1_squared"), 16)
            sp.dma_start(x1_dram.rearrange("p (i t) -> p i t", i=KT), x1[:, :, :]).then_inc(sem("x1_stored"), 16)
            with sp.Fori(1, FT) as k:
                for kc in range(4):
                    load(k * 4 + (C_UP + kc), 0, kc, rows2(w_up, kc)[:, :, :, ds(k * P, P)], two=True)

            def down(k, i):
                r0, n = (i * 4, 4) if i < 8 else (32 + (i - 8) * 3, 3)
                src = w_down[r0 * P:(r0 + n) * P, :].rearrange("(t p) n -> p t n", p=P)[:, :, ds(k * 256, 256)]
                load(k * 12 + (C_DOWN + i), 0, i % 4, src, n=n * 256)

            for i in range(12):
                down(0, i)
            sp.wait_ge(sem("x1_stored"), 16)
            sp.wait_ge(multiplied, C_DOWN)
            sp.dma_start(x1r[:, :, :], x1_dram.rearrange("p (i t) -> p i t", i=KT)).then_inc(sem("x1_landed"), 16)
            with sp.Fori(1, 8) as k:
                for i in range(12):
                    down(k, i)
            sp.wait_ge(sem("out_rows"), 12)
            for c, (t0, n) in enumerate(TOK[:2]):
                sp.dma_start(o['y_prompt'][0, t0:t0 + n, :], on[:, c, :]).then_inc(sem("y_stored"), 16)
            sp.dma_start(o['y_sample'].rearrange("b t d -> (b t) d"), on[0:32, 2, :]).then_inc(sem("y_stored"), 16)
            sp.wait_ge(sem("y_stored"), 48)

        @block.gpsimd
        def _(pool):
            made = sem("masks_made")
            for m, v in ((ident, 0.0), (ones, 1.0), (tri, 1.0), (btri, 1.0), (bones, 1.0), (bmask, 1.0), (sh5, None)):
                if v is not None:
                    pool.memset(m[:, :], v).then_inc(made, 1)
            pool.wait_ge(made, 6)
            pool.affine_select(out=ident[:, :], in_=ident[:, :], compare_op=ALU.not_equal, fill=1.0,
                               base=0, pattern=[[-1, P]], channel_multiplier=1).then_inc(made, 1)
            pool.affine_select(out=tri[:, :], in_=tri[:, :], compare_op=ALU.is_ge, fill=0.0,
                               base=0, pattern=[[1, P]], channel_multiplier=-1).then_inc(made, 1)
            pool.affine_select(out=btri[:, :], in_=btri[:, :], compare_op=ALU.is_ge, fill=0.0,
                               base=0, pattern=[[1, 32]], channel_multiplier=-1).then_inc(made, 1)
            pool.affine_select(out=bones[:, :], in_=bones[:, :], compare_op=ALU.is_ge, fill=0.0,
                               base=DL - 1, pattern=[[DL, DB], [0, DL]], channel_multiplier=-1).then_inc(made, 1)
            pool.affine_select(out=bmask[:, :], in_=bmask[:, :], compare_op=ALU.is_ge, fill=0.0,
                               base=DL - 1, pattern=[[DL, DB]], channel_multiplier=-1).then_inc(made, 1)
            pool.wait_ge(made, 11)
            pool.affine_select(out=btri[:, :], in_=btri[:, :], compare_op=ALU.is_ge, fill=0.0,
                               base=0, pattern=[[-DL, DB], [0, DL]], channel_multiplier=1).then_inc(made, 1)
            pool.affine_select(out=bones[:, :], in_=bones[:, :], compare_op=ALU.is_ge, fill=0.0,
                               base=0, pattern=[[-DL, DB], [0, DL]], channel_multiplier=1).then_inc(made, 1)
            pool.affine_select(out=bmask[:, :], in_=bmask[:, :], compare_op=ALU.is_ge, fill=0.0,
                               base=0, pattern=[[-DL, DB]], channel_multiplier=1).then_inc(made, 1)
            pool.memset(eps1[:, 0:1], EPS).then_inc(made, 1)
            pool.memset(eps1[:, 1:2], 4 * EPS).then_inc(made, 1)
            pool.memset(eps1[:, 2:3], float(np.pi / 2)).then_inc(made, 1)
            pool.memset(ya[:, :, :], 0.0).then_inc(made, 1)
            pool.memset(craw[:, :, :], 0.0).then_inc(made, 1)
            pool.memset(sst[:, :], 0.0).then_inc(made, 1)

            def squares(g):
                pool.wait_ge(sem("y_split"), g * 4 + 4)
                pool.tensor_tensor(yb[:, :, :], yb[:, :, :], yb[:, :, :], ALU.mult).then_inc(sem("y_squared"), 1)
                pool.wait_ge(sem("y_squared"), g + 1)
                for i in range(4):
                    wait(pool, "y_summed", g * 4 + i)
                    pool.tensor_tensor(sst[:, :], sst[:, :], yb[:, i, :], ALU.add).then_inc(sem("y_summed"), 1)

            pool.wait_ge(made, 20)
            squares(0)
            with pool.Fori(1, NG) as g:
                squares(g)

            pool.wait_ge(multiplied, C_GATE)
            pool.wait_ge(sem("y_split"), 4 * NG)
            groups_stored(pool)
            z = sem("s5_zeros")
            pool.memset(qbd[:, :, :, :], 0.0).then_inc(z, 1)
            pool.memset(sh5[:, :, :], 0.0).then_inc(z, 1)
            pool.memset(st5[:, :, :, 0:1], 0.0).then_inc(z, 1)
            pool.wait_ge(sem("c_ready"), 4)
            pool.memset(qbd2[:, :, :, :], 0.0).then_inc(z, 1)
            pool.wait_ge(z, 4)
            for k in range(3):
                n = 64 - 16 * (k + 1)
                for r in range(2):
                    v = sh5[:, k, r * 64:r * 64 + n]
                    pool.affine_select(out=v, in_=v, compare_op=ALU.not_equal, fill=1.0,
                                       base=-(r * 64 + 16 * (k + 1)), pattern=[[-1, n]],
                                       channel_multiplier=1).then_inc(z, 1)

            pool.wait_ge(sem("rstd_ready"), 1)
            pool.wait_ge(sem("ya_added"), 16 * NG)
            pool.tensor_tensor(ya[:, :, :], ya[:, :, :], bc(rstd[:, :], KT, 1), ALU.mult).then_inc(sem("ya_normed"), 1)
            pool.wait_ge(multiplied, C_GLU)
            for m in (obd, obd2, tbd):
                pool.memset(m[:, :, :, :], 0.0).then_inc(sem("s5_bd_zero"), 1)
            for i in range(KT):
                pool.wait_ge(*reach("gelu_out", i + 1))
                pool.wait_ge(*reach("v_rounded", i + 1))
                pool.tensor_tensor(h_lo[:, i, :], gou[:, i % 2, :], h_hi[:, i, :].bitcast(F32), ALU.subtract).then_inc(sem("v_ready"), 1)

        @block.scalar
        def _(act):
            copy = lambda out, in_, **k: nc.scalar.activation(out, in_, ACT.Copy, **k)

            pl = sem("params_landed")
            act.dma_start(vraw[0:96, 0, :], a['conv_w'][0, 0:2].rearrange("k (i p) -> (k i) p", p=P)).then_inc(pl, 16)
            act.dma_start(vraw[0:96, 1, :], a['conv_w'][0, 2:4].rearrange("k (i p) -> (k i) p", p=P)).then_inc(pl, 16)
            for k, nm in enumerate(('norm_mix_pre', 'norm_mix_post', 'norm_ffn_pre', 'norm_ffn_post')):
                act.dma_start(vraw[k * 16:(k + 1) * 16, 2, :], a[nm][0].rearrange("(i p) -> i p", p=P)).then_inc(pl, 16)
            act.dma_start(vraw[64:112, 2, :], a['conv_b'][0].rearrange("(i p) -> i p", p=P)).then_inc(pl, 16)
            act.dma_start(vraw[0:32, 3, :], a['norm_ssm'][0].rearrange("(i p) -> i p", p=P)).then_inc(pl, 16)
            act.dma_start(vraw[32:48, 3, :], a['s5_d'][0].rearrange("(i p) -> i p", p=P)).then_inc(pl, 16)
            for k, nm in enumerate(('dt_bias', 'a_log', 'd_ssm')):
                act.dma_start(rowv[:, k, :], a[nm].to_broadcast([P, HEADS])).then_inc(pl, 16)

            act.wait_ge(sem("x_landed"), 48)
            for c, (t0, n) in enumerate(TOK):
                wait(act, "x_squared", c)
                nc.scalar.activation(x_sq[0:n, :], xnat[0:n, c, :], ACT.Square, accum_out=sx[0:n, c:c + 1]).then_inc(sem("x_squared"), 1)
            act.wait_ge(sem("x_squared"), 3)
            act.wait_ge(sem("masks_made"), 20)
            nc.scalar.activation(sx[:, 0:2], sx[:, 0:2], ACT.Sqrt, scale=1.0 / D_MODEL, bias=eps1[:, 0:1]).then_inc(sem("x_rms"), 1)
            nc.scalar.activation(sx[0:32, 2:3], sx[0:32, 2:3], ACT.Sqrt, scale=1.0 / D_MODEL, bias=eps1[0:32, 0:1]).then_inc(sem("x_rms"), 1)
            act.wait_ge(sem("x_rstd_spread"), 1)
            copy(rstd[:, :], s3[:, 0:T]).then_inc(sem("rstd_copied"), 1)
            for i in range(KT):
                act.wait_ge(sem("x_turned"), i + 1)
                if i >= 3:
                    act.wait_ge(xT_stored[i % 3], 16 * (i // 3))
                    act.wait_ge(sem("h_scaled"), i - 2)
                copy(xts[:, i % 3, :], acc[i % 4][:, 0:T]).then_inc(sem("xT_copied"), 1)
                act.wait_ge(sem("xT_copied"), i + 1)
                act.dma_start(xT_dram[:, i * T:(i + 1) * T], xts[:, i % 3, :]).then_inc(xT_stored[i % 3], 16)
                if i:
                    act.wait_ge(sem("h_scaled"), i)
                    copy(h_hi[:, i - 1, :], hf[:, (i - 1) % 3, :]).then_inc(sem("h_rounded"), 1)
            act.wait_ge(sem("h_scaled"), KT)
            copy(h_hi[:, KT - 1, :], hf[:, (KT - 1) % 3, :]).then_inc(sem("h_rounded"), 1)

            def split(c, q, slot, n=1024):
                act.wait_ge(landed[slot], q * 32 + 32)
                if not isinstance(c, int) or c >= RING:
                    act.wait_ge(multiplied, c - (RING - 1))
                copy(w_hi[:, slot, 0:n], raw[:, slot, 0:n]).then_inc(hi_ready, 1)

            def split_at(g, t):
                split(chunk_at(g, t) + LEAD, quarter(g, t + LEAD), (t + LEAD) % 4)

            def conv_in(k, n, c_last, par):
                act.wait_ge(multiplied, c_last + 1)
                wait(act, "conv_tapped", n * 18 + 3 * (k - 1))
                wait(act, "conv_out", n * 6 + (k - 1))
                if k < 2:
                    wait(act, "z_done", n * 4)
                b = k % 2
                src = acc_of(par, 8 + k // 2)[k % 2]
                copy(craw[:, b, 3:3 + SEQ], src[:, 0:SEQ])
                row = craw[:, b, SEQ + 3:XR].rearrange("p (b t) -> p b t", t=7)
                copy(row[:, :, 3:7], src[:, SEQ:T].rearrange("p (b t) -> p b t", t=DL))
                copy(row[:, :, 0:3], hist[:, k, :].rearrange("p (b t) -> p b t", t=3)).then_inc(sem("conv_in_ready"), 1)
                act.wait_ge(sem("conv_in_ready"), n * 6 + (k + 1))
                act.wait_ge(sem("conv_vectors"), n + 1)
                nc.scalar.activation(cacc[:, b, :], craw[:, b, 0:XO], ACT.Identity, bias=gcv[:, 0, k:k + 1],
                                     scale=gcv[:, 1, k:k + 1]).then_inc(sem("conv_tap0"), 1)

            def conv_tanh(k, n):
                act.wait_ge(sem("conv_tapped"), n * 18 + 3 * (k + 1))
                nc.scalar.activation(cth[:, k % 2, :], cacc[:, k % 2, :], ACT.Tanh).then_inc(sem("conv_tanh"), 1)

            def z_tanh(k, n, c_last, par):
                act.wait_ge(multiplied, c_last + 1)
                wait(act, "z_done", n * 4 + (k - 1))
                if k < 2:
                    act.wait_ge(sem("conv_out"), n * 6 + 6)
                nc.scalar.activation(th[:, k % 2, :], acc_of(par, 11 + k // 2)[k % 2][:, 0:T], ACT.Tanh, scale=0.5).then_inc(sem("z_tanh"), 1)

            def seg_exp(c, g):
                act.wait_ge(sem("seg_clamped"), g * 3 + (c + 1))
                v = seg[:, c, :] if c < 2 else seg[0:32, 0, 0:HG * 32]
                nc.scalar.activation(v, v, ACT.Exp).then_inc(sem("seg_exp"), 1)

            def side_work(t, g, par, ssd, conv):
                n = g + 1
                c0 = chunk_at(g, 0)
                if ssd:
                    for k in (2, 3) if t == 0 else ():
                        z_tanh(k, g, c0 - 1 if not (isinstance(g, int) and g == 0) else C_IT0 - 1, 1 - par)
                    if t == 1:
                        act.wait_ge(sem("b_turned"), g + 1)
                        copy(btok[:, 0:2, :], s0[:, 0:256].rearrange("p (c n) -> p c n", c=2))
                        copy(btok[0:32, 2, :], s0[0:32, 256:384]).then_inc(sem("btok_ready"), 1)
                    if t == 4:
                        seg_exp(0, g)
                    if t == 5:
                        act.wait_ge(sem("e1_ready"), g + 1)
                        nc.scalar.activation(ee[:, :, 0:P], s1[:, :].rearrange("p (i q) -> p i q", i=4), ACT.Exp).then_inc(sem("e1_exp"), 1)
                    if t == 6:
                        seg_exp(1, g)
                    if t == 7:
                        act.wait_ge(sem("es_ready"), g + 1)
                        nc.scalar.activation(ee[:, :, P:160], s0[:, 0:P].rearrange("p (i q) -> p i q", i=4), ACT.Exp).then_inc(sem("es_exp"), 1)
                        act.wait_ge(sem("ht_ready"), g + 1)
                        copy(ht[:, :], s1[:, :]).then_inc(sem("ht_copied"), 1)
                    if t == 8:
                        seg_exp(2, g)
                    if t == 9:
                        act.wait_ge(sem("prompt_state"), g + 1)
                        wait(act, "prompt_state_stored", g * 16)
                        copy(pout[:, :], s3[:, :]).then_inc(sem("prompt_state_ready"), 1)
                    if 13 <= t < 21:
                        b = t - 13
                        act.wait_ge(sem("h0_turned"), g * 8 + (b + 1))
                        copy(h0t[:, b % 2, :], (s3 if b % 2 == 0 else s1)[:, :]).then_inc(sem("h0t_copied"), 1)
                    if t == 24:
                        act.wait_ge(sem("y_gated"), g + 1)
                        if not (isinstance(g, int) and g == 0):
                            act.wait_ge(multiplied, chunk_at(g, 8))
                        for i in range(4):
                            copy(y_hi[:, i, :], yb[:, i, :], scale=gnv[:, 0, i:i + 1]).then_inc(sem("y_rounded"), 1)
                if conv:
                    if t == 5:
                        act.wait_ge(sem("history_turned"), n + 1)
                        wait(act, "conv_in_ready", n * 6)
                        copy(hist[:, :, :], s0[:, 0:144].rearrange("p (k b) -> p k b", k=6)).then_inc(sem("history_ready"), 1)
                        act.wait_ge(sem("history_ready"), n + 1)
                    for j in range(3):
                        if t in (12 + 4 * j, 13 + 4 * j):
                            conv_in(2 * j + t % 4, n, chunk_at(g, 11 + 4 * j), par)
                        if t in (14 + 4 * j, 15 + 4 * j):
                            conv_tanh(2 * j + t % 4 - 2, n)
                    if t in (24, 25):
                        z_tanh(t - 24, n, chunk_at(g, 23), par)
                    if t == 26:
                        act.wait_ge(sem("conv_rows_turned"), n + 1)
                        wait(act, "conv_stored", n * 96)
                        copy(cout[:, 0:512], s2[0:27, :])
                        copy(cout[:, 512:768], s3[0:27, 0:256]).then_inc(sem("conv_rows_ready"), 1)

            for c in range(4):
                if c < LEAD:
                    split(c, 0, c, 512)
            for t in range(4):
                split(t + LEAD, (t + LEAD) // 4, (t + LEAD) % 4, 512 if t == 0 else 1024)
            side_work(5, -1, 1, False, True)
            act.wait_ge(multiplied, 4)
            copy(dtT[:, :], acc[0][0:HEADS, 0:T]).then_inc(sem("dt_copied"), 1)
            act.wait_ge(sem("dt_biased"), 1)
            nc.scalar.activation(dw[:, 1, :], dw[:, 0, :], ACT.Abs).then_inc(sem("dt_act"), 1)
            act.wait_ge(sem("dt_act"), 1)
            nc.scalar.activation(dw[:, 2, :], dw[:, 1, :], ACT.Exp, scale=-1.0).then_inc(sem("dt_act"), 1)
            nc.scalar.activation(rowv[:, 1, :], rowv[:, 1, :], ACT.Exp).then_inc(sem("a_exp"), 1)
            act.wait_ge(sem("dt_u"), 1)
            nc.scalar.activation(dw[:, 4, :], dw[:, 3, :], ACT.Ln).then_inc(sem("dt_act"), 1)
            act.wait_ge(sem("dec_raw"), 1)
            nc.scalar.activation(tokv[:, DEC:CDEC + 1, :], tokv[:, DEC:CDEC + 1, :], ACT.Exp).then_inc(sem("dec_ready"), 1)
            for t in range(8, 28):
                split_at(-1, t)
                side_work(t, -1, 1, False, True)
            for t in range(28):
                if t >= 8:
                    split_at(0, t)
                side_work(t, 0, 0, True, True)

            def iteration(g, par):
                for t in range(28):
                    split_at(g, t)
                    side_work(t, g, par, True, True)

            with act.Fori(0, 3) as i:
                iteration(i * 2 + 1, 1)
                iteration(i * 2 + 2, 0)

            def u_copy(k, m):
                act.wait_ge(multiplied, chunk_at(7, 8) + 4 * k + 4)
                if k:
                    act.wait_ge(sem("u_stored"), 16 * k)
                copy(uo[:, m, :].rearrange("p (j k) -> p j k", j=DL),
                     acc[2 * ((7 + 8 + k) % 2) + m][:, 0:T].rearrange("p (k j) -> p j k", j=DL)).then_inc(sem("u_ready"), 1)

            for t in range(40):
                split_at(7, t)
                side_work(t, 7, 1, True, False)
                if t >= 12 and t % 4 < 2:
                    u_copy((t - 12) // 4, t % 4)
            for t in range(8):
                if t + LEAD < 8:
                    split(C_TAIL + t + LEAD, (C_TAIL + t + LEAD) // 4, (t + LEAD) % 4)
                if t < 2:
                    u_copy(7, t)

            def norm(k, scale, eps, summed=None):
                act.wait_ge(*reach(*(summed or ("squares_summed", min(k, 3)))))
                act.activation(rstd[:, :], s0[:, 0:T], ACT.Sqrt, scale=scale, bias=eps1[:, eps:eps + 1]).then_inc(sem("rms_ready"), 1)

            norm(1, 1.0 / D_INNER, 1)

            def splits(k, c0, t):
                act_c = k * 4 + (c0 + t + LEAD)
                split(act_c, k + (c0 + t + LEAD) // 4, (t + LEAD) % 4)

            act.wait_ge(*reach("lam_turned", 1))
            copy(lam[:, :, :], s0[:, 0:3 * PAIRS].rearrange("p (k g) -> p k g", k=3)).then_inc(sem("lam_ready"), 1)
            act.wait_ge(*reach("lam_ready", 1))
            nc.scalar.activation(pr5[:, 0, :], lam[:, 2, :], ACT.Exp).then_inc(sem("s5_step"), 1)
            act.wait_ge(*reach("s5_exponents", 1))
            nc.scalar.activation(pr5[:, 3, :], pr5[:, 1, :], ACT.Exp).then_inc(sem("s5_mag"), 1)
            nc.scalar.activation(pr5[:, 6, :], pr5[:, 5, :], ACT.Abs).then_inc(sem("s5_abs"), 1)
            act.wait_ge(*reach("s5_abs", 1))
            nc.scalar.activation(pr5[:, 7, :], pr5[:, 5, :], ACT.Sin).then_inc(sem("s5_sin"), 1)
            nc.scalar.activation(pr5[:, 8, :], pr5[:, 6, :], ACT.Sin, scale=-1.0, bias=eps1[:, 2:3]).then_inc(sem("s5_sin"), 1)
            for k in range(2):
                for h in range(2):
                    act.wait_ge(sem("c_turned"), 2 * k + h + 1)
                    copy(ct5[:, k, 32 * h:32 * h + 32, :], (s2 if h == 0 else s3)[:, :].rearrange("p (g c) -> p g c", c=S5C), scale=(1.0, -1.0)[k]).then_inc(sem("c_ready"), 1)
            act.wait_ge(sem("s5_zeros"), 10)
            for k in range(2):
                act.wait_ge(*reach("s5_states_turned", k + 1))
                copy(st5[:, k, :, 64:72], (s0 if k == 0 else s1)[:, :].rearrange("p (b g) -> p g b", b=DB)).then_inc(sem("s5_states_ready"), 1)

            def s5_pass1(i):
                for k in range(2):
                    act.wait_ge(sem("q_turned"), i * 2 + (k + 1))
                    wait(act, "p_product", i * 3)
                    for h in range(2):
                        copy(pw5[:, k, 4 * h:4 * h + 4, :], turned[k][h][:, :].rearrange("p (g m) -> p g m", m=P)).then_inc(sem("p_ready"), 1)

                for m, (p0, n) in enumerate(TRIPLES):
                    act.wait_ge(sem("p_product"), i * 3 + (m + 1))
                    src = acc[m][:, 0:2 * n * NK].rearrange("p (g c k) -> p c g k", c=2, k=NK)
                    copy(st5[:, :, ds(i * PB + p0, n), 1:64], src[:, :, :, 0:63])
                    copy(en5[:, :, ds(i * PB + p0, n), :], src[:, :, :, 63:72]).then_inc(sem("p_copied"), 1)

            s5_pass1(0)
            with act.Fori(1, 8) as i:
                s5_pass1(i)
            for c in range(LEAD):
                split(C_GATE + c, C_GATE // 4, c)

            def gate(k, b, lead=4):
                for t in range(lead):
                    splits(k, C_GATE, t)
                for m in range(2):
                    act.wait_ge(multiplied, k * 4 + (C_GATE + 4))
                    wait(act, "gate_done", k * 2 + (m - 1))
                    nc.scalar.activation(gth[:, m, :], acc[2 * ((113 + b) % 2) + m][:, 0:T], ACT.Tanh, scale=0.5).then_inc(sem("gate_tanh"), 1)

            gate(0, 0)
            gate(1, 1)
            with act.Fori(1, 7) as i:
                gate(i * 2, 0)
                gate(i * 2 + 1, 1)
            gate(14, 0)
            gate(15, 1, lead=1)

            for k in range(3):
                for h in range(2):
                    act.wait_ge(sem("t_shifted"), 2 * k + h + 1)
                    copy(tt5[:, 2 - k, 32 * h:32 * h + 32, :], (acc[h])[:, :].rearrange("p (g c) -> p g c", c=S5C)).then_inc(sem("t_ready"), 1)
            act.wait_ge(sem("t_ready"), 6)
            act.wait_ge(sem("gs_ready"), 8)
            copy(tt5[:, 3, :, :], gs5[:, :, :]).then_inc(sem("t_ready"), 1)
            act.wait_ge(sem("t_ready"), 7)
            act.wait_ge(*reach("s5_bd_zero", 3))
            def t_block(i, b):
                wait(act, "y5_product", i * 2 - 2)
                for g2 in range(2):
                    r = slice(64 * g2, 64 * g2 + 64)
                    for j in range(DL):
                        last = copy(tbd[r, b, :, 64 * g2 + 16 * j:64 * g2 + 16 * j + 16], tt5[r, j, ds(i * PB, PB), :])
                last.then_inc(sem("tbd_ready"), 1)

            def y_out(i, b):
                for h in range(2):
                    act.wait_ge(sem("y5_product"), i * 2 + (h + 1))
                    copy(u2[:, ds(i * PB + 4 * h, 4), :], acc[2 * b + h][:, 0:4 * NK].rearrange("p (g k) -> p g k", k=NK)).then_inc(sem("s5_y_copied"), 1)

            t_block(0, 0)
            t_block(1, 1)
            for n in range(5):
                act.wait_ge(*reach("s5_finals_turned", n + 1))
                m = 4 if n < 4 else 2
                copy(fo5[:, 4 * n:4 * n + m, :], side[n % 4][0:PAIRS, 0:m * P].rearrange("p (b n) -> p b n", n=P)).then_inc(sem("fo_copied"), 1)
            y_out(0, 0)
            with act.Fori(1, 4) as i:
                t_block(i * 2, 0)
                y_out(i * 2 - 1, 1)
                t_block(i * 2 + 1, 1)
                y_out(i * 2, 0)
            y_out(7, 1)
            for i in range(KT + 2):
                if i < KT:
                    act.wait_ge(*reach("gelu_y", i + 1))
                    wait(act, "gelu_arg", i - 1)
                    nc.scalar.activation(gsq[:, i % 2, :], yt5[:, i, :], ACT.Square).then_inc(sem("gelu_squared"), 1)
                if 1 <= i <= KT:
                    act.wait_ge(*reach("gelu_arg", i))
                    nc.scalar.activation(gar[:, (i - 1) % 2, :], gar[:, (i - 1) % 2, :], ACT.Tanh, scale=GELU_C * GELU_A).then_inc(sem("gelu_tanh"), 1)
                if i >= 2:
                    act.wait_ge(*reach("gelu_out", i - 1))
                    copy(h_hi[:, i - 2, :], gou[:, (i - 2) % 2, :]).then_inc(sem("v_rounded"), 1)

            for c in range(LEAD):
                split(C_GLU + c, C_GLU // 4, c)

            def glu(k, b):
                for t in range(4):
                    splits(k, C_GLU, t)
                act.wait_ge(multiplied, k * 4 + (C_GLU + 4))
                wait(act, "merged", k - 1)
                nc.scalar.activation(gl[:, b, 0, :], acc[2 * ((129 + b) % 2) + 1][:, 0:T], ACT.Tanh, scale=0.25).then_inc(sem("glu_tanh"), 1)
                act.wait_ge(*reach("glu_summed", k + 1))
                copy(mg_hi[:, ds(k, 1), :].rearrange("p o t -> p (o t)"), gl[:, b, 1, :]).then_inc(sem("glu_rounded"), 1)

            glu(0, 0)
            glu(1, 1)
            with act.Fori(1, 8) as i:
                glu(i * 2, 0)
                glu(i * 2 + 1, 1)

            def squared(k, b, c_last, s_sq, s_sum, sq, base_og):
                for m in range(2):
                    act.wait_ge(multiplied, c_last + 1)
                    wait(act, s_sum, k * 2 + (m - 1))
                    nc.scalar.activation(sq[:, m, :], acc[2 * ((base_og + b) % 2) + m][:, 0:T], ACT.Square).then_inc(sem(s_sq), 1)

            def proj(k, b):
                for t in range(4):
                    splits(k, C_OUT, t)
                squared(k, b, k * 4 + (C_OUT + 3), "m_squared", "m_summed", msq, 145)

            proj(0, 0)
            proj(1, 1)
            with act.Fori(1, 4) as i:
                proj(i * 2, 0)
                proj(i * 2 + 1, 1)
            norm(2, 1.0 / D_MODEL, 1)
            for i in range(KT):
                act.wait_ge(*reach("x1_ready", i + 1))
                wait(act, "x1_summed", i - 1)
                nc.scalar.activation(msq[:, i % 2, :], x1[:, i, :], ACT.Square).then_inc(sem("x1_squared"), 1)
            norm(3, 1.0 / D_MODEL, 0, summed=("x1_summed", KT))
            for i in range(KT):
                act.wait_ge(*reach("h2_scaled", i + 1))
                copy(h_hi[:, i, :], msq[:, i % 3, :]).then_inc(sem("h2_rounded"), 1)

            def up(k, b, last=False):
                for t in range(4):
                    splits(k, C_UP, t)
                act.wait_ge(multiplied, k * 4 + (C_UP + 4))
                wait(act, "f_split", k - 1)
                nc.scalar.activation(fg[:, b, 0, :], acc[2 * ((153 + b) % 2)][:, 0:T], ACT.Tanh, scale=0.5).then_inc(sem("f_tanh"), 1)
                act.wait_ge(*reach("f_out", k + 1))
                copy(f_hi[:, ds(k, 1), :].rearrange("p o t -> p (o t)"), fg[:, b, 1, :]).then_inc(sem("f_rounded"), 1)

            act.wait_ge(sem("x1_stored"), 16)
            up(0, 0)
            up(1, 1)
            with act.Fori(1, FT // 2) as i:
                up(i * 2, 0)
                up(i * 2 + 1, 1)

            def down(k, b, last=False):
                for t in range(12):
                    tt = t + LEAD
                    if last and tt >= 12:
                        continue
                    n = 1024 if tt % 12 < 8 else 768
                    split(k * 12 + (C_DOWN + tt), k * 3 + (C_DOWN + tt) // 4, tt % 4, n)
                squared(k, b, k * 12 + (C_DOWN + 11), "f_squared", "f_summed", fsq, 197)

            down(0, 0)
            down(1, 1)
            with act.Fori(1, 3) as i:
                down(i * 2, 0)
                down(i * 2 + 1, 1)
            down(6, 0)
            down(7, 1, last=True)
            norm(4, 1.0 / D_MODEL, 1)
            for c, (t0, n) in enumerate(TOK):
                for j in range(4):
                    act.wait_ge(sem("out_turned"), 4 * c + j + 1)
                    copy(on[0:n, c, j * 512:(j + 1) * 512], side[j][0:n, :]).then_inc(sem("out_rows"), 1)

        @block.vector
        def _(dve):
            tt, stt, ts = dve.tensor_tensor, dve.scalar_tensor_tensor, dve.tensor_scalar

            def split(c, slot, n=1024):
                dve.wait_ge(hi_ready, c + 1)
                tt(w_lo[:, slot, 0:n], raw[:, slot, 0:n], w_hi[:, slot, 0:n].bitcast(F32), ALU.subtract).then_inc(lo_ready, 1)

            def split_at(g, t):
                split(chunk_at(g, t) + LEAD, (t + LEAD) % 4)

            dve.wait_ge(sem("vec_turned"), 1)
            vs = sem("vec_ready")
            dve.tensor_copy(vec[:, 0:64], s0[:, 0:64]).then_inc(vs, 1)
            ts(vec[:, 64:304], s0[:, 64:304], 0.5, None, ALU.mult).then_inc(vs, 1)
            dve.tensor_copy(vec[:, 304:352], s0[:, 304:352]).then_inc(vs, 1)
            d2 = rowv[:, 2, :].rearrange("p (i h) -> p i h", h=2)
            dve.tensor_copy(dcol[0:64, :], d2[0:64, :, 0]).then_inc(vs, 1)
            dve.tensor_copy(dcol[64:P, :], d2[64:P, :, 1]).then_inc(vs, 1)
            dve.wait_ge(sem("x_rms"), 2)
            dve.reciprocal(sx[:, 0:2], sx[:, 0:2]).then_inc(sem("x_rstd"), 1)
            dve.reciprocal(sx[0:32, 2:3], sx[0:32, 2:3]).then_inc(sem("x_rstd"), 1)
            dve.wait_ge(vs, 5)
            dve.wait_ge(sem("rstd_copied"), 1)
            for i in range(KT + 1):
                if i < KT:
                    dve.wait_ge(sem("xT_copied"), i + 1)
                    wait(dve, "h_ready", i - 2)
                    stt(hf[:, i % 3, :], xts[:, i % 3, :], vec[:, N_PRE + i:N_PRE + i + 1], rstd[:, :],
                        ALU.mult, ALU.mult).then_inc(sem("h_scaled"), 1)
                if i >= 1:
                    dve.wait_ge(sem("h_scaled"), i)
                    dve.wait_ge(sem("h_rounded"), i)
                    tt(h_lo[:, i - 1, :], hf[:, (i - 1) % 3, :], h_hi[:, i - 1, :].bitcast(F32), ALU.subtract).then_inc(sem("h_ready"), 1)

            def conv_taps(k, n):
                b = k % 2
                dve.wait_ge(sem("conv_in_ready"), n * 6 + (k + 1))
                wait(dve, "conv_rows_turned", n)
                dve.tensor_copy(cnew[:, k, 0:3], craw[:, b, SEQ:SEQ + 3])
                row = craw[:, b, SEQ + 3:XR].rearrange("p (b t) -> p b t", t=7)
                dve.tensor_copy(cnew[:, k, 3:27].rearrange("p (b t) -> p b t", t=3), row[:, :, 4:7]).then_inc(sem("conv_rows"), 1)
                dve.wait_ge(sem("conv_tap0"), n * 6 + (k + 1))
                for j in range(1, CW):
                    stt(cacc[:, b, :], craw[:, b, j:j + XO], gcv[:, 1 + j, k:k + 1], cacc[:, b, :],
                        ALU.mult, ALU.add).then_inc(sem("conv_tapped"), 1)
                    dve.wait_ge(sem("conv_tapped"), n * 18 + (3 * k + j))

            def conv_silu(k, n, parn):
                b = k % 2
                dve.wait_ge(sem("conv_tanh"), n * 6 + (k + 1))
                dst = xc[:, parn, k, :]
                stt(dst[:, 0:SEQ], cth[:, b, 0:SEQ], 1.0, cacc[:, b, 0:SEQ], ALU.add, ALU.mult)
                smp = lambda v: v[:, SEQ + 3:XR].rearrange("p (b t) -> p b t", t=7)[:, :, 0:DL]
                th7 = cth[:, b, SEQ + 3:XO]
                stt(dst[:, SEQ:T - DL].rearrange("p (b t) -> p b t", t=DL),
                    cth[:, b, SEQ + 3:SEQ + 52].rearrange("p (b t) -> p b t", t=7)[:, :, 0:DL], 1.0,
                    cacc[:, b, SEQ + 3:SEQ + 52].rearrange("p (b t) -> p b t", t=7)[:, :, 0:DL], ALU.add, ALU.mult)
                stt(dst[:, T - DL:T], cth[:, b, XO - DL:XO], 1.0, cacc[:, b, XO - DL:XO],
                    ALU.add, ALU.mult).then_inc(sem("conv_out"), 1)

            def z_silu(k, n, parn, par):
                dve.wait_ge(sem("z_tanh"), n * 4 + (k + 1))
                stt(zs[:, parn, k, :], th[:, k % 2, :], 1.0, acc_of(par, 11 + k // 2)[k % 2][:, 0:T],
                    ALU.add, ALU.mult).then_inc(sem("z_done"), 1)

            def ya_add(og, m, c_last, pair):
                dve.wait_ge(multiplied, c_last + 1)
                v = ya[:, 2 * og + m, :]
                tt(v, acc[2 * pair + m][:, 0:T], v, ALU.add).then_inc(sem("ya_added"), 1)

            def clamp(c, g):
                n, w = TOK[c][1], TOK[c][1]
                if c == 0:
                    dve.wait_ge(sem("acs0_spread"), g + 1)
                if c == 1:
                    dve.wait_ge(sem("acs1_spread"), g + 1)
                if c == 2:
                    dve.wait_ge(sem("es_exp"), g + 1)
                    dve.wait_ge(sem("y0_ready"), g + 1)
                else:
                    wait(dve, "y2_ready" if c == 0 else "y1_ready", g)
                for j in range(HG):
                    src = (s2, s3)[j // 4][0:n, (j % 4) * P:(j % 4) * P + w] if c < 2 else s0[0:n, P + j * w:P + (j + 1) * w]
                    last = ts(seg[0:n, c % 2, j * w:(j + 1) * w], src, gtv[0:n, ACS + c, j:j + 1], 0.0,
                              ALU.subtract, ALU.min)
                last.then_inc(sem("seg_clamped"), 1)

            def mask(c, g):
                n, t0 = TOK[c][1], TOK[c][0]
                dve.wait_ge(sem("seg_exp"), g * 3 + (c + 1))
                v = seg[0:n, c % 2, 0:HG * n].rearrange("s (j q) -> s j q", j=HG)
                tt(v, v, bc(cbm[0:n, t0:t0 + n], HG, 1), ALU.mult).then_inc(sem("m_ready"), 1)

            def by_head(ap):
                return ap.rearrange("s (j p) -> s j p", j=HG)

            def skip(c, bank, g, par):
                t0, n = TOK[c]
                for i in range(4):
                    last = stt(yb[:, i, t0:t0 + n], xc[:, par, 2 + i, t0:t0 + n], gnv[:, 1, i:i + 1],
                               bank[:, i * n:(i + 1) * n], ALU.mult, ALU.add)
                last.then_inc(sem("y_skip"), 1)

            def side_work(t, g, par, ssd, conv):
                n = g + 1
                if ssd:
                    if t == 0:
                        for k in (2, 3):
                            z_silu(k, g, par, 1 - par)
                        wait(dve, "y_split", g * 4)
                        dve.tensor_copy(gtv[:, :, :], tokv[:, :, ds(g * HG, HG)])
                        dve.tensor_copy(gnv[:, 0, :], vec[:, ds(g * 4 + V_NS, 4)])
                        dve.tensor_copy(gnv[:, 1, :], dcol[:, ds(g * 4, 4)]).then_inc(sem("group_vectors"), 1)
                        dve.wait_ge(sem("group_vectors"), g + 1)
                        dve.tensor_copy(by_head(dta1[:, :]), bc(gtv[:, DTA + 1, :], HD, 2))
                        dve.tensor_copy(by_head(dta2[:, :]), bc(gtv[0:32, DTA + 2, :], HD, 2)).then_inc(sem("dta_spread"), 1)
                    if t == 1:
                        dve.wait_ge(sem("cb_ready"), g + 1)
                        tt(cbm[:, 0:SEQ].rearrange("s (c q) -> s c q", c=2), s1[:, 0:SEQ].rearrange("s (c q) -> s c q", c=2),
                           bc(tri[:, :], 2, 1), ALU.mult)
                        tt(cbm[0:32, SEQ:T], s1[0:32, SEQ:T], btri[:, :], ALU.mult).then_inc(sem("cb_masked"), 1)
                        dve.wait_ge(sem("x01_turned"), g + 1)
                        for c in range(2):
                            tt(by_head(xdt[:, c, :]), by_head((s2, s3)[c][:, :]), bc(gtv[:, DT + c, :], HD, 2),
                               ALU.mult).then_inc(sem("xdt_ready"), 1)
                    if t == 2:
                        dve.wait_ge(sem("xdt_ready"), g * 3 + 2)
                        for c in range(2):
                            tt(by_head(xw[:, c, :]), by_head(xdt[:, c, :]), bc(gtv[:, DEC + c, :], HD, 2),
                               ALU.mult).then_inc(sem("xw_ready"), 1)
                        dve.wait_ge(sem("xw_ready"), g * 4 + 2)
                        tt(by_head(xw[:, 3, :]), by_head(xw[:, 0, :]), bc(gtv[:, CDEC, :], HD, 2),
                           ALU.mult).then_inc(sem("xw_ready"), 1)
                    if t == 3:
                        clamp(0, g)
                        dve.wait_ge(sem("x2_turned"), g + 1)
                        tt(by_head(xdt[0:32, 2, :]), by_head(s0[0:32, :]), bc(gtv[0:32, DT + 2, :], HD, 2),
                           ALU.mult).then_inc(sem("xdt_ready"), 1)
                    if t == 4:
                        dve.wait_ge(sem("xdt_ready"), g * 3 + 3)
                        tt(by_head(xw[0:32, 2, :]), by_head(xdt[0:32, 2, :]), bc(gtv[0:32, DEC + 2, :], HD, 2),
                           ALU.mult).then_inc(sem("xw_ready"), 1)
                        dve.wait_ge(sem("btok_ready"), g + 1)
                        tt(bm[:, :, :], bc(btok[0:32, 2, :], DB, 1), bc(bmask[:, :], NS, 2), ALU.mult).then_inc(sem("bm_ready"), 1)
                    if t == 5:
                        mask(0, g)
                        clamp(1, g)
                    if t == 7:
                        mask(1, g)
                        clamp(2, g)
                    if t == 9:
                        dve.wait_ge(sem("y0_ready"), g + 1)
                        wait(dve, "y_summed", g * 4)
                        skip(0, s2, g, par)
                        mask(2, g)
                    if t == 11:
                        dve.wait_ge(sem("off1_ready"), g + 1)
                        tt(offe[:, :].rearrange("p (i q) -> p i q", i=4), s1[:, :].rearrange("p (i q) -> p i q", i=4),
                           ee[:, :, 0:P], ALU.mult).then_inc(sem("off1_scaled"), 1)
                        dve.wait_ge(sem("y1_ready"), g + 1)
                        skip(1, s2, g, par)
                    if t == 12:
                        dve.wait_ge(sem("y_skip"), g * 3 + 2)
                        v = yb[:, :, P:SEQ]
                        tt(v, v, offe[:, :].rearrange("p (i q) -> p i q", i=4), ALU.add).then_inc(sem("off1_added"), 1)
                    if 13 <= t < 21:
                        b = t - 13
                        dve.wait_ge(sem("h0_product"), g * 8 + (b + 1))
                        for i in range(4):
                            q = P + DL * b + DL - 1
                            last = stt(h0[:, b % 4, i, :], h0[:, b % 4, i, :], ee[:, i, q:q + 1],
                                       s2[:, i * P:(i + 1) * P], ALU.mult, ALU.add)
                        last.then_inc(sem("h0_updated"), 1)
                    if t == 21:
                        dve.wait_ge(sem("h0_read"), g * 8 + 8)
                        skip(2, s0, g, par)
                        tt(offe[:, 0:P].rearrange("p (i q) -> p i q", i=4), s0[:, P:2 * P].rearrange("p (i q) -> p i q", i=4),
                           ee[:, :, P:160], ALU.mult).then_inc(sem("off2_scaled"), 1)
                        dve.wait_ge(sem("off2_scaled"), g + 1)
                        dve.wait_ge(sem("y_skip"), g * 3 + 3)
                        v = yb[:, :, SEQ:T]
                        tt(v, v, offe[:, 0:P].rearrange("p (i q) -> p i q", i=4), ALU.add).then_inc(sem("off2_added"), 1)
                    if t == 22:
                        dve.wait_ge(sem("off2_added"), g + 1)
                        dve.wait_ge(sem("off1_added"), g + 1)
                        tt(yb[:, :, :], yb[:, :, :], zs[:, par, :, :], ALU.mult).then_inc(sem("y_gated"), 1)
                    if t == 25:
                        for i in range(4):
                            dve.wait_ge(sem("y_rounded"), g * 4 + (i + 1))
                            stt(y_lo[:, i, :], yb[:, i, :], gnv[:, 0, i:i + 1], y_hi[:, i, :].bitcast(F32),
                                ALU.mult, ALU.subtract).then_inc(sem("y_split"), 1)
                    if not (isinstance(g, int) and g == 0) and 1 <= t < 9:
                        og = t - 1
                        for m in range(2):
                            ya_add(og, m, chunk_at(g, og), (par + og) % 2)
                if conv:
                    if t == 11:
                        cv = vec[:, V_CB:V_CB + 240].rearrange("p (k i) -> p k i", k=5)
                        dve.tensor_copy(gcv[:, :, 0:1], cv[:, :, ds(n + 32, 1)])
                        dve.tensor_copy(gcv[:, :, 1:2], cv[:, :, ds(n + 40, 1)])
                        dve.tensor_copy(gcv[:, :, 2:6], cv[:, :, ds(n * 4, 4)]).then_inc(sem("conv_vectors"), 1)
                        dve.wait_ge(sem("conv_vectors"), n + 1)
                    for j in range(3):
                        if t in (13 + 4 * j, 14 + 4 * j):
                            conv_taps(2 * j + (t - 13) % 4, n)
                        if t in (15 + 4 * j, 16 + 4 * j):
                            conv_silu(2 * j + (t - 15) % 4, n, 1 - par)
                    if t in (25, 26):
                        z_silu(t - 25, n, 1 - par, par)

            for c in range(LEAD):
                split(c, c, 512)
            for t in range(4):
                split(t + LEAD, (t + LEAD) % 4, 512 if t == 0 else 1024)
            st = sem("vector_steps")
            step = [0]

            def link(ins):
                step[0] += 1
                ins.then_inc(st, 1)
                dve.wait_ge(st, step[0])

            three = lambda v: v.rearrange("p (c h) -> p c h", c=3)
            link(dve.memset(dw[:, 0, :], 0.0))
            link(dve.memset(tokv[:, :, :], 0.0))
            dve.wait_ge(sem("dt_turned"), 1)
            tt(dw[:, 0, 0:128].rearrange("p (c h) -> p c h", c=2), s1[:, 0:128].rearrange("p (c h) -> p c h", c=2),
               bc(rowv[:, 0, :], 2, 1), ALU.add)
            tt(dw[0:32, 0, 128:192], s1[0:32, 128:192], rowv[0:32, 0, :], ALU.add).then_inc(sem("dt_biased"), 1)
            dve.wait_ge(sem("dt_act"), 2)
            ts(dw[:, 3, :], dw[:, 2, :], 1.0, None, ALU.add).then_inc(sem("dt_u"), 1)
            dve.wait_ge(sem("dt_u"), 1)
            link(ts(dw[:, 5, :], dw[:, 3, :], 1.0, None, ALU.subtract))
            link(ts(dw[:, 6, :], dw[:, 5, :], 1e-30, None, ALU.max))
            link(dve.reciprocal(dw[:, 6, :], dw[:, 6, :]))
            link(tt(dw[:, 6, :], dw[:, 6, :], dw[:, 2, :], ALU.mult))
            link(stt(dw[:, 5, :], dw[:, 5, :], 0.0, dw[:, 2, :], ALU.is_equal, ALU.mult))
            dve.wait_ge(sem("dt_act"), 3)
            link(tt(dw[:, 6, :], dw[:, 6, :], dw[:, 4, :], ALU.mult))
            link(tt(dw[:, 6, :], dw[:, 6, :], dw[:, 5, :], ALU.add))
            link(stt(tokv[:, DT:DT + 3, :], three(dw[:, 0, :]), 0.0, three(dw[:, 6, :]), ALU.max, ALU.add))
            dve.wait_ge(sem("a_exp"), 1)
            stt(tokv[:, DTA:DTA + 3, :], tokv[:, DT:DT + 3, :], -1.0, bc(rowv[:, 1, :], 3, 1),
                ALU.mult, ALU.mult).then_inc(sem("dta_ready"), 1)
            dve.wait_ge(sem("acs_ready"), 1)
            dve.tensor_copy(tokv[:, ACS:ACS + 2, :], s2[:, 0:128].rearrange("p (c h) -> p c h", c=2))
            link(dve.tensor_copy(tokv[0:32, ACS + 2, :], s2[0:32, 128:192]))
            tt(tokv[:, DEC:DEC + 2, :], s3[:, 0:128].rearrange("p (c h) -> p c h", c=2), tokv[:, ACS:ACS + 2, :], ALU.subtract)
            tt(tokv[0:32, DEC + 2, :], s3[0:32, 128:192], tokv[0:32, ACS + 2, :], ALU.subtract)
            dve.tensor_copy(tokv[:, CDEC, :], s3[:, 64:128]).then_inc(sem("dec_raw"), 1)

            for t in range(8, 28):
                split_at(-1, t)
                side_work(t, -1, 1, False, True)
            dve.wait_ge(sem("dec_ready"), 1)
            for k, s in enumerate(xT_stored):
                dve.wait_ge(s, 16 * len(range(k, KT, 3)))
            for t in range(28):
                if t >= 8:
                    split_at(0, t)
                side_work(t, 0, 0, True, True)

            def iteration(g, par):
                for t in range(28):
                    split_at(g, t)
                    side_work(t, g, par, True, True)

            with dve.Fori(0, 3) as i:
                iteration(i * 2 + 1, 1)
                iteration(i * 2 + 2, 0)
            for t in range(40):
                split_at(7, t)
                side_work(t, 7, 1, True, False)
            for t in range(8):
                if t + LEAD < 8:
                    split(C_TAIL + t + LEAD, (t + LEAD) % 4)
                if t >= 1:
                    for m in range(2):
                        ya_add(t - 1, m, C_TAIL + t - 1, (105 + t - 1) % 2)
            for m in range(2):
                ya_add(7, m, C_TAIL + 7, (105 + 7) % 2)

            def norm(k):
                dve.wait_ge(sem("rms_ready"), k)
                dve.reciprocal(rstd[:, :], rstd[:, :]).then_inc(sem("rstd_ready"), 1)
                dve.wait_ge(sem("rstd_ready"), k)

            def splits(k, c0, t):
                split(k * 4 + (c0 + t + LEAD), (t + LEAD) % 4)

            norm(1)

            def tile(v, i):
                return v[:, ds(i, 1), :].rearrange("p o t -> p (o t)")

            dve.wait_ge(*reach("lambda_landed", 48))
            dve.tensor_copy(ln5[:, 2, :].rearrange("p (g n) -> p g n", g=2), bc(ldt[:, :], S5N, 2)).then_inc(sem("ldt_spread"), 1)
            dve.wait_ge(*reach("s5_step", 1))
            pr = lambda k: pr5[:, k, :]
            link(tt(pr(1), lam[:, 0, :], pr(0), ALU.mult))
            link(tt(pr(2), lam[:, 1, :], pr(0), ALU.mult))
            link(ts(pr(4), pr(2), float(1 / (2 * np.pi)), None, ALU.mult))
            link(ts(pr(4), pr(4), ROUND, None, ALU.add))
            link(ts(pr(4), pr(4), ROUND, None, ALU.subtract))
            link(stt(pr(5), pr(4), -TWO_PI_HI, pr(2), ALU.mult, ALU.add))
            link(stt(pr(5), pr(4), -TWO_PI_LO, pr(5), ALU.mult, ALU.add))
            ts(pr(5), pr(5), PI_IN, -PI_IN, ALU.min, ALU.max).then_inc(sem("s5_exponents"), 1)
            dve.wait_ge(*reach("s5_sin", 2))
            dve.wait_ge(*reach("s5_mag", 1))
            link(tt(pr(9), pr(3), pr(8), ALU.mult))
            link(tt(pr(10), pr(3), pr(7), ALU.mult))
            lr, li, ar, ai = lam[:, 0, :], lam[:, 1, :], pr(9), pr(10)
            link(tt(pr(11), lr, lr, ALU.mult))
            link(tt(pr(0), li, li, ALU.mult))
            link(tt(pr(11), pr(11), pr(0), ALU.add))
            link(dve.reciprocal(pr(11), pr(11)))
            link(stt(pr(12), ar, 1.0, lr, ALU.subtract, ALU.mult))
            link(tt(pr(0), ai, li, ALU.mult))
            link(tt(pr(12), pr(12), pr(0), ALU.add))
            link(tt(pr(12), pr(12), pr(11), ALU.mult))
            link(stt(pr(13), ar, 1.0, li, ALU.subtract, ALU.mult))
            link(tt(pr(0), ai, lr, ALU.mult))
            link(tt(pr(13), pr(0), pr(13), ALU.subtract))
            link(tt(pr(13), pr(13), pr(11), ALU.mult))
            link(dve.memset(pq5[:, 0, 3, :], 1.0))
            link(dve.memset(pq5[:, 1, 3, :], 0.0))
            link(dve.tensor_copy(po5[:, 0, 0, :], ar))
            link(dve.tensor_copy(po5[:, 1, 0, :], ai))
            for k, (x, y) in ((1, (0, 0)), (2, (1, 0)), (3, (1, 1))):
                xr, xi, yr, yi = po5[:, 0, x, :], po5[:, 1, x, :], po5[:, 0, y, :], po5[:, 1, y, :]
                link(tt(pr(0), xr, yr, ALU.mult))
                link(tt(pr(1), xi, yi, ALU.mult))
                link(tt(po5[:, 0, k, :], pr(0), pr(1), ALU.subtract))
                link(tt(pr(0), xr, yi, ALU.mult))
                link(tt(pr(1), xi, yr, ALU.mult))
                link(tt(po5[:, 1, k, :], pr(0), pr(1), ALU.add))
            for k in range(3):
                link(dve.tensor_copy(pq5[:, :, 2 - k, :], po5[:, :, k, :]))
            link(ts(a4x[:, 0, :], po5[:, 1, 3, :], -1.0, None, ALU.mult))
            link(dve.tensor_copy(a4x[:, 1, :], po5[:, 1, 3, :]))
            br, bi = bb5[:, 0], bb5[:, 1]
            dve.wait_ge(sem("s5_params_landed"), 16 * 34)
            t0, t1 = [pw5[:, k].rearrange("p a (b c) -> p (a b) c", c=S5C) for k in range(2)]
            t2, t3 = tm5[:, :, :].rearrange("p k (b c) -> p (k b) c", c=S5C), gs5[:, :, :]
            qr, qi = bc(pr(12), S5C, 2), bc(pr(13), S5C, 2)
            link(tt(t0, br, qr, ALU.mult))
            link(tt(t1, bi, qi, ALU.mult))
            link(tt(t2, bi, qr, ALU.mult))
            link(tt(t3, br, qi, ALU.mult))
            link(tt(br, t0, t1, ALU.subtract))
            tt(bi, t2, t3, ALU.add).then_inc(sem("bbar_ready"), 1)
            dve.wait_ge(*reach("bbar_ready", 1))
            dve.wait_ge(sem("s5_zeros"), 10)
            dve.wait_ge(sem("c_ready"), 4)

            def block_diag(i, bd, tm, src, pows, re_sub, im_rev, s):
                xr, xi = [bc(src[:, k, ds(i * PB, PB), :], DL, 2) for k in range(2)]
                qr, qi = [bc(pows[:, k, :, ds(i * PB, PB)].rearrange("x j p -> x p j"), S5C, 3) for k in range(2)]
                v = [tm[:, k, :].rearrange("x (p j c) -> x p j c", p=PB, j=DL) for k in range(2)]
                n = i * 4
                for part, (x0, q0, x1, q1, op) in enumerate(((xr, qr, xi, qi, re_sub), (xi, qr, xr, qi, im_rev))):
                    tt(v[0], x0, q0, ALU.mult).then_inc(sem(s + "_products"), 1)
                    tt(v[1], x1, q1, ALU.mult).then_inc(sem(s + "_products"), 1)
                    dve.wait_ge(sem(s + "_products"), n + (2 * part + 2))
                    for g2 in range(2):
                        r = slice(64 * g2, 64 * g2 + 64)
                        dst = bd[r, part, :, 64 * g2:64 * g2 + 64].rearrange("x p (j c) -> x p j c", j=DL)
                        last = tt(dst, v[0][r], v[1][r], op)
                    last.then_inc(sem(s + "_matrices"), 1)
                    dve.wait_ge(sem(s + "_matrices"), i * 2 + (part + 1))

            def gs_copy(i):
                dve.wait_ge(sem("g_product"), i + 1)
                dve.tensor_copy(gs5[:, ds(i * PB, PB), :], s0[:, 0:P].rearrange("p (g c) -> p g c", c=S5C)).then_inc(sem("gs_ready"), 1)

            def q_block(i, b):
                wait(dve, "g_product", i - 1)
                block_diag(i, (qbd, qbd2)[b], tm5, bb5, pq5, ALU.subtract, ALU.add, "q")
                if not (isinstance(i, int) and i == 0):
                    gs_copy(i - 1)

            q_block(0, 0)
            q_block(1, 1)
            with dve.Fori(1, 4) as i:
                q_block(i * 2, 0)
                q_block(i * 2 + 1, 1)
            gs_copy(7)
            for c in range(LEAD):
                split(C_GATE + c, c)
            dve.wait_ge(sem("p_copied"), 24)
            dve.wait_ge(*reach("s5_states_ready", 2))
            dve.drain().then_inc(sem("scan_stepped"), 1)
            col = lambda n: st5[:, :, :, ds(n, 1)].rearrange("p c g o -> p c (g o)")
            scr = [scr5[:, m, :].rearrange("p (c g) -> p c g", c=2) for m in range(2)]
            a4r = bc(po5[:, 0, 3, :], 2, 1)

            def scan_products(n):
                dve.wait_ge(sem("scan_stepped"), n)
                now = col(n)
                tt(scr[0], now, a4r, ALU.mult)
                tt(scr[1][:, 0], now[:, 1, :], a4x[:, 0, :], ALU.mult)
                tt(scr[1][:, 1], now[:, 0, :], a4x[:, 1, :], ALU.mult).then_inc(sem("scan_products"), 1)

            def scan_sums(n):
                dve.wait_ge(sem("scan_products"), n)
                tt(scr[0], scr[0], scr[1], ALU.add).then_inc(sem("scan_decayed"), 1)
                dve.wait_ge(sem("scan_decayed"), n)
                tt(col(n + 1), col(n + 1), scr[0], ALU.add).then_inc(sem("scan_stepped"), 1)

            def gate(k, b, second, lead=4):
                for t in range(4):
                    n = k * 4 + (t + 1)
                    scanned = isinstance(n, int) and n > 62
                    if not scanned:
                        scan_products(n)
                    if t < lead:
                        splits(k, C_GATE, t)
                    if not scanned:
                        scan_sums(n)
                for m in range(2):
                    dve.wait_ge(*reach("gate_tanh", k * 2 + (m + 1)))
                    i = k * 2 + m
                    if second:
                        ins = ts(tile(sgb, i - KT), gth[:, m, :], 0.25, 0.25, ALU.mult, ALU.add)
                    else:
                        ins = stt(tile(ya, i), gth[:, m, :], 1.0, tile(ya, i), ALU.add, ALU.mult)
                    ins.then_inc(sem("gate_done"), 1)

            dve.wait_ge(sem("ya_normed"), 1)
            with dve.Fori(0, 4) as i:
                gate(i * 2, 0, False)
                gate(i * 2 + 1, 1, False)
            with dve.Fori(4, 7) as i:
                gate(i * 2, 0, True)
                gate(i * 2 + 1, 1, True)
            gate(14, 0, True)
            gate(15, 1, True, lead=1)

            dve.wait_ge(multiplied, C_GLU)
            dve.wait_ge(sem("scan_stepped"), 63)
            f9 = lambda v: v.rearrange("p g b -> p b g")
            tmf = tmo[:, :, :].rearrange("p k n -> p (k n)")[:, 0:9 * PAIRS].rearrange("p (b g) -> p b g", b=9)
            a4i = bc(po5[:, 1, 3, :], 9, 1)
            a4rr = bc(po5[:, 0, 3, :], 9, 1)
            sre, sim = f9(st5[:, 0, :, 63:72]), f9(st5[:, 1, :, 63:72])
            for part, (x, y, op) in enumerate(((sre, sim, ALU.subtract), (sim, sre, ALU.add))):
                link(tt(fin5[:, part], x, a4rr, ALU.mult))
                link(tt(tmf, y, a4i, ALU.mult))
                link(tt(fin5[:, part], fin5[:, part], tmf, op))
                link(tt(fin5[:, part], fin5[:, part], f9(en5[:, part]), ALU.add))
            dve.drain().then_inc(sem("s5_scanned"), 1)

            def o_block(i, b):
                wait(dve, "y5_product", i * 2 - 2)
                block_diag(i, (obd, obd2)[b], tmo, ct5, po5, ALU.add, ALU.subtract, "o")

            dve.wait_ge(*reach("s5_bd_zero", 3))
            o_block(0, 0)
            o_block(1, 1)
            with dve.Fori(1, 4) as i:
                o_block(i * 2, 0)
                o_block(i * 2 + 1, 1)
            dve.wait_ge(*reach("ut_landed", 16))
            js = lambda v: v.rearrange("p (j k) -> p j k", j=DL)
            for i in range(KT + 2):
                if i < KT:
                    dve.wait_ge(sem("yt_landed"), 16 * (i // 4 + 1))
                    if i == 4:
                        dve.wait_ge(*reach("ut_landed", 32))
                    stt(yt5[:, i, :], (ut4 if i < 4 else ut5)[:, i, :], vec[:, V_D5 + i:V_D5 + i + 1], yt5[:, i, :], ALU.mult, ALU.add).then_inc(sem("gelu_y"), 1)
                if 1 <= i <= KT:
                    k = i - 1
                    dve.wait_ge(*reach("gelu_y", i))
                    dve.wait_ge(*reach("gelu_squared", i))
                    wait(dve, "gelu_out", i - 2)
                    stt(gar[:, k % 2, :], gsq[:, k % 2, :], 1 / GELU_A, yt5[:, k, :], ALU.add, ALU.mult).then_inc(sem("gelu_arg"), 1)
                if 2 <= i <= KT + 1:
                    k = i - 2
                    dve.wait_ge(*reach("gelu_tanh", i - 1))
                    wait(dve, "v_ready", i - 3)
                    stt(gou[:, k % 2, :].rearrange("p (k j) -> p j k", j=DL), js(gar[:, k % 2, :]), 1.0,
                        js(yt5[:, k, :]), ALU.add, ALU.mult).then_inc(sem("gelu_out"), 1)

            for c in range(LEAD):
                split(C_GLU + c, c)

            def glu(k, b):
                for t in range(4):
                    splits(k, C_GLU, t)
                v = gl[:, b, 1, :]
                dve.wait_ge(*reach("glu_tanh", k + 1))
                stt(v, gl[:, b, 0, :], 1.0, acc[2 * ((129 + b) % 2)][:, 0:T], ALU.add, ALU.mult).then_inc(freed, 1)
                dve.wait_ge(freed, k + 1)
                tt(v, v, tile(sgb, k), ALU.mult).then_inc(sem("glu_gated"), 1)
                dve.wait_ge(*reach("glu_gated", k + 1))
                tt(v, v, tile(ya, k), ALU.add).then_inc(sem("glu_summed"), 1)
                dve.wait_ge(*reach("glu_summed", k + 1))
                dve.wait_ge(*reach("glu_rounded", k + 1))
                tt(tile(mg_lo, k), v, tile(mg_hi, k).bitcast(F32), ALU.subtract).then_inc(sem("merged"), 1)

            with dve.Fori(0, 8) as i:
                glu(i * 2, 0)
                glu(i * 2 + 1, 1)

            dve.memset(sst[:, :], 0.0).then_inc(sem("sst_zero"), 1)

            def summed(k, b, s_sq, s_sum, sq, dst, base_og):
                for m in range(2):
                    dve.wait_ge(*reach(s_sq, k * 2 + (m + 1)))
                    dve.tensor_copy(tile(dst, k * 2 + m), acc[2 * ((base_og + b) % 2) + m][:, 0:T]).then_inc(sem(s_sum + "_copied"), 1)
                    wait(dve, s_sum, k * 2 + m)
                    tt(sst[:, :], sst[:, :], sq[:, m, :], ALU.add).then_inc(sem(s_sum), 1)
                dve.wait_ge(sem(s_sum + "_copied"), k * 2 + 2)
                dve.wait_ge(*reach(s_sum, k * 2 + 2))
                dve.tensor_copy(sx2[:, 0:1], eps1[:, 0:1]).then_inc(freed, 1)

            def proj(k, b):
                for t in range(4):
                    splits(k, C_OUT, t)
                summed(k, b, "m_squared", "m_summed", msq, mt, 145)

            dve.wait_ge(sem("sst_zero"), 1)
            proj(0, 0)
            proj(1, 1)
            with dve.Fori(1, 4) as i:
                proj(i * 2, 0)
                proj(i * 2 + 1, 1)
            norm(2)
            dve.memset(sst[:, :], 0.0).then_inc(sem("sst_zero"), 1)
            dve.wait_ge(sem("xT_landed"), 16)
            dve.wait_ge(sem("sst_zero"), 2)
            for i in range(KT + 1):
                if i < KT:
                    stt(mt[:, i, :], mt[:, i, :], vec[:, N_POST + i:N_POST + i + 1], rstd[:, :], ALU.mult, ALU.mult).then_inc(sem("m_normed"), 1)
                if 1 <= i <= KT:
                    dve.wait_ge(*reach("m_normed", i))
                    tt(x1[:, i - 1, :], x1[:, i - 1, :], mt[:, i - 1, :], ALU.add).then_inc(sem("x1_ready"), 1)
            norm(3)
            for i in range(KT + 1):
                if i < KT:
                    wait(dve, "h2_ready", i - 2)
                    stt(msq[:, i % 3, :], x1[:, i, :], vec[:, N_FPRE + i:N_FPRE + i + 1], rstd[:, :],
                        ALU.mult, ALU.mult).then_inc(sem("h2_scaled"), 1)
                if i >= 1:
                    dve.wait_ge(*reach("h2_scaled", i))
                    dve.wait_ge(*reach("h2_rounded", i))
                    tt(h_lo[:, i - 1, :], msq[:, (i - 1) % 3, :], h_hi[:, i - 1, :].bitcast(F32), ALU.subtract).then_inc(sem("h2_ready"), 1)

            def up(k, b):
                for t in range(4):
                    splits(k, C_UP, t)
                pair = (153 + b) % 2
                v = fg[:, b, 1, :]
                dve.wait_ge(*reach("f_tanh", k + 1))
                stt(v, fg[:, b, 0, :], 1.0, acc[2 * pair][:, 0:T], ALU.add, ALU.mult).then_inc(sem("f_silu"), 1)
                dve.wait_ge(*reach("f_silu", k + 1))
                tt(v, v, acc[2 * pair + 1][:, 0:T], ALU.mult).then_inc(sem("f_out"), 1)
                dve.wait_ge(*reach("f_out", k + 1))
                dve.tensor_copy(sx2[:, 1:2], eps1[:, 0:1]).then_inc(freed, 1)
                dve.wait_ge(*reach("f_rounded", k + 1))
                tt(tile(f_lo, k), v, tile(f_hi, k).bitcast(F32), ALU.subtract).then_inc(sem("f_split"), 1)

            dve.wait_ge(sem("x1_stored"), 16)
            with dve.Fori(0, FT // 2) as i:
                up(i * 2, 0)
                up(i * 2 + 1, 1)

            def down(k, b, last=False):
                for t in range(12):
                    tt_ = t + LEAD
                    if last and tt_ >= 12:
                        continue
                    split(k * 12 + (C_DOWN + tt_), tt_ % 4, 1024 if tt_ % 12 < 8 else 768)
                summed(k, b, "f_squared", "f_summed", fsq, fT, 197)

            dve.memset(sst[:, :], 0.0).then_inc(sem("sst_zero"), 1)
            dve.wait_ge(sem("sst_zero"), 3)
            down(0, 0)
            down(1, 1)
            with dve.Fori(1, 3) as i:
                down(i * 2, 0)
                down(i * 2 + 1, 1)
            down(6, 0)
            down(7, 1, last=True)
            norm(4)
            dve.wait_ge(*reach("x1_landed", 16))
            for i in range(KT + 1):
                if i < KT:
                    stt(fT[:, i, :], fT[:, i, :], vec[:, N_FPOST + i:N_FPOST + i + 1], rstd[:, :], ALU.mult, ALU.mult).then_inc(sem("f_normed"), 1)
                if i >= 1:
                    dve.wait_ge(sem("f_normed"), i)
                    tt(x1r[:, i - 1, :], x1r[:, i - 1, :], fT[:, i - 1, :], ALU.add).then_inc(sem("y_ready"), 1)

        @block.tensor
        def _(pe):
            mm = pe.matmul
            one = dict(start=True, stop=True)

            def turn(out, in_):
                k = in_.shape[0]
                return pe.transpose(out, in_, ident[0:k, 0:k])

            def chunk(c, slot, pair, xh, xl, tiles, first, last, width=2 * P):
                pe.wait_ge(lo_ready, c + 1)
                n = len(tiles)
                for i, kt in enumerate(tiles):
                    for m in range(width // P):
                        o_ = acc[2 * pair + m][:, 0:T]
                        at_ = i * width + m * P
                        wh, wl = w_hi[:, slot, at_:at_ + P], w_lo[:, slot, at_:at_ + P]
                        mm(o_, wh, xh[:, kt, :], start=first and i == 0, stop=False)
                        mm(o_, wh, xl[:, kt, :], start=False, stop=False)
                        done = mm(o_, wl, xh[:, kt, :], start=False, stop=last and i == n - 1)
                done.then_inc(multiplied, 1)

            pe.wait_ge(sem("masks_made"), 20)
            pe.wait_ge(sem("params_landed"), 16 * 12)
            for src, n, col in ((2, 112, 0), (0, 96, 112), (1, 96, 208), (3, 48, 304)):
                last = turn(s0[:, col:col + n], vraw[0:n, src, :])
            last.then_inc(sem("vec_turned"), 1)
            pe.wait_ge(sem("x_rstd"), 2)
            for c, (t0, n) in enumerate(TOK):
                last = mm(s3[:, t0:t0 + n], sx[0:n, c:c + 1].to_broadcast([n, P]), ident[0:n, 0:n], **one)
            last.then_inc(sem("x_rstd_spread"), 1)
            for i in range(KT):
                if i >= 4:
                    pe.wait_ge(sem("xT_copied"), i - 3)
                for c, (t0, n) in enumerate(TOK):
                    last = turn(acc[i % 4][:, t0:t0 + n], xnat[0:n, c, i * P:(i + 1) * P])
                last.then_inc(sem("x_turned"), 1)

            def history(n):
                pe.wait_ge(sem("history_landed"), n * 48 + 48)
                for k in range(6):
                    last = mm(s0[:, k * 24:(k + 1) * 24], cst[:, k * P:(k + 1) * P], ident[0:24, 0:24], **one)
                last.then_inc(sem("history_turned"), 1)

            pe.wait_ge(sem("vec_ready"), 3)
            history(0)
            pe.wait_ge(sem("h_ready"), KT)
            for c in range(4):
                chunk(c, c, 0, h_hi, h_lo, range(4 * c, 4 * c + 4), c == 0, c == 3, width=P)
            pe.wait_ge(sem("dt_copied"), 1)
            for c, (t0, n) in enumerate(TOK):
                last = turn(s1[0:n, c * HEADS:(c + 1) * HEADS], dtT[:, t0:t0 + n])
            last.then_inc(sem("dt_turned"), 1)

            def running_sums():
                pe.wait_ge(sem("dta_ready"), 1)
                for c, (t0, n) in enumerate(TOK):
                    dta = tokv[0:n, DTA + c, :]
                    mm(s2[0:n, c * HEADS:(c + 1) * HEADS], tri[:, :] if c < 2 else btri[:, :], dta, **one)
                    last = mm(s3[0:n, c * HEADS:(c + 1) * HEADS], ones[:, :] if c < 2 else bones[:, :], dta, **one)
                last.then_inc(sem("acs_ready"), 1)

            def freed_for(l, g):
                if isinstance(g, int) and g == -1:
                    if l == 9:
                        pe.wait_ge(sem("dt_copied"), 1)
                elif isinstance(g, int) and g == 0:
                    if l == 8:
                        pe.wait_ge(sem("z_done"), 2)
                    if l == 9:
                        pe.wait_ge(sem("z_done"), 4)
                else:
                    if l < 2:
                        pe.wait_ge(sem("z_done"), g * 4 + (2 + 2 * l))
                    elif l < 10:
                        pe.wait_ge(sem("ya_added"), g * 16 + (2 * (l - 1) - 16))
                if l >= 10:
                    if isinstance(g, int) and g == 7:
                        pe.wait_ge(sem("u_ready"), 2 * (l - 9))
                    else:
                        pe.wait_ge(sem("conv_in_ready"), g * 6 + (6 + 2 * (l - 9)))

            def spread(bank, c, g):
                n = TOK[c][1]
                for j in range(HG):
                    lhs = gtv[0:n, DTA + c, j:j + 1].to_broadcast([n, n])
                    if c < 2:
                        last = mm(bank[j // 4][:, (j % 4) * P:(j % 4 + 1) * P], lhs, tri[:, :], **one)
                    else:
                        last = mm(bank[0:n, P + j * n:P + (j + 1) * n], lhs, btri[:, :], **one)
                return last

            def by_feature(bank, c):
                n = TOK[c][1]
                for i in range(4):
                    lhs = (dta1, dta2)[c - 1][0:n, i * P:(i + 1) * P]
                    last = mm(bank[:, i * n:(i + 1) * n], lhs, tri[:, :] if c < 2 else btri[:, :], **one)
                return last

            def within(bank, c, g):
                n = TOK[c][1]
                pe.wait_ge(sem("m_ready"), g * 3 + (c + 1))
                for j in range(HG):
                    r = 64 * (j % 2)
                    last = mm(bank[r:r + 64, (j // 2) * n:(j // 2 + 1) * n], xdt[0:n, c, j * HD:(j + 1) * HD],
                              seg[0:n, c % 2, j * n:(j + 1) * n], **one)
                return last

            def side_work(t, g, par, ssd, conv):
                n = g + 1
                bT, cT = xc[:, par, 0, :], xc[:, par, 1, :]
                if ssd:
                    if t == 0:
                        wait(pe, "off2_scaled", g)
                        wait(pe, "conv_rows_ready", n)
                        pe.wait_ge(sem("conv_out"), g * 6 + 6)
                        for c, (t0, m) in enumerate(TOK):
                            last = turn(s0[0:m, c * P:(c + 1) * P], bT[:, t0:t0 + m])
                        last.then_inc(sem("b_turned"), 1)
                        for c, (t0, m) in enumerate(TOK):
                            last = mm(s1[0:m, t0:t0 + m], bT[:, t0:t0 + m], cT[:, t0:t0 + m], **one)
                        last.then_inc(sem("cb_ready"), 1)
                        for c in range(2):
                            for i in range(4):
                                last = turn((s2, s3)[c][:, i * P:(i + 1) * P], xc[:, par, 2 + i, c * P:(c + 1) * P])
                        last.then_inc(sem("x01_turned"), 1)
                    if t == 2:
                        pe.wait_ge(sem("btok_ready"), g + 1)
                        for i in range(4):
                            last = turn(s0[0:32, i * P:(i + 1) * P], xc[:, par, 2 + i, SEQ:T])
                        last.then_inc(sem("x2_turned"), 1)
                        pe.wait_ge(sem("xdt_ready"), g * 3 + 2)
                        pe.wait_ge(sem("group_vectors"), g + 1)
                        spread((s2, s3), 0, g).then_inc(sem("acs0_spread"), 1)
                    if t == 4:
                        pe.wait_ge(sem("cb_masked"), g + 1)
                        pe.wait_ge(sem("dta_spread"), g + 1)
                        by_feature(s1, 1).then_inc(sem("e1_ready"), 1)
                        pe.wait_ge(sem("seg_clamped"), g * 3 + 1)
                        spread((s2, s3), 1, g).then_inc(sem("acs1_spread"), 1)
                    if t == 6:
                        pe.wait_ge(sem("xdt_ready"), g * 3 + 3)
                        if conv:
                            pe.wait_ge(sem("history_ready"), n + 1)
                        by_feature(s0, 2)
                        spread(s0, 2, g).then_inc(sem("es_ready"), 1)
                        pe.wait_ge(sem("e1_exp"), g + 1)
                        pe.wait_ge(sem("xw_ready"), g * 4 + 4)
                        mm(s1[:, :], btok[:, 0, :], xw[:, 0, :], **one).then_inc(sem("ht_ready"), 1)
                    if t == 7:
                        pe.wait_ge(sem("seg_clamped"), g * 3 + 2)
                        within(s2, 0, g).then_inc(sem("y0_ready"), 1)
                    if t == 8:
                        for i in range(4):
                            v = s3[:, i * P:(i + 1) * P]
                            mm(v, xw[:, 3, i * P:(i + 1) * P], btok[:, 0, :], start=True, stop=False)
                            last = mm(v, xw[:, 1, i * P:(i + 1) * P], btok[:, 1, :], start=False, stop=True)
                        last.then_inc(sem("prompt_state"), 1)
                    if t == 9:
                        pe.wait_ge(sem("ht_copied"), g + 1)
                        for i in range(4):
                            last = mm(s1[:, i * P:(i + 1) * P], ht[:, i * P:(i + 1) * P], cT[:, P:SEQ], **one)
                        last.then_inc(sem("off1_ready"), 1)
                    if t == 10:
                        pe.wait_ge(sem("y_skip"), g * 3 + 1)
                        within(s2, 1, g).then_inc(sem("y1_ready"), 1)
                    if t == 11:
                        pe.wait_ge(sem("es_exp"), g + 1)
                        pe.wait_ge(sem("seg_clamped"), g * 3 + 3)
                        within(s0, 2, g).then_inc(sem("y2_ready"), 1)
                    if 12 <= t < 20:
                        b = t - 12
                        pe.wait_ge(h0_landed[b % 4], g * 32 + 16 * (b // 4 + 1))
                        if b == 0:
                            pe.wait_ge(sem("prompt_state_ready"), g + 1)
                        if b == 1:
                            pe.wait_ge(sem("off1_scaled"), g + 1)
                        if b >= 2:
                            pe.wait_ge(sem("h0t_copied"), g * 8 + (b - 1))
                        for i in range(4):
                            last = turn((s3 if b % 2 == 0 else s1)[:, i * P:(i + 1) * P], h0[:, b % 4, i, :])
                        last.then_inc(sem("h0_turned"), 1)
                        if b == 0:
                            pe.wait_ge(sem("y_skip"), g * 3 + 2)
                            pe.wait_ge(sem("bm_ready"), g + 1)
                        else:
                            pe.wait_ge(sem("h0_updated"), g * 8 + b)
                        for i in range(4):
                            last = mm(s2[:, i * P:(i + 1) * P], xw[0:32, 2, i * P:(i + 1) * P], bm[:, b, :], **one)
                        last.then_inc(sem("h0_product"), 1)
                    if 13 <= t < 21:
                        b = t - 13
                        pe.wait_ge(sem("h0t_copied"), g * 8 + (b + 1))
                        for i in range(4):
                            col = P + 32 * i + DL * b
                            last = mm(s0[:, col:col + DL], h0t[:, b % 2, i * P:(i + 1) * P],
                                      cT[:, SEQ + DL * b:SEQ + DL * b + DL], **one)
                        last.then_inc(sem("h0_read"), 1)
                if conv:
                    if t == 4 and ssd:
                        pe.wait_ge(sem("xdt_ready"), g * 3 + 3)
                        history(n)
                    if t == 25:
                        pe.wait_ge(sem("conv_rows"), n * 6 + 6)
                        if ssd:
                            pe.wait_ge(sem("h0_updated"), g * 8 + 8)
                            pe.wait_ge(sem("h0t_copied"), g * 8 + 7)
                        for k in range(6):
                            bank = s2 if k < 4 else s3
                            last = turn(bank[0:27, (k % 4) * P:(k % 4 + 1) * P], cnew[:, k, :])
                        last.then_inc(sem("conv_rows_turned"), 1)

            def group_chunk(t, g, par):
                l = 8 + (t - 8) // 4
                if t % 4 == 0:
                    freed_for(l, g)
                kc = t % 4
                chunk(chunk_at(g, t), kc, (par + l) % 2, h_hi, h_lo, range(4 * kc, 4 * kc + 4), kc == 0, kc == 3)

            def g2_chunk(t, g, par):
                freed_for(t, g)
                if t == 0:
                    pe.wait_ge(sem("y_split"), g * 4)
                chunk(chunk_at(g, t), t % 4, (par + t) % 2, y_hi, y_lo, range(4), True, True)

            for t in range(8, 28):
                if t == 10:
                    running_sums()
                group_chunk(t, -1, 1)
                side_work(t, -1, 1, False, True)
            for t in range(28):
                if t >= 8:
                    group_chunk(t, 0, 0)
                side_work(t, 0, 0, True, True)

            def iteration(g, par):
                for t in range(28):
                    if t < 8:
                        g2_chunk(t, g, par)
                    else:
                        group_chunk(t, g, par)
                    side_work(t, g, par, True, True)

            with pe.Fori(0, 3) as i:
                iteration(i * 2 + 1, 1)
                iteration(i * 2 + 2, 0)
            for t in range(40):
                if t < 8:
                    g2_chunk(t, 7, 1)
                else:
                    group_chunk(t, 7, 1)
                side_work(t, 7, 1, True, False)
            pe.wait_ge(sem("y_split"), 32)
            for t in range(8):
                if t < 2:
                    pe.wait_ge(sem("u_ready"), 14 + 2 * t)
                else:
                    pe.wait_ge(sem("ya_added"), 112 + 2 * (t - 1))
                chunk(C_TAIL + t, t % 4, (105 + t) % 2, y_hi, y_lo, range(4), True, True)

            def sum_squares():
                mm(s0[:, 0:T], ones[:, :], sst[:, :], **one).then_inc(sem("squares_summed"), 1)

            pe.wait_ge(sem("y_summed"), 4 * NG)
            sum_squares()

            def outgroup(k, c0, pair, xh, xl, ready=None):
                for kc in range(4):
                    if ready:
                        pe.wait_ge(*reach(ready, 4 * kc + 4))
                    chunk(k * 4 + (c0 + kc), kc, pair, xh, xl, range(4 * kc, 4 * kc + 4), kc == 0, kc == 3)

            pe.wait_ge(*reach("lambda_landed", 48))
            pe.wait_ge(sem("rms_ready"), 1)
            pe.wait_ge(*reach("ldt_spread", 1))
            for k in range(3):
                last = turn(s0[:, k * PAIRS:(k + 1) * PAIRS], ln5[:, k, :])
            last.then_inc(sem("lam_turned"), 1)
            pe.wait_ge(sem("s5_params_landed"), 16 * 34)
            for k in range(2):
                for b in range(8):
                    if k == 1 and b % 4 == 0:
                        pe.wait_ge(sem("c_ready"), b // 4 + 1)
                    last = turn((s2 if b < 4 else s3)[:, (b % 4) * P:(b % 4 + 1) * P], cn5[:, k, b, :])
                    if b % 4 == 3:
                        last.then_inc(sem("c_turned"), 1)
            pe.wait_ge(sem("s5_states_landed"), 32)
            pe.wait_ge(*reach("lam_ready", 1))
            for k in range(2):
                for b in range(DB):
                    last = turn((s0 if k == 0 else s1)[:, b * PAIRS:(b + 1) * PAIRS], sn5[:, k, b, :])
                last.then_inc(sem("s5_states_turned"), 1)
            pe.wait_ge(sem("ya_added"), 16 * NG)
            pe.wait_ge(*reach("s5_states_ready", 2))
            pe.wait_ge(*reach("u2_landed", 16 * 8))
            pe.wait_ge(sem("c_ready"), 4)

            def s5_pass1(i, b):
                q = (qbd, qbd2)[b]
                for k in range(2):
                    pe.wait_ge(sem("q_matrices"), i * 2 + (k + 1))
                    for p in range(PB):
                        last = turn(turned[k][p // 4][:, (p % 4) * P:(p % 4 + 1) * P], q[:, k, p, :])
                    last.then_inc(sem("q_turned"), 1)
                wait(pe, "gs_ready", i)
                def response(p):
                    v = s0[:, p * S5C:(p + 1) * S5C]
                    for k in range(2):
                        last = mm(v, q[:, k, p, :], ct5[:, k, ds(i * PB + p, 1), :].rearrange("x o c -> x (o c)"),
                                  start=k == 0, stop=k == 1)
                    if p == PB - 1:
                        last.then_inc(sem("g_product"), 1)

                for p in range(4):
                    response(p)
                pe.wait_ge(sem("p_ready"), i * 4 + 4)
                for m, (p0, n) in enumerate(TRIPLES):
                    wait(pe, "p_copied", i * 3 + (m - 2))
                    for p in range(p0, p0 + n):
                        for k in range(2):
                            at_ = (2 * (p - p0) + k) * NK
                            last = mm(acc[m][:, at_:at_ + NK], pw5[:, k, p, :],
                                      u2[:, ds(i * PB + p, 1), :].rearrange("x o c -> x (o c)"), **one)
                        if p == p0 + n - 1:
                            last.then_inc(sem("p_product"), 1)
                        if p < 4:
                            response(p + 4)

            s5_pass1(0, 0)
            s5_pass1(1, 1)
            with pe.Fori(1, 4) as i:
                s5_pass1(i * 2, 0)
                s5_pass1(i * 2 + 1, 1)
            pe.wait_ge(sem("p_copied"), 24)
            def gate(k, b):
                if isinstance(k, int) and k < 2:
                    pe.wait_ge(sem("ya_added"), 126 + 2 * k)
                else:
                    pe.wait_ge(*reach("gate_done", k * 2 - 2))
                outgroup(k, C_GATE, (113 + b) % 2, h_hi, h_lo)

            gate(0, 0)
            gate(1, 1)
            with pe.Fori(1, 8) as i:
                gate(i * 2, 0)
                gate(i * 2 + 1, 1)

            pe.wait_ge(*reach("gate_done", 32))
            pe.wait_ge(sem("gs_ready"), 8)
            pe.wait_ge(sem("p_copied"), 24)
            for k in range(3):
                for h in range(2):
                    wait(pe, "t_ready", 2 * k + h - 1)
                    mm(acc[h][:, :], sh5[:, k, :], gs5[:, 32 * h:32 * h + 32, :].rearrange("p g c -> p (g c)"),
                       **one).then_inc(sem("t_shifted"), 1)
            pe.wait_ge(sem("t_ready"), 7)
            pe.wait_ge(*reach("s5_scanned", 1))
            pe.wait_ge(sem("tbd_ready"), 1)
            pe.wait_ge(sem("o_matrices"), 2)
            for n in range(5):
                if n == 4:
                    pe.wait_ge(*reach("fo_copied", 1))
                for m in range(4 if n < 4 else 2):
                    k, b = (4 * n + m) // 9, (4 * n + m) % 9
                    last = turn(side[n % 4][0:PAIRS, m * P:(m + 1) * P], fin5[:, k, b, :])
                last.then_inc(sem("s5_finals_turned"), 1)

            def s5_out(i, b):
                q = (obd, obd2)[b]
                pe.wait_ge(sem("tbd_ready"), i + 1)
                pe.wait_ge(sem("o_matrices"), i * 2 + 2)
                for p in range(PB):
                    if p % 4 == 0:
                        wait(pe, "s5_y_copied", i * 2 + (p // 4 - 3))
                    v = acc[2 * b + p // 4][:, (p % 4) * NK:(p % 4 + 1) * NK]
                    pair = ds(i * PB + p, 1)
                    mm(v, tbd[:, b, p, :], u2[:, pair, :].rearrange("x o c -> x (o c)"), start=True, stop=False)
                    mm(v, q[:, 0, p, :], st5[:, 0, pair, :].rearrange("x o c -> x (o c)"), start=False, stop=False)
                    last = mm(v, q[:, 1, p, :], st5[:, 1, pair, :].rearrange("x o c -> x (o c)"), start=False, stop=True)
                    if p % 4 == 3:
                        last.then_inc(sem("y5_product"), 1)

            s5_out(0, 0)
            s5_out(1, 1)
            with pe.Fori(1, 4) as i:
                s5_out(i * 2, 0)
                s5_out(i * 2 + 1, 1)
            pe.wait_ge(*reach("v_ready", KT))
            pe.wait_ge(*reach("fo_copied", 5))

            def glu(k, b):
                wait(pe, "acc_freed", k - 1)
                outgroup(k, C_GLU, (129 + b) % 2, h_hi, h_lo)

            glu(0, 0)
            glu(1, 1)
            with pe.Fori(1, 8) as i:
                glu(i * 2, 0)
                glu(i * 2 + 1, 1)

            def proj(k, b, ready=None):
                pe.wait_ge(freed, k + 15)
                outgroup(k, C_OUT, (145 + b) % 2, mg_hi, mg_lo, ready)

            proj(0, 0, "merged")
            proj(1, 1)
            with pe.Fori(1, 4) as i:
                proj(i * 2, 0)
                proj(i * 2 + 1, 1)
            pe.wait_ge(*reach("m_summed", 16))
            sum_squares()
            pe.wait_ge(sem("rms_ready"), 2)
            for i in range(KT):
                pe.wait_ge(sem("x1_squared"), i + 1)
                last = mm(s0[:, 0:T], ones[:, :], msq[:, i % 2, :], start=i == 0, stop=i == KT - 1)
                last.then_inc(sem("x1_summed"), 1)

            def up(k, b, ready=None):
                pe.wait_ge(freed, k + 23)
                outgroup(k, C_UP, (153 + b) % 2, h_hi, h_lo, ready)

            up(0, 0, "h2_ready")
            up(1, 1)
            with pe.Fori(1, FT // 2) as i:
                up(i * 2, 0)
                up(i * 2 + 1, 1)

            def down(k, b, ready=None):
                pe.wait_ge(freed, k + (24 + FT - 1))
                for i in range(12):
                    tiles = range(4 * i, 4 * i + 4) if i < 8 else range(32 + 3 * (i - 8), 35 + 3 * (i - 8))
                    if ready:
                        pe.wait_ge(*reach(ready, tiles[-1] + 1))
                    chunk(k * 12 + (C_DOWN + i), i % 4, (197 + b) % 2, f_hi, f_lo, tiles, i == 0, i == 11)

            down(0, 0, "f_split")
            down(1, 1)
            with pe.Fori(1, 4) as i:
                down(i * 2, 0)
                down(i * 2 + 1, 1)
            pe.wait_ge(*reach("f_summed", 16))
            pe.wait_ge(sem("rms_ready"), 3)
            sum_squares()
            pe.wait_ge(sem("rstd_ready"), 4)
            for c, (t0, n) in enumerate(TOK):
                for j in range(4):
                    if c:
                        pe.wait_ge(sem("out_rows"), 4 * (c - 1) + j + 1)
                    else:
                        pe.wait_ge(sem("y_ready"), 4 * j + 4)
                    for i in range(4):
                        last = turn(side[j][0:n, i * P:(i + 1) * P], x1r[:, 4 * j + i, t0:t0 + n])
                    last.then_inc(sem("out_turned"), 1)


def kernel(**inputs):
    import numpy as _np
    import concourse.bacc as _bacc
    from concourse.bass_utils import run_bass_kernel_spmd as _run

    nc = _bacc.Bacc("TRN2", target_bir_lowering=False, num_devices=1)
    arrays, a, o = {}, {}, {}
    for name in NAMES:
        x = _np.ascontiguousarray(inputs[name])
        arrays[f"in_{name}_dram"] = x
        a[name] = nc.dram_tensor(f"in_{name}_dram", x.shape, mybir.dt.from_np(x.dtype), kind="ExternalInput").ap()
    for name, shape in OUTS:
        o[name] = nc.dram_tensor(f"out_{name}_dram", shape, F32, kind="ExternalOutput").ap()
    build(nc, a, o)
    r = _run(nc, [arrays], core_ids=[0])
    return tuple(r.results[0][f"out_{name}_dram"] for name, _ in OUTS)
```
